# Optimizing a Trainium2 kernel written in Bass

```python
import jax
import jax.numpy as jnp
from jax import lax
import numpy as np
import jax, jax.numpy as jnp

D_MODEL = 1024
BATCH = 1
SEQ = 256
DEPTH = 2

D_FF = 2816
DN_HEADS = 4
DN_HEAD_DIM = 128
DN_KEY_DIM = DN_HEADS * DN_HEAD_DIM
DN_VAL_DIM = DN_HEADS * DN_HEAD_DIM
DN_CONV = 4
DN_CHUNK = 64
CV_CHANNELS = 512
CV_KERNEL = 31
MLA_HEADS = 4
MLA_Q_LORA = 384
MLA_KV_LORA = 256
MLA_NOPE = 128
MLA_ROPE = 64
MLA_V = 128
ATTN_BLOCK = 128
ROPE_THETA = 10000.0
N_BRANCHES = 3
DEEPNORM_ALPHA = (2 * DEPTH) ** 0.25
DEEPNORM_BETA = (8 * DEPTH) ** -0.25
NORM_EPS = 1e-5
IN_SIZES = (DN_KEY_DIM, DN_KEY_DIM, DN_VAL_DIM, DN_VAL_DIM, DN_HEADS, DN_HEADS,
            2 * CV_CHANNELS, MLA_Q_LORA, MLA_KV_LORA, MLA_ROPE, N_BRANCHES * D_MODEL)
D_IN = sum(IN_SIZES)


def _split_points():
    return [int(v) for v in np.cumsum(IN_SIZES)[:-1]]

def layer_norm(x, g, b):
    xf = x.astype(jnp.float32)
    mu = jnp.mean(xf, axis=-1, keepdims=True)
    var = jnp.mean(jnp.square(xf - mu), axis=-1, keepdims=True)
    return ((xf - mu) * lax.rsqrt(var + NORM_EPS) * g + b).astype(x.dtype)

def rms_norm(x, w):
    xf = x.astype(jnp.float32)
    return (xf * lax.rsqrt(jnp.mean(jnp.square(xf), axis=-1, keepdims=True) + NORM_EPS) * w).astype(x.dtype)

def l2_normalize(x):
    xf = x.astype(jnp.float32)
    return xf * lax.rsqrt(jnp.sum(jnp.square(xf), axis=-1, keepdims=True) + 1e-6)

def swiglu(x, w_gate, w_up, w_down):
    return (jax.nn.silu(x @ w_gate) * (x @ w_up)) @ w_down

def causal_depthwise_conv(x, w):
    k, c = w.shape
    return lax.conv_general_dilated(
        x, w[:, None, :].astype(x.dtype), window_strides=(1,), padding=[(k - 1, 0)],
        dimension_numbers=('NWC', 'WIO', 'NWC'), feature_group_count=c)

def rope_tables(positions):
    half = MLA_ROPE // 2
    inv_freq = ROPE_THETA ** (-jnp.arange(half, dtype=jnp.float32) / half)
    ang = positions.astype(jnp.float32)[..., None] * inv_freq
    return jnp.cos(ang), jnp.sin(ang)

def apply_rope(x, cos, sin):
    half = x.shape[-1] // 2
    xf = x.astype(jnp.float32)
    x1, x2 = xf[..., :half], xf[..., half:]
    return jnp.concatenate([x1 * cos - x2 * sin, x2 * cos + x1 * sin], axis=-1).astype(x.dtype)

def gated_delta_rule(q, k, v, g, beta):
    b, t, h, dk = q.shape
    dv = v.shape[-1]
    c = DN_CHUNK
    n = t // c
    f32 = jnp.float32

    def chunks(a):
        a = a.reshape(b, n, c, h, *a.shape[3:])
        return jnp.moveaxis(a, (1, 3), (0, 2))

    q = chunks(q.astype(f32)) * (dk ** -0.5)
    k = chunks(k.astype(f32))
    v = chunks(v.astype(f32))
    beta = chunks(beta.astype(f32))
    g = jnp.cumsum(chunks(g.astype(f32)), axis=-1)
    causal = jnp.tril(jnp.ones((c, c), dtype=bool))
    strict = jnp.tril(jnp.ones((c, c), dtype=bool), -1)
    decay = jnp.exp(jnp.where(causal, g[..., :, None] - g[..., None, :], -jnp.inf))
    kk = jnp.einsum('nbhik,nbhjk->nbhij', k, k)
    a_mat = jnp.where(strict, beta[..., None] * kk * decay, 0.0) + jnp.eye(c, dtype=f32)
    rhs = jnp.concatenate([v * beta[..., None], k * (beta * jnp.exp(g))[..., None]], axis=-1)
    sol = lax.linalg.triangular_solve(a_mat, rhs, left_side=True, lower=True, unit_diagonal=True)
    u, w = sol[..., :dv], sol[..., dv:]
    qk = jnp.where(causal, jnp.einsum('nbhik,nbhjk->nbhij', q, k) * decay, 0.0)
    q_dec = q * jnp.exp(g)[..., None]
    g_last = g[..., -1]
    k_dec = k * jnp.exp(g_last[..., None] - g)[..., None]

    def step(state, xs):
        u_i, w_i, qk_i, q_dec_i, k_dec_i, gl_i = xs
        v_new = u_i - jnp.einsum('bhck,bhkv->bhcv', w_i, state)
        o = jnp.einsum('bhck,bhkv->bhcv', q_dec_i, state) + jnp.einsum('bhij,bhjv->bhiv', qk_i, v_new)
        state = state * jnp.exp(gl_i)[..., None, None] + jnp.einsum('bhck,bhcv->bhkv', k_dec_i, v_new)
        return state, o

    s0 = jnp.zeros((b, h, dk, dv), f32)
    _, o = lax.scan(step, s0, (u, w, qk, q_dec, k_dec, g_last))
    return jnp.moveaxis(o, (0, 2), (1, 3)).reshape(b, t, h, dv)

def deltanet_branch(q, k, v, z, a, beta_logit, conv_w, a_log, dt_bias, norm_w, w_o):
    b, t, _ = q.shape
    qkv = jax.nn.silu(causal_depthwise_conv(jnp.concatenate([q, k, v], axis=-1), conv_w))
    q, k, v = jnp.split(qkv, [DN_KEY_DIM, 2 * DN_KEY_DIM], axis=-1)
    q = l2_normalize(q.reshape(b, t, DN_HEADS, DN_HEAD_DIM))
    k = l2_normalize(k.reshape(b, t, DN_HEADS, DN_HEAD_DIM))
    v = v.reshape(b, t, DN_HEADS, DN_HEAD_DIM)
    beta = jax.nn.sigmoid(beta_logit.astype(jnp.float32))
    g = -jnp.exp(a_log.astype(jnp.float32)) * jax.nn.softplus(a.astype(jnp.float32) + dt_bias.astype(jnp.float32))
    o = gated_delta_rule(q, k, v, g, beta)
    o = rms_norm(o, norm_w) * jax.nn.silu(z.reshape(b, t, DN_HEADS, DN_HEAD_DIM).astype(jnp.float32))
    return o.reshape(b, t, DN_VAL_DIM).astype(z.dtype) @ w_o

def conv_branch(u, glu_b, dw_w, dw_b, ln_g, ln_b, w_pw2, b_pw2):
    u = u + glu_b
    h = u[..., :CV_CHANNELS] * jax.nn.sigmoid(u[..., CV_CHANNELS:])
    h = causal_depthwise_conv(h, dw_w) + dw_b
    h = jax.nn.silu(layer_norm(h, ln_g, ln_b))
    return h @ w_pw2 + b_pw2

def causal_block_attention(q_nope, q_rope, k_nope, k_rope, v):
    t = q_nope.shape[1]
    scale = (MLA_NOPE + MLA_ROPE) ** -0.5
    outs = []
    for i in range(t // ATTN_BLOCK):
        q0, q1 = i * ATTN_BLOCK, (i + 1) * ATTN_BLOCK
        s = (jnp.einsum('bqhd,bkhd->bhqk', q_nope[:, q0:q1], k_nope[:, :q1])
             + jnp.einsum('bqhr,bkr->bhqk', q_rope[:, q0:q1], k_rope[:, :q1])).astype(jnp.float32) * scale
        mask = jnp.arange(q1)[None, :] <= jnp.arange(q0, q1)[:, None]
        p = jax.nn.softmax(jnp.where(mask, s, -jnp.inf), axis=-1).astype(v.dtype)
        outs.append(jnp.einsum('bhqk,bkhv->bqhv', p, v[:, :q1]))
    return jnp.concatenate(outs, axis=1)

def mla_branch(c_q, c_kv, k_r, cos, sin, q_norm_w, w_uq, kv_norm_w, w_ukv, w_o):
    b, t, _ = c_q.shape
    q = (rms_norm(c_q, q_norm_w) @ w_uq).reshape(b, t, MLA_HEADS, MLA_NOPE + MLA_ROPE)
    q_nope = q[..., :MLA_NOPE]
    q_rope = apply_rope(q[..., MLA_NOPE:], cos[:, :, None, :], sin[:, :, None, :])
    kv = (rms_norm(c_kv, kv_norm_w) @ w_ukv).reshape(b, t, MLA_HEADS, MLA_NOPE + MLA_V)
    k_nope, v = kv[..., :MLA_NOPE], kv[..., MLA_NOPE:]
    k_rope = apply_rope(k_r, cos, sin)
    o = causal_block_attention(q_nope, q_rope, k_nope, k_rope, v)
    return o.reshape(b, t, MLA_HEADS * MLA_V) @ w_o

def hybrid_mixer(x, cos, sin, w_in, b_gate,
                 dn_conv_w, dn_a_log, dn_dt_bias, dn_norm_w, dn_w_o,
                 cv_glu_b, cv_dw_w, cv_dw_b, cv_ln_g, cv_ln_b, cv_w_pw2, cv_b_pw2,
                 mla_q_norm_w, mla_w_uq, mla_kv_norm_w, mla_w_ukv, mla_w_o, w_out):
    b, t, d = x.shape
    proj = x @ w_in
    (dq, dk, dv, dz, da, dbeta, glu, c_q, c_kv, k_r, gate_logits) = jnp.split(proj, _split_points(), axis=-1)
    y_dn = deltanet_branch(dq, dk, dv, dz, da, dbeta, dn_conv_w, dn_a_log, dn_dt_bias, dn_norm_w, dn_w_o)
    y_cv = conv_branch(glu, cv_glu_b, cv_dw_w, cv_dw_b, cv_ln_g, cv_ln_b, cv_w_pw2, cv_b_pw2)
    y_mla = mla_branch(c_q, c_kv, k_r, cos, sin, mla_q_norm_w, mla_w_uq, mla_kv_norm_w, mla_w_ukv, mla_w_o)
    gates = jax.nn.sigmoid((gate_logits + b_gate).astype(jnp.float32)).astype(x.dtype).reshape(b, t, N_BRANCHES, d)
    merged = gates[:, :, 0] * y_dn + gates[:, :, 1] * y_cv + gates[:, :, 2] * y_mla
    return merged @ w_out

def first_inputs(seed: int = 0) -> dict:
    key = jax.random.key(seed)
    ks = iter(jax.random.split(key, 48))
    L = DEPTH
    f32 = jnp.float32

    def w(shape, fan_in, scale=1.0):
        return jax.random.normal(next(ks), shape, f32) * (scale * fan_in ** -0.5)

    def gain(shape):
        return 1.0 + 0.02 * jax.random.normal(next(ks), shape, f32)

    def bias(shape):
        return 0.02 * jax.random.normal(next(ks), shape, f32)

    x = jax.random.normal(next(ks), (BATCH, SEQ, D_MODEL), f32)
    positions = (jax.random.randint(next(ks), (BATCH, 1), 0, 4096, dtype=jnp.int32)
                 + jnp.arange(SEQ, dtype=jnp.int32)[None, :])
    dt = jnp.exp(jax.random.uniform(next(ks), (L, DN_HEADS), f32, np.log(1e-3), np.log(1e-1)))
    return {
        'x': x,
        'positions': positions,
        'ln1_g': gain((L, D_MODEL)),
        'ln1_b': bias((L, D_MODEL)),
        'ffn1_w_gate': w((L, D_MODEL, D_FF), D_MODEL),
        'ffn1_w_up': w((L, D_MODEL, D_FF), D_MODEL),
        'ffn1_w_down': w((L, D_FF, D_MODEL), D_FF, DEEPNORM_BETA),
        'w_in': w((L, D_MODEL, D_IN), D_MODEL),
        'b_gate': bias((L, N_BRANCHES * D_MODEL)),
        'dn_conv_w': w((L, DN_CONV, 2 * DN_KEY_DIM + DN_VAL_DIM), DN_CONV),
        'dn_a_log': jnp.log(jax.random.uniform(next(ks), (L, DN_HEADS), f32, 1.0, 16.0)),
        'dn_dt_bias': dt + jnp.log(-jnp.expm1(-dt)),
        'dn_norm_w': gain((L, DN_HEAD_DIM)),
        'dn_w_o': w((L, DN_VAL_DIM, D_MODEL), DN_VAL_DIM, DEEPNORM_BETA),
        'cv_glu_b': bias((L, 2 * CV_CHANNELS)),
        'cv_dw_w': w((L, CV_KERNEL, CV_CHANNELS), CV_KERNEL),
        'cv_dw_b': bias((L, CV_CHANNELS)),
        'cv_ln_g': gain((L, CV_CHANNELS)),
        'cv_ln_b': bias((L, CV_CHANNELS)),
        'cv_w_pw2': w((L, CV_CHANNELS, D_MODEL), CV_CHANNELS, DEEPNORM_BETA),
        'cv_b_pw2': bias((L, D_MODEL)),
        'mla_q_norm_w': gain((L, MLA_Q_LORA)),
        'mla_w_uq': w((L, MLA_Q_LORA, MLA_HEADS * (MLA_NOPE + MLA_ROPE)), MLA_Q_LORA),
        'mla_kv_norm_w': gain((L, MLA_KV_LORA)),
        'mla_w_ukv': w((L, MLA_KV_LORA, MLA_HEADS * (MLA_NOPE + MLA_V)), MLA_KV_LORA),
        'mla_w_o': w((L, MLA_HEADS * MLA_V, D_MODEL), MLA_HEADS * MLA_V, DEEPNORM_BETA),
        'w_out': w((L, D_MODEL, D_MODEL), D_MODEL, DEEPNORM_BETA),
        'ln2_g': gain((L, D_MODEL)),
        'ln2_b': bias((L, D_MODEL)),
        'ffn2_w_gate': w((L, D_MODEL, D_FF), D_MODEL),
        'ffn2_w_up': w((L, D_MODEL, D_FF), D_MODEL),
        'ffn2_w_down': w((L, D_FF, D_MODEL), D_FF, DEEPNORM_BETA),
        'ln3_g': gain((L, D_MODEL)),
        'ln3_b': bias((L, D_MODEL)),
    }

def first_block(x, positions, ln1_g, ln1_b, ffn1_w_gate, ffn1_w_up, ffn1_w_down, w_in, b_gate,
              dn_conv_w, dn_a_log, dn_dt_bias, dn_norm_w, dn_w_o,
              cv_glu_b, cv_dw_w, cv_dw_b, cv_ln_g, cv_ln_b, cv_w_pw2, cv_b_pw2,
              mla_q_norm_w, mla_w_uq, mla_kv_norm_w, mla_w_ukv, mla_w_o,
              w_out, ln2_g, ln2_b, ffn2_w_gate, ffn2_w_up, ffn2_w_down, ln3_g, ln3_b):
    cos, sin = rope_tables(positions)
    h = x
    for l in range(DEPTH):
        h = layer_norm(DEEPNORM_ALPHA * h + 0.5 * swiglu(h, ffn1_w_gate[l], ffn1_w_up[l], ffn1_w_down[l]),
                       ln1_g[l], ln1_b[l])
        mix = hybrid_mixer(h, cos, sin, w_in[l], b_gate[l],
                           dn_conv_w[l], dn_a_log[l], dn_dt_bias[l], dn_norm_w[l], dn_w_o[l],
                           cv_glu_b[l], cv_dw_w[l], cv_dw_b[l], cv_ln_g[l], cv_ln_b[l], cv_w_pw2[l], cv_b_pw2[l],
                           mla_q_norm_w[l], mla_w_uq[l], mla_kv_norm_w[l], mla_w_ukv[l], mla_w_o[l], w_out[l])
        h = layer_norm(DEEPNORM_ALPHA * h + mix, ln2_g[l], ln2_b[l])
        h = layer_norm(DEEPNORM_ALPHA * h + 0.5 * swiglu(h, ffn2_w_gate[l], ffn2_w_up[l], ffn2_w_down[l]),
                       ln3_g[l], ln3_b[l])
    return h


N_MIXERS = 2
CONV_WIDTH = 3
ATTN_GROUPS = ((128, 1), (512, 4), (2048, 16))
N_GROUPS = len(ATTN_GROUPS)
HEADS_PER_GROUP = 5
HEAD_DIM = 64
ATTN_WIDTH = N_GROUPS * HEADS_PER_GROUP * HEAD_DIM
N_EXPERTS = 8
TOP_K = 2
D_FF_EXPERT = 2816
RMS_EPS = 1e-6
N_EVEN = (DEPTH + 1) // 2
N_ODD = DEPTH // 2


def rms_norm_2(x, g):
    xf = x.astype(jnp.float32)
    y = xf * lax.rsqrt(jnp.mean(xf * xf, axis=-1, keepdims=True) + RMS_EPS)
    return (y * g.astype(jnp.float32)).astype(x.dtype)

def ada_params(c, w, b):
    mod = jax.nn.silu(c) @ w + b
    shift, scale, gate = jnp.split(mod, 3, axis=-1)
    return shift[:, None, :], scale[:, None, :], gate[:, None, :]

def modulated_residual(x, c, g, w_mod, b_mod, fn):
    shift, scale, gate = ada_params(c, w_mod, b_mod)
    h = rms_norm_2(x, g) * (1 + scale) + shift
    return x + gate * fn(h)

def rope(x, positions):
    inv_freq = ROPE_THETA ** (-jnp.arange(0, HEAD_DIM, 2, dtype=jnp.float32) / HEAD_DIM)
    ang = positions.astype(jnp.float32)[..., None] * inv_freq
    cos, sin = jnp.cos(ang)[:, :, None, :], jnp.sin(ang)[:, :, None, :]
    xf = x.astype(jnp.float32)
    x1, x2 = jnp.split(xf, 2, axis=-1)
    return jnp.concatenate([x1 * cos - x2 * sin, x2 * cos + x1 * sin], axis=-1).astype(x.dtype)

def short_conv_mixer(h, w_in, conv_w, w_out):
    b_gate, c_gate, u = jnp.split(h @ w_in, 3, axis=-1)
    v = c_gate * u
    conv = lax.conv_general_dilated(
        v, conv_w.astype(v.dtype)[:, None, :], window_strides=(1,),
        padding=[(CONV_WIDTH - 1, 0)], dimension_numbers=('NWC', 'WIO', 'NWC'),
        feature_group_count=v.shape[-1])
    return (b_gate * conv) @ w_out

def dilated_group_attention(q, k, v, dilation, steps):
    b, s, nh, dh = q.shape
    chunk = dilation * steps
    sp = -(-s // chunk) * chunk
    nb = sp // chunk
    pad = [(0, 0), (0, sp - s), (0, 0), (0, 0)]

    def to_blocks(t):
        return jnp.pad(t, pad).reshape(b, nb, steps, dilation, nh, dh)

    def with_prev(t):
        prev = jnp.pad(t[:, :-1], [(0, 0), (1, 0), (0, 0), (0, 0), (0, 0), (0, 0)])
        return jnp.concatenate([prev, t], axis=2)

    qb = to_blocks(q)
    kk = with_prev(to_blocks(k))
    vv = with_prev(to_blocks(v))
    scores = jnp.einsum('bnqrhd,bnkrhd->bnrhqk', qb, kk,
                        preferred_element_type=jnp.float32) * (dh ** -0.5)
    a = jnp.arange(steps)[:, None]
    j = jnp.arange(2 * steps)[None, :]
    band = (j >= a) & (j <= a + steps)
    not_first = jnp.arange(nb)[:, None, None] > 0
    valid = band[None] & (not_first | (j >= steps)[None])
    scores = jnp.where(valid[None, :, None, None], scores, -jnp.inf)
    lse = jax.nn.logsumexp(scores, axis=-1)
    p = jnp.exp(scores - lse[..., None])
    o = jnp.einsum('bnrhqk,bnkrhd->bnqrhd', p.astype(v.dtype), vv)
    o = o.reshape(b, sp, nh, dh)[:, :s]
    lse = lse.transpose(0, 1, 4, 2, 3).reshape(b, sp, nh)[:, :s]
    return o, lse

def dilated_attention_mixer(h, positions, w_qkv, w_o):
    b, s, _ = h.shape
    nh = N_GROUPS * HEADS_PER_GROUP
    qkv = (h @ w_qkv).reshape(b, s, 3, nh, HEAD_DIM)
    q = rope(qkv[:, :, 0], positions).reshape(b, s, N_GROUPS, HEADS_PER_GROUP, HEAD_DIM)
    k = rope(qkv[:, :, 1], positions).reshape(b, s, N_GROUPS, HEADS_PER_GROUP, HEAD_DIM)
    v = qkv[:, :, 2].reshape(b, s, N_GROUPS, HEADS_PER_GROUP, HEAD_DIM)
    outs, lses = [], []
    for g, (window, dil) in enumerate(ATTN_GROUPS):
        o, l = dilated_group_attention(q[:, :, g], k[:, :, g], v[:, :, g], dil, window // dil)
        outs.append(o)
        lses.append(l)
    alpha = jax.nn.softmax(jnp.stack(lses, axis=2), axis=2)
    o = jnp.stack(outs, axis=2) * alpha[..., None].astype(h.dtype)
    return o.reshape(b, s, ATTN_WIDTH) @ w_o

def swiglu_2(h, w_gate, w_up, w_down):
    return (jax.nn.silu(h @ w_gate) * (h @ w_up)) @ w_down

def moe_swiglu(h, w_router, w_gate, w_up, w_down):
    logits = jnp.einsum('bsd,de->bse', h, w_router, preferred_element_type=jnp.float32)
    top_val, top_idx = lax.top_k(logits, TOP_K)
    top_w = jax.nn.softmax(top_val, axis=-1)
    gates = jnp.sum(jax.nn.one_hot(top_idx, N_EXPERTS, dtype=jnp.float32) * top_w[..., None],
                    axis=-2).astype(h.dtype)
    out = jnp.zeros_like(h)
    for e in range(N_EXPERTS):
        out = out + gates[..., e:e + 1] * swiglu_2(h, w_gate[e], w_up[e], w_down[e])
    return out

def second_inputs(seed: int = 0) -> dict:
    key = jax.random.key(seed)
    ks = jax.random.split(key, 20)
    D, F, FE, E = D_MODEL, D_FF, D_FF_EXPERT, N_EXPERTS

    def w(k, shape, fan_in, scale=1.0):
        return jax.random.normal(k, shape, jnp.float32) * (scale * fan_in ** -0.5)

    offsets = jax.random.randint(ks[2], (BATCH, 1), 0, 1024, dtype=jnp.int32)
    return {
        "x": jax.random.normal(ks[0], (BATCH, SEQ, D), jnp.float32),
        "c": jax.random.normal(ks[1], (BATCH, D), jnp.float32),
        "positions": offsets + jnp.arange(SEQ, dtype=jnp.int32)[None, :],
        "mod_w": w(ks[3], (DEPTH, 2, D, 3 * D), D, 0.5),
        "mod_b": 0.02 * jax.random.normal(ks[4], (DEPTH, 2, 3 * D), jnp.float32),
        "norm_g": 1.0 + 0.05 * jax.random.normal(ks[5], (DEPTH, 2, D), jnp.float32),
        "conv_w_in": w(ks[6], (N_EVEN, D, 3 * D), D),
        "conv_w": w(ks[7], (N_EVEN, CONV_WIDTH, D), CONV_WIDTH),
        "conv_w_out": w(ks[8], (N_EVEN, D, D), D),
        "ffn_w_gate": w(ks[9], (N_EVEN, D, F), D),
        "ffn_w_up": w(ks[10], (N_EVEN, D, F), D),
        "ffn_w_down": w(ks[11], (N_EVEN, F, D), F),
        "attn_w_qkv": w(ks[12], (N_ODD, D, 3 * ATTN_WIDTH), D),
        "attn_w_o": w(ks[13], (N_ODD, ATTN_WIDTH, D), ATTN_WIDTH),
        "router_w": w(ks[14], (N_ODD, D, E), D),
        "moe_w_gate": w(ks[15], (N_ODD, E, D, FE), D),
        "moe_w_up": w(ks[16], (N_ODD, E, D, FE), D),
        "moe_w_down": w(ks[17], (N_ODD, E, FE, D), FE),
        "final_g": 1.0 + 0.05 * jax.random.normal(ks[18], (D,), jnp.float32),
    }

def second_block(x, c, positions, mod_w, mod_b, norm_g, conv_w_in, conv_w, conv_w_out,
              ffn_w_gate, ffn_w_up, ffn_w_down, attn_w_qkv, attn_w_o, router_w,
              moe_w_gate, moe_w_up, moe_w_down, final_g):
    c = c.astype(x.dtype)
    for i in range(DEPTH):
        j = i // N_MIXERS
        if i % N_MIXERS == 0:
            mixer = lambda h, j=j: short_conv_mixer(h, conv_w_in[j], conv_w[j], conv_w_out[j])
            channel = lambda h, j=j: swiglu_2(h, ffn_w_gate[j], ffn_w_up[j], ffn_w_down[j])
        else:
            mixer = lambda h, j=j: dilated_attention_mixer(h, positions, attn_w_qkv[j], attn_w_o[j])
            channel = lambda h, j=j: moe_swiglu(h, router_w[j], moe_w_gate[j], moe_w_up[j],
                                                moe_w_down[j])
        x = modulated_residual(x, c, norm_g[i, 0], mod_w[i, 0], mod_b[i, 0], mixer)
        x = modulated_residual(x, c, norm_g[i, 1], mod_w[i, 1], mod_b[i, 1], channel)
    return rms_norm_2(x, final_g)


def setup_inputs(seed=0):
    out = dict(first_inputs(seed))
    for name, value in second_inputs(seed + 1).items():
        if name != "x":
            out[name + "_2"] = value
    return out


def reference(
    x, positions, ln1_g, ln1_b, ffn1_w_gate, ffn1_w_up, ffn1_w_down, w_in, b_gate, dn_conv_w,
    dn_a_log, dn_dt_bias, dn_norm_w, dn_w_o, cv_glu_b, cv_dw_w, cv_dw_b, cv_ln_g, cv_ln_b,
    cv_w_pw2, cv_b_pw2, mla_q_norm_w, mla_w_uq, mla_kv_norm_w, mla_w_ukv, mla_w_o, w_out, ln2_g,
    ln2_b, ffn2_w_gate, ffn2_w_up, ffn2_w_down, ln3_g, ln3_b, c_2, positions_2, mod_w_2,
    mod_b_2, norm_g_2, conv_w_in_2, conv_w_2, conv_w_out_2, ffn_w_gate_2, ffn_w_up_2,
    ffn_w_down_2, attn_w_qkv_2, attn_w_o_2, router_w_2, moe_w_gate_2, moe_w_up_2, moe_w_down_2,
    final_g_2,
):
    x = first_block(
        x, positions, ln1_g, ln1_b, ffn1_w_gate, ffn1_w_up, ffn1_w_down, w_in, b_gate,
        dn_conv_w, dn_a_log, dn_dt_bias, dn_norm_w, dn_w_o, cv_glu_b, cv_dw_w, cv_dw_b, cv_ln_g,
        cv_ln_b, cv_w_pw2, cv_b_pw2, mla_q_norm_w, mla_w_uq, mla_kv_norm_w, mla_w_ukv, mla_w_o,
        w_out, ln2_g, ln2_b, ffn2_w_gate, ffn2_w_up, ffn2_w_down, ln3_g, ln3_b,
    )
    return second_block(
        x, c_2, positions_2, mod_w_2, mod_b_2, norm_g_2, conv_w_in_2, conv_w_2, conv_w_out_2,
        ffn_w_gate_2, ffn_w_up_2, ffn_w_down_2, attn_w_qkv_2, attn_w_o_2, router_w_2,
        moe_w_gate_2, moe_w_up_2, moe_w_down_2, final_g_2,
    )


_drawn_inputs = setup_inputs


def setup_inputs(seed=0):
    import zlib

    import numpy as np

    out = dict(_drawn_inputs(seed))
    spreads = {}
    factors = {'b_gate': 8.0,
     'dn_a_log': 2.888,
     'dn_norm_w': 18.223,
     'cv_glu_b': 7.794,
     'cv_dw_b': 6.033,
     'cv_ln_g': 8.0,
     'cv_ln_b': 8.0,
     'cv_b_pw2': 4.579,
     'mla_q_norm_w': 8.0,
     'mla_kv_norm_w': 8.0}
    for name, (base, spread) in spreads.items():
        noise = np.random.default_rng([zlib.crc32(name.encode()), seed]).standard_normal(out[name].shape)
        drawn = base * np.exp(spread * noise) if base else spread * noise
        out[name] = jnp.asarray(drawn.astype(out[name].dtype))
    for name, factor in factors.items():
        out[name] = (out[name] * factor).astype(out[name].dtype)
    return out
```

```python
from contextlib import ExitStack

import numpy as np

import concourse.bass as bass
from concourse import mybir

F32 = mybir.dt.float32
I32 = mybir.dt.int32
ALU = mybir.AluOpType
ACT = mybir.ActivationFunctionType
AX = mybir.AxisListType

P = 128
SEQ, D, DEPTH = 256, 1024, 2
TT = SEQ // P
KD = D // P
FF, FSTEP = 2816, 256
NS = FF // FSTEP
FB = FSTEP // P
HEADS, HD, CHUNK = 4, 128, 64
CV, TAPS = 512, 31
CB = CV // P
QL, KVL, NOPE, ROPE, VD = 384, 256, 128, 64, 128
HALF = ROPE // 2
QB, KVB = QL // P, KVL // P
ALPHA = (2 * DEPTH) ** 0.25
LN_EPS, RMS_EPS, L2_EPS = 1e-5, 1e-6, 1e-6
MLA_SCALE = (NOPE + ROPE) ** -0.5
DN_SCALE = HD ** -0.5
MASKED = -1e30
C_Z, C_GLU, C_CQ, C_KR, C_GATE = 1536, 2056, 3080, 3720, 3784
PANEL = 512
GATE_PANELS = 3 * D // PANEL
AH, AD, AG, AJ = 15, 64, 3, 5
AW = AH * AD
A_SCALE = AD ** -0.5
DILATIONS = (1, 4, 16)
NE = 8
ITEMS = 16
MOD_UNITS = 12
MOD_COLS = 3 * D // MOD_UNITS
FFN_LAYER = 2 * NS
MIX_USES = 20
LN_LAYER = 3

ROW_GATE, ROW_CONV, ROW_GLU, ROW_DWB, ROW_LNG, ROW_LNB, ROW_PW, ROW_QN, ROW_KVN, ROWS = (
    0, 24, 72, 80, 84, 88, 92, 100, 103, 105)
TWO_PI = 2 * np.pi
ROUND = 1.5 * 2.0 ** 23
PI_A = 6.28125
PI_B = float((np.array(TWO_PI - PI_A, np.float32).view(np.int32) & np.int32(-4096)).view(np.float32))
PI_C = float(np.float32(TWO_PI - PI_A - PI_B))
PI_SAFE = 3.1415925

MIXER_PANELS = (
    [("qkv", [("w_in", 0, D, PANEL * i, PANEL)]) for i in range(3)]
    + [("glu", [("w_in", 0, D, C_GLU + PANEL * i, PANEL)]) for i in range(2)]
    + [("z", [("w_in", 0, D, C_Z, 520)]),
       ("lora", [("w_in", 0, D, C_CQ, PANEL)]),
       ("lora", [("w_in", 0, D, C_CQ + PANEL, C_GATE - C_CQ - PANEL)])]
    + [("gate", [("w_in", 0, D, C_GATE + PANEL * i, PANEL)]) for i in range(GATE_PANELS)]
    + [("cv_out", [("cv_w_pw2", 0, CV, 0, D)]),
       ("dn_out", [("dn_w_o", 0, HEADS * HD, 0, D)]),
       ("mla_up", [("mla_w_uq", 0, QL, 0, HEADS * (NOPE + ROPE)), ("mla_w_ukv", 0, KVL, 0, HEADS * (NOPE + VD))]),
       ("mla_out", [("mla_w_o", 0, HEADS * VD, 0, D)]),
       ("out", [("w_out", 0, D // 2, 0, D)]),
       ("out", [("w_out", D // 2, D // 2, 0, D)])])
SECOND_PANELS = (
    [("conv_in", [("conv_w_in_2", 0, D, PANEL * i, PANEL)]) for i in range(6)]
    + [("conv_out", [("conv_w_out_2", 0, D // 2, 0, D)]), ("conv_out", [("conv_w_out_2", D // 2, D // 2, 0, D)])]
    + [("qk", [("attn_w_qkv_2", 0, D, PANEL * i, min(PANEL, 2 * AW - PANEL * i))]) for i in range(4)]
    + [("v", [("attn_w_qkv_2", 0, D, 2 * AW + 480 * i, 480)]) for i in range(2)]
    + [("attn_out", [("attn_w_o_2", 0, PANEL, 0, D)]),
       ("attn_out", [("attn_w_o_2", PANEL, 384, 0, D), ("attn_w_o_2", 896, 64, 0, D)])])
assert len(MIXER_PANELS) == MIX_USES
PANEL_WORDS = max(sum(-(-rows // P) * cols for _, rows, cols in [(m, r, c) for m, _, r, _, c in pieces])
                  for _, pieces in MIXER_PANELS + SECOND_PANELS)


def landed(use):
    return 16 * sum(len(MIXER_PANELS[u][1]) for u in range(use % 2, use + 1, 2))


LANDED_LAYER = [landed(MIX_USES - 2), landed(MIX_USES - 1)]


def landed_second(use):
    return DEPTH * LANDED_LAYER[use % 2] + 16 * sum(len(SECOND_PANELS[u][1]) for u in range(use % 2, use + 1, 2))


def build(nc, a, out):
    with ExitStack() as ctx:
        def sb(name, shape, dt=F32):
            return ctx.enter_context(nc.sbuf_tensor(name, shape, dt))

        def sem(name):
            return ctx.enter_context(nc.semaphore(name))

        def v3(tile, at, *dims):
            n = int(np.prod(dims))
            piece = tile[:, at:at + n]
            if len(dims) == 1:
                return piece
            names = "abcd"[:len(dims)]
            return piece.rearrange(f"p ({' '.join(names)}) -> p {' '.join(names)}", **dict(zip(names, dims)))

        gate_w = sb("gate_w", [P, KD, FSTEP])
        up_w = sb("up_w", [P, KD, FSTEP])
        down_w = sb("down_w", [P, FB, D])
        panel = [sb(f"panel{i}", [P, PANEL_WORDS]) for i in range(2)]
        mod_unit = sb("mod_unit", [P, KD * MOD_COLS])
        mod_sum = sb("mod_sum", [P, 3 * D])
        H = sb("H", [P, TT, D])
        HT = sb("HT", [P, KD, SEQ])
        ffn_tmp = sb("ffn_tmp", [P, 2 * FB * SEQ])
        row_g = sb("row_g", [P, D])
        row_b = sb("row_b", [P, D])
        rows = sb("rows", [P, 2, P])
        pcol = sb("pcol", [P, ROWS])
        dwcol = sb("dwcol", [P, TAPS * CB])
        ident = sb("ident", [P, P])
        ones = sb("ones", [P, P])
        causal = sb("causal", [P, P])
        prefix = sb("prefix", [P, P])
        strict = sb("strict", [P, P])
        same = sb("same", [P, P])
        in_chunk = sb("in_chunk", [P, 2, P])
        level = sb("level", [P, 6, P])
        band = sb("band", [P, AG, 3, P])
        cosine = sb("cosine", [P, 2, TT, HALF])
        sine = sb("sine", [P, 2, TT, HALF])
        mod_col = sb("mod_col", [P, 2 * DEPTH * 24])
        mod_bias = sb("mod_bias", [P, P])
        misc_col = sb("misc_col", [P, 32])
        norm_row = sb("norm_row", [P, HD])
        head_rows = sb("head_rows", [P, 2 * HEADS])
        router = sb("router", [P, KD, NE])
        stats = sb("stats", [P, TT, 2, 6])
        moments = sb("moments", [P, TT, 2])
        spread = sb("spread", [P, TT, 2])
        small = sb("small", [P, 328])
        arena = sb("arena", [P, 21552])
        banks = ctx.enter_context(nc.psum_tensor("banks", [P, 8, 512], F32))
        acc = banks[:, 0:4, :].rearrange("p (t n) c -> p t (n c)", t=TT)

        sig = v3(ffn_tmp, 0, FB, SEQ)
        act_t = v3(ffn_tmp, FB * SEQ, FB, SEQ)
        mod_w = v3(mod_unit, 0, KD, MOD_COLS)
        gates = v3(arena, 0, 3 * KD, SEQ)
        raw = v3(arena, 6144, 12, 260)
        q_tok = v3(arena, 6144, TT, HEADS, HD)
        k_tok = v3(arena, 7168, TT, HEADS, HD)
        inv = v3(arena, 6144, TT, HEADS, P)
        inv_t = v3(arena, 7168, TT, HEADS, P)
        v_beta = v3(arena, 8192, TT, HEADS, HD)
        v_new = v_beta
        conv = v3(arena, 9264, 12, SEQ)
        lower = v3(arena, 9264, TT, HEADS, P)
        qk = v3(arena, 10288, TT, HEADS, P)
        g_wide = v3(arena, 11312, TT, HEADS, P)
        e_row = v3(arena, 11312, TT, HEADS, P)
        square = v3(arena, 9264, TT, HEADS * HD)
        qT = v3(arena, 12336, HEADS, SEQ)
        kT = v3(arena, 13360, HEADS, SEQ)
        part = v3(arena, 12336, TT, HEADS, P)
        turn_b = v3(arena, 13360, TT, HEADS, P)
        k_beta = v3(arena, 14384, TT, HEADS, HD)
        o_tok = k_beta
        k_dec = v3(arena, 15408, TT, HEADS, HD)
        oT = v3(arena, 15408, HEADS, SEQ)
        qk_sq = v3(arena, 16432, 4, HEADS, HD)
        u_tok = v3(arena, 16432, TT, HEADS, HD)
        wT = v3(arena, 17456, TT, HEADS, P)
        states = [v3(arena, 18480, HEADS, HD), v3(arena, 13360, HEADS, HD)]
        glu_pad = v3(arena, 18992, CB, 288)
        z_tok = v3(mod_sum, 2048, TT, HEADS * HD)
        lora = v3(arena, 20144, TT, 704)
        glu_a = v3(mod_unit, 0, CB, SEQ)
        glu_s = v3(mod_unit, 1024, CB, SEQ)
        cv_tok = v3(mod_unit, 0, TT, CV)
        cvT = v3(mod_unit, 1024, CB, SEQ)
        cv_acc = v3(ffn_tmp, 0, CB, SEQ)
        merged = v3(mod_sum, 0, KD, SEQ)
        branch = v3(ffn_tmp, 0, 2, SEQ)
        cqT = v3(arena, 6144, QB, SEQ)
        ckvT = v3(arena, 6912, KVB, SEQ)
        qnT = v3(arena, 7424, HEADS, SEQ)
        knT = v3(arena, 8448, HEADS, SEQ)
        q_rot = v3(arena, 9472, TT, HEADS, ROPE)
        qrT = v3(arena, 9984, 2, SEQ)
        k_rot = v3(arena, 10496, TT, 2, ROPE)
        krT = v3(arena, 10752, SEQ)
        v_tok = v3(arena, 11008, TT, HEADS * VD)
        first_s = v3(arena, 12032, HEADS, P)
        second_s = v3(arena, 12544, HEADS, SEQ)
        probT = v3(arena, 13568, HEADS, 3, P)
        moT = v3(arena, 15104, HEADS, SEQ)
        rope_t = v3(arena, 16128, 4, TT * (HEADS + 1) * HALF)
        x_norm = v3(arena, 0, TT, D)
        b_conv = v3(arena, 2048, KD, SEQ)
        c_conv = v3(arena, 4096, KD, SEQ)
        v_pad = v3(arena, 6144, KD, 260)
        conv_o = v3(arena, 8224, KD, SEQ)
        a_v = v3(arena, 0, TT, AW)
        a_qk = v3(arena, 2048, TT, 2 * AW)
        a_rot = v3(arena, 5888, TT, 2 * AW)
        a_pT = v3(arena, 2048, AH, 3, P)
        a_qT = v3(arena, 9728, KD, SEQ)
        a_kT = v3(arena, 11776, KD, SEQ)
        a_s = v3(arena, 13824, AH, 3 * P)
        a_o = v3(arena, 19584, TT, AW)
        a_oT = v3(arena, 9728, KD, SEQ)
        a_t = v3(mod_sum, 0, 2, AW)
        a_t2 = v3(mod_unit, 0, 2, AW)
        diag = v3(mod_unit, 0, KD, P)
        experts_sum = v3(arena, 2048, TT, D)
        pick = v3(arena, 4096, TT, P)
        weigh = v3(arena, 4352, TT, P)
        weighT = v3(arena, 4608, TT, P)
        slot_out = v3(arena, 4864, D)
        item_hot, item_tmp = v3(mod_sum, 0, ITEMS, NE), v3(mod_sum, 128, ITEMS, NE)
        item_slot, item_gate = v3(mod_sum, 256, TT, ITEMS), v3(mod_sum, 288, TT, ITEMS)
        item_expert, item_pass = mod_sum[:, 320:336], mod_sum[:, 360:376]
        passes, first_item, end_item = mod_sum[:, 336:344], mod_sum[:, 344:352], mod_sum[:, 352:360]
        count_up = mod_sum[:, 384:512]
        token_rank = v3(mod_sum, 512, TT, NE)
        counts, more = mod_sum[:, 528:536], mod_sum[:, 536:544]
        plan = mod_sum[:, 544:544 + ITEMS + 1].bitcast(I32)
        gate_row = row_g

        log_g, beta = small[:, 0:8], small[:, 8:16]
        cum, total, chunk_total = small[:, 16:24], small[:, 24:32], small[:, 32:48]
        logits = v3(small, 48, TT, 8)
        soft_x, soft_n = small[:, 64:72], small[:, 72:80]
        tok_sum, tok_scale = small[:, 80:96], small[:, 96:112]
        k_scale, dec_scale, chunk_e = small[:, 112:120], small[:, 120:128], small[:, 128:144]
        o_sum, o_scale = small[:, 144:152], small[:, 152:160]
        inv_freq = small[:, 160:192]
        lora_stats, lora_mom, lora_ms, lora_scale = v3(small, 192, TT, 2, 6), v3(small, 216, TT, 2, 2), small[:, 224:228], small[:, 228:232]
        s_max, s_sum = small[:, 240:248], small[:, 248:256]
        cum_e = small[:, 264:272]
        cv_stats, cv_mom, cv_scale = v3(small, 272, TT, 6), v3(small, 284, TT, 2), small[:, 288:290]
        neg_a = small[:, 292:296]

        mod_scale = small[:, 300:308]
        a_neg, a_sum, a_up, a_coef, a_low = small[:, 0:30], small[:, 32:62], small[:, 64:94], small[:, 96:126], small[:, 126:136]
        r_log, r_first, r_eq, r_second = v3(small, 136, TT, NE), small[:, 152:154], v3(small, 156, TT, NE), small[:, 172:174]
        r_top, r_hot1, r_hot2 = small[:, 174:176], v3(small, 176, TT, NE), v3(small, 192, TT, NE)
        r_exp, r_w1, r_rest, r_rank = small[:, 208:210], small[:, 210:212], v3(small, 212, TT, NE), small[:, 232:240]
        route = small[:, 256:272]
        chosen = v3(small, 272, TT, NE)

        setup_in, setup_row = sem("setup_in"), sem("setup_row")
        const_ready, setup_done, setup_turned = sem("const_ready"), sem("setup_done"), sem("setup_turned")
        pos_ready, col_ready, angle_ready, rope_ready = sem("pos_ready"), sem("col_ready"), sem("angle_ready"), sem("rope_ready")
        gate_in, up_in, down_in, mod_in = sem("gate_in"), sem("up_in"), sem("down_in"), sem("mod_in")
        gate_done, up_done, down_done = sem("gate_done"), sem("up_done"), sem("down_done")
        silu_done, act_ready, mod_used = sem("silu_done"), sem("act_ready"), sem("mod_used")
        mod_summed, mod_col_done = sem("mod_summed"), sem("mod_col_done")
        panel_in = [sem("panel0_in"), sem("panel1_in")]
        panel_used = sem("panel_used")
        norm_in, param_in = sem("norm_in"), sem("param_in")
        var_ready, std_ready, norm_done = sem("var_ready"), sem("std_ready"), sem("norm_done")
        turned, ht_ready = sem("turned"), sem("ht_ready")
        param_turned, param_ready = sem("param_turned"), sem("param_ready")
        pair_done, pair_taken = sem("pair_done"), sem("pair_taken")
        z_done, z_taken, lora_done, lora_taken = sem("z_done"), sem("z_taken"), sem("lora_done"), sem("lora_taken")
        qkv_conv, qkv_silu = sem("qkv_conv"), sem("qkv_silu")
        glu_ready = sem("glu_ready")
        beta_ready, soft_ready, decay_in, gate_log = sem("beta_ready"), sem("soft_ready"), sem("decay_in"), sem("gate_log")
        tok_done, tok_sq, tok_var, tok_std = sem("tok_done"), sem("tok_sq"), sem("tok_var"), sem("tok_std")
        tok_scaled, v_done, v_copied = sem("tok_scaled"), sem("v_done"), sem("v_copied")
        back_done, back_copied = sem("back_done"), sem("back_copied")
        cum_done, cum_taken, clamp_ready, decay_ready = sem("cum_done"), sem("cum_taken"), sem("clamp_ready"), sem("decay_ready")
        e_row_ready, kk_done, lower_ready = sem("e_row_ready"), sem("kk_done"), sem("lower_ready")
        inv_start, start_done, inv_ready = sem("inv_start"), sem("start_done"), sem("inv_ready")
        part_ready, turn_done, turn_copied, step_done = sem("part_ready"), sem("turn_done"), sem("turn_copied"), sem("step_done")
        join_done, uw_done, uw_copied = sem("join_done"), sem("uw_done"), sem("uw_copied")
        read_done, v_new_ready, o_done, o_copied = sem("read_done"), sem("v_new_ready"), sem("o_done"), sem("o_copied")
        write_done, state_ready = sem("write_done"), sem("state_ready")
        o_var, o_std, o_ready, o_turned, oT_ready = sem("o_var"), sem("o_std"), sem("o_ready"), sem("o_turned"), sem("oT_ready")
        z_scaled = sem("z_scaled")
        cv_conv, cv_turned, cv_var, cv_std, cv_norm = sem("cv_conv"), sem("cv_turned"), sem("cv_var"), sem("cv_std"), sem("cv_norm")
        cv_back, cv_ready = sem("cv_back"), sem("cv_ready")
        y_done, y_merged = sem("y_done"), sem("y_merged")
        lora_var, lora_std, lora_norm, lora_turned, lora_ready = (
            sem("lora_var"), sem("lora_std"), sem("lora_norm"), sem("lora_turned"), sem("lora_ready"))
        up_pair, up_taken, qv_done, v_taken, q_rotated = sem("up_pair"), sem("up_taken"), sem("qv_done"), sem("v_taken"), sem("q_rotated")
        rot_turned, rot_ready = sem("rot_turned"), sem("rot_ready")
        score_done, max_ready, exp_ready, prob_ready = sem("score_done"), sem("max_ready"), sem("exp_ready"), sem("prob_ready")
        probT_done, probT_ready, mo_done, mo_ready = sem("probT_done"), sem("probT_ready"), sem("mo_done"), sem("mo_ready")
        mix_done = sem("mix_done")
        diag_ready, grow_done, grow_ready, conv_ready = sem("diag_ready"), sem("grow_done"), sem("grow_ready"), sem("conv_ready")
        a_rotated, a_turned, a_qk_ready = sem("a_rotated"), sem("a_turned"), sem("a_qk_ready")
        a_scored, a_masked, a_max, a_exp = sem("a_scored"), sem("a_masked"), sem("a_max"), sem("a_exp")
        a_pT_done, a_pT_ready, a_o_done, a_o_ready = sem("a_pT_done"), sem("a_pT_ready"), sem("a_o_done"), sem("a_o_ready")
        a_oT_done, a_oT_ready = sem("a_oT_done"), sem("a_oT_ready")
        route_done, route_exp, route_ready = sem("route_done"), sem("route_exp"), sem("route_ready")
        chosen_ready, counted, plan_ready = sem("chosen_ready"), sem("counted"), sem("plan_ready")
        pick_ready, gathered, x_ready = sem("pick_ready"), sem("gathered"), sem("x_ready")
        weigh_ready, weigh_turned, weigh_taken = sem("weigh_ready"), sem("weigh_turned"), sem("weigh_taken")
        slots_taken, scattered, sum_done = sem("slots_taken"), sem("scattered"), sem("sum_done")
        out_ready, stored = sem("out_ready"), sem("stored")

        block = ctx.enter_context(nc.Block())

        @block.sync
        def _(sp):
            def row(ap):
                return ap.to_broadcast([P, ap.shape[-1]])

            def ffn_loads(gate, up, down, n, mod=None, extra=None):
                def loads(s, c, j):
                    sp.wait_ge(gate_done, n + s + 1)
                    sp.dma_start(gate_w[:], gate[:, :, c]).then_inc(gate_in, 16)
                    sp.wait_ge(up_done, n + s + 1)
                    sp.dma_start(up_w[:], up[:, :, c]).then_inc(up_in, 16)
                    if mod is not None:
                        mod_load(s, c)
                    sp.wait_ge(down_done, n + s + 1)
                    sp.dma_start(down_w[:], down[:, j, :]).then_inc(down_in, 16)

                def mod_load(s, c):
                    source, m = mod
                    sp.wait_ge(mod_used, m * MOD_UNITS + s + 1)
                    sp.dma_start(mod_w, source[:, :, c]).then_inc(mod_in, 16)

                for s in (0, 1):
                    loads(s, slice(s * FSTEP, (s + 1) * FSTEP), slice(s * FB, (s + 1) * FB))
                if extra is not None:
                    extra()
                with sp.Fori(2, NS) as s:
                    loads(s, bass.ds(s * FSTEP, FSTEP), bass.ds(s * FB, FB))
                if mod is not None:
                    mod_load(NS, slice(NS * MOD_COLS, 3 * D))

            def by_k(ap):
                return ap.rearrange("(k p) n -> p k n", p=P)

            def of_layer(name, l):
                w = a[name][bass.ds(l, 1)]
                return w.rearrange("o (k p) n -> p (o k) n", p=P)

            def panel_load(pieces, use, parity, l=None):
                sp.wait_ge(panel_used, use + 1)
                at = 0
                for name, r0, nr, c0, cols in pieces:
                    k = -(-nr // P)
                    src = a[name][bass.ds(l, 1), r0:r0 + nr, c0:c0 + cols] if l is not None else a[name][0:1, r0:r0 + nr, c0:c0 + cols]
                    if nr % P:
                        dst = panel[parity][0:nr, at:at + cols]
                        src = src.rearrange("o p n -> p (o n)")
                    else:
                        dst = v3(panel[parity], at, k, cols)
                        src = src.rearrange("o (k p) n -> p (o k) n", p=P)
                    sp.dma_start(dst, src).then_inc(panel_in[parity], 16)
                    at += k * cols

            def norm_loads(which, l):
                sp.dma_start(row_g[:], row(a[which + "_g"][bass.ds(l, 1), :])).then_inc(norm_in, 16)
                sp.dma_start(row_b[:], row(a[which + "_b"][bass.ds(l, 1), :])).then_inc(norm_in, 16)

            def param_loads(l):
                def to(at, n, name, pat, **kw):
                    sp.dma_start(rows[at:at + n, 0, :], a[name][bass.ds(l, 1)].rearrange(pat, **kw)).then_inc(param_in, 16)
                to(ROW_GATE, 24, "b_gate", "o (b p) -> (o b) p", p=P)
                to(ROW_CONV, 48, "dn_conv_w", "o j (b p) -> (o j b) p", p=P)
                to(ROW_GLU, 8, "cv_glu_b", "o (b p) -> (o b) p", p=P)
                to(ROW_DWB, 4, "cv_dw_b", "o (b p) -> (o b) p", p=P)
                to(ROW_LNG, 4, "cv_ln_g", "o (b p) -> (o b) p", p=P)
                to(ROW_LNB, 4, "cv_ln_b", "o (b p) -> (o b) p", p=P)
                to(ROW_PW, 8, "cv_b_pw2", "o (b p) -> (o b) p", p=P)
                to(ROW_QN, QB, "mla_q_norm_w", "o (b p) -> (o b) p", p=P)
                to(ROW_KVN, KVB, "mla_kv_norm_w", "o (b p) -> (o b) p", p=P)
                sp.dma_start(rows[0:TAPS * CB, 1, :],
                             a["cv_dw_w"][bass.ds(l, 1)].rearrange("o j (b p) -> (o j b) p", p=P)).then_inc(param_in, 16)
                sp.dma_start(norm_row[:], row(a["dn_norm_w"][bass.ds(l, 1), :])).then_inc(param_in, 16)
                sp.dma_start(head_rows[:, 0:HEADS], row(a["dn_a_log"][bass.ds(l, 1), :])).then_inc(param_in, 16)
                sp.dma_start(head_rows[:, HEADS:], row(a["dn_dt_bias"][bass.ds(l, 1), :])).then_inc(param_in, 16)

            sp.dma_start(H[:], a["x"][0].rearrange("(t p) d -> p t d", p=P)).then_inc(setup_in, 16)
            sp.dma_start(rows[0:96, 0, :], a["mod_b_2"].rearrange("i j (b p) -> (i j b) p", p=P)).then_inc(setup_row, 16)
            sp.dma_start(rows[96:128, 0, :], a["norm_g_2"].rearrange("i j (b p) -> (i j b) p", p=P)).then_inc(setup_row, 16)
            sp.dma_start(rows[0:8, 1, :], a["c_2"].rearrange("o (b p) -> (o b) p", p=P)).then_inc(setup_row, 16)
            sp.dma_start(rows[8:32, 1, :], a["conv_w_2"][0].rearrange("j (b p) -> (j b) p", p=P)).then_inc(setup_row, 16)
            pos = small[0:2 * TT, 0:P].bitcast(I32)
            sp.dma_start(pos[0:TT, :], a["positions"].rearrange("o (t p) -> (o t) p", p=P)).then_inc(setup_row, 16)
            sp.dma_start(pos[TT:2 * TT, :], a["positions_2"].rearrange("o (t p) -> (o t) p", p=P)).then_inc(setup_row, 16)
            sp.dma_start(router[:], by_k(a["router_w_2"][0])).then_inc(setup_row, 16)

            with sp.Fori(0, DEPTH) as l:
                n = l * FFN_LAYER
                mod = a["mod_w_2"][bass.ds(l, 1)]

                def first_extra():
                    param_loads(l)
                    norm_loads("ln1", l)
                ffn_loads(of_layer("ffn1_w_gate", l), of_layer("ffn1_w_up", l), of_layer("ffn1_w_down", l), n,
                          (mod[:, 0].rearrange("o (k p) n -> p (o k) n", p=P), l * 2), first_extra)
                for use, (_, pieces) in enumerate(MIXER_PANELS):
                    panel_load(pieces, l * MIX_USES + use, use % 2, l)
                    if use == 4:
                        norm_loads("ln2", l)
                ffn_loads(of_layer("ffn2_w_gate", l), of_layer("ffn2_w_up", l), of_layer("ffn2_w_down", l), n + NS,
                          (mod[:, 1].rearrange("o (k p) n -> p (o k) n", p=P), l * 2 + 1), lambda: norm_loads("ln3", l))

            for use, (name, pieces) in enumerate(SECOND_PANELS):
                panel_load(pieces, DEPTH * MIX_USES + use, use % 2)
                if name == "conv_out" and use == 7:
                    ffn_loads(by_k(a["ffn_w_gate_2"][0]), by_k(a["ffn_w_up_2"][0]), by_k(a["ffn_w_down_2"][0]), DEPTH * FFN_LAYER)
            sp.wait_ge(plan_ready, 1)
            items = sp.value_load(plan[0:1, ITEMS:ITEMS + 1], min_val=1, max_val=ITEMS - 1)
            with sp.Fori(0, items) as i:
                e = sp.value_load(plan[0:1, bass.ds(i, 1)], min_val=0, max_val=NE - 1)
                expert = [a[name][0, bass.ds(e, 1)].rearrange("o (k p) n -> p (o k) n", p=P)
                          for name in ("moe_w_gate_2", "moe_w_up_2", "moe_w_down_2")]
                ffn_loads(*expert, DEPTH * FFN_LAYER + NS + i * NS)
            sp.wait_ge(norm_done, DEPTH * LN_LAYER * TT)
            sp.dma_start(row_b[:], row(a["final_g_2"].rearrange("(o d) -> o d", o=1))).then_inc(norm_in, 16)
            for t in range(TT):
                sp.wait_ge(out_ready, t + 1)
                sp.dma_start(out[0, t * P:(t + 1) * P, :], H[:, t, :]).then_inc(stored, 16)
            sp.wait_ge(stored, 16 * TT)

        @block.gpsimd
        def _(pool):
            def keep(tile, op, pattern, base, step, fill):
                pool.drain()
                nc.gpsimd.affine_select(out=tile, in_=tile, pattern=pattern, compare_op=op, fill=fill, base=base,
                                        channel_multiplier=step)

            for tile, value in ((ident, 0.0), (ones, 1.0), (causal, 0.0), (prefix, 1.0), (strict, 1.0), (same, 1.0),
                                (in_chunk, 0.0), (level, 1.0)):
                nc.gpsimd.memset(tile[:], value)
            nc.gpsimd.memset(glu_pad[:, :, 0:32], 0.0)
            for j in range(HALF):
                nc.gpsimd.memset(small[:, 160 + j:161 + j], float(np.float32(10000.0) ** np.float32(-j / HALF)))
            keep(ident[:], ALU.not_equal, [[-1, P]], 0, 1, 1.0)
            keep(causal[:], ALU.is_ge, [[-1, P]], 0, 1, MASKED)
            keep(prefix[:], ALU.is_ge, [[1, P]], 0, -1, 0.0)
            keep(strict[:], ALU.is_ge, [[-1, P]], -1, 1, 0.0)
            for i in range(6):
                b = 1 << i
                m = P // (2 * b)
                tile = level[:, i, :].rearrange("p (m s r) -> p m s r", s=2, r=b)
                keep(tile, ALU.is_ge, [[-2 * b, m], [0, 2], [0, b]], -b, 1, 0.0)
                keep(tile, ALU.is_ge, [[2 * b, m], [0, 2], [0, b]], 2 * b - 1, -1, 0.0)
            pool.drain()
            nc.gpsimd.memset(prefix[0:CHUNK, CHUNK:], 0.0)
            pool.drain()
            nc.gpsimd.memset(strict[CHUNK:, 0:CHUNK], 0.0)
            pool.drain()
            nc.gpsimd.memset(same[0:CHUNK, CHUNK:], 0.0)
            pool.drain()
            nc.gpsimd.memset(same[CHUNK:, 0:CHUNK], 0.0)
            for half in range(2):
                pool.drain()
                nc.gpsimd.memset(in_chunk[half * CHUNK:(half + 1) * CHUNK, half, :], 1.0)
            pool.drain()
            for i in range(6):
                b = 1 << i
                nc.gpsimd.memset(level[:, i, :].rearrange("p (m s r) -> p m s r", s=2, r=b)[:, :, 1, :], 0.0)
            pool.drain().then_inc(const_ready, 1)
            pool.wait_ge(angle_ready, 1)
            nc.gpsimd.memset(band[:, 0, :, :], 0.0)
            keep(band[:, 0, 1, :], ALU.is_ge, [[1, P]], 0, -1, MASKED)
            for g in range(AG):
                for i in (0, 2):
                    keep(band[:, g, i, :], ALU.is_ge, [[-1, P]], 0, 1, MASKED)
            pool.drain().then_inc(setup_done, 1)

            with pool.Fori(0, DEPTH) as l:
                pool.wait_ge(z_taken, l + 1)
                z = z_tok.rearrange("p t (h v) -> p (t h) v", h=HEADS)
                nc.gpsimd.tensor_tensor(z, z, norm_row[:].rearrange("p (o v) -> p o v", o=1).to_broadcast([P, TT * HEADS, HD]),
                                        ALU.mult).then_inc(z_scaled, 1)
                pool.wait_ge(lower_ready, l + 1)
                for i in range(1, 6):
                    if i > 1:
                        pool.wait_ge(turn_done, l * 10 + 2 * (i - 1))
                    nc.gpsimd.tensor_tensor(part.rearrange("p t h c -> p (t h) c"), lower.rearrange("p t h c -> p (t h) c"),
                                            level[:, i:i + 1, :].to_broadcast([P, TT * HEADS, P]), ALU.mult).then_inc(part_ready, 1)

        mm = nc.tensor.matmul

        def turn(out, tile):
            k = tile.shape[0]
            return nc.tensor.transpose(out, tile, ident[0:k, 0:k])

        def ffn_gate(pe, n, s, width=SEQ):
            pe.wait_ge(gate_in, (n + s) * 16 + 16)
            pe.wait_ge(silu_done, n + s + 1)
            for f in range(FB):
                for k in range(KD):
                    last = mm(banks[:, 4, f * width:(f + 1) * width], gate_w[:, k, f * P:(f + 1) * P], HT[:, k, 0:width],
                              start=k == 0, stop=k == KD - 1)
            last.then_inc(gate_done, 1)

        def ffn_up(pe, n, s, width=SEQ):
            pe.wait_ge(up_in, (n + s) * 16 + 16)
            for f in range(FB):
                for k in range(KD):
                    last = mm(banks[:, 5, f * width:(f + 1) * width], up_w[:, k, f * P:(f + 1) * P], HT[:, k, 0:width],
                              start=k == 0, stop=k == KD - 1)
            last.then_inc(up_done, 1)

        def ffn_down(pe, n, s, first=False, final=False, width=SEQ):
            pe.wait_ge(down_in, (n + s) * 16 + 16)
            pe.wait_ge(act_ready, n + s + 2)
            for f in range(FB):
                for t in range(width // P):
                    for c in range(2):
                        last = mm(banks[:, 2 * t + c, :], act_t[:, f, t * P:(t + 1) * P], down_w[:, f, c * 512:(c + 1) * 512],
                                  start=first and f == 0, stop=final and f == FB - 1)
            last.then_inc(down_done, 1)

        def ffn_pe(pe, n, ht):
            pe.wait_ge(ht_ready, ht)
            ffn_gate(pe, n, 0)
            ffn_up(pe, n, 0)
            ffn_gate(pe, n, 1)
            ffn_down(pe, n, 0, first=True)
            ffn_up(pe, n, 1)
            with pe.Fori(2, NS) as s:
                ffn_gate(pe, n, s)
                ffn_down(pe, n, s - 1)
                ffn_up(pe, n, s)
            ffn_down(pe, n, NS - 1, final=True)

        def gather_pe(pe, i):
            pe.wait_ge(pick_ready, i + 1)
            for b in range(KD):
                for t in range(TT):
                    last = mm(banks[:, 6 + b // 4, (b % 4) * P:(b % 4 + 1) * P], x_norm[:, t, b * P:(b + 1) * P], pick[:, t, :],
                              start=t == 0, stop=t == TT - 1)
            last.then_inc(gathered, 1)

        def expert_pe(pe, n, i):
            pe.wait_ge(x_ready, i + 1)
            ffn_gate(pe, n, 0, P)
            ffn_up(pe, n, 0, P)
            pe.wait_ge(weigh_ready, i + 1)
            pe.wait_ge(sum_done, i * 2 + 2)
            for t in range(TT):
                last = turn(banks[:, 2, t * P:(t + 1) * P], weigh[:, t, :])
            last.then_inc(weigh_turned, 1)
            ffn_gate(pe, n, 1, P)
            ffn_down(pe, n, 0, first=True, width=P)
            ffn_up(pe, n, 1, P)
            with pe.Fori(2, NS) as s:
                ffn_gate(pe, n, s, P)
                ffn_down(pe, n, s - 1, width=P)
                ffn_up(pe, n, s, P)
            gather_pe(pe, i + 1)
            ffn_down(pe, n, NS - 1, final=True, width=P)
            pe.wait_ge(slots_taken, i + 1)
            pe.wait_ge(weigh_taken, i + 1)
            pe.wait_ge(x_ready, i + 2)
            for t in range(TT):
                for c in range(2):
                    last = mm(banks[:, (2, 6)[t] + c, :], weighT[:, t, :], slot_out[:, c * 512:(c + 1) * 512], start=True, stop=True)
                last.then_inc(scattered, 1)

        def mod_pe(pe, m):
            pe.wait_ge(mod_summed, m + 1)
            for b in range(24):
                last = mm(banks[:, 4, b:b + 1], mod_sum[:, b * P:(b + 1) * P], ones[:, 0:1], start=True, stop=True)
            last.then_inc(mod_col_done, 1)

        def turn_h(pe, done=None):
            for t in range(TT):
                if done is not None:
                    pe.wait_ge(norm_done, done + t + 1)
                for half in range(2):
                    for j in range(4):
                        b = 4 * half + j
                        last = turn(banks[:, (6, 4)[t] + half, j * P:(j + 1) * P], H[:, t, b * P:(b + 1) * P])
                    last.then_inc(turned, 1)

        act_fn = nc.scalar.activation

        def ffn_act(act, n, width=SEQ, between=None):
            def silu(s):
                act.wait_ge(gate_done, n + s + 2)
                act.wait_ge(act_ready, n + s + 1)
                act_fn(ffn_tmp[:, 0:FB * width], banks[:, 4, 0:FB * width], ACT.Silu).then_inc(silu_done, 1)
            silu(0)
            if between is not None:
                between()
            with act.Fori(1, NS) as s:
                silu(s)

        def std_act(act, m, eps):
            act.wait_ge(var_ready, m)
            act_fn(spread[:, :, 0], moments[:, :, 1], ACT.Sqrt, bias=eps).then_inc(std_ready, 1)

        def ht_act(act, before):
            for i in range(4):
                t, half = i // 2, i % 2
                act.wait_ge(turned, before + i + 1)
                act_fn(HT[:, 4 * half:4 * half + 4, t * P:(t + 1) * P],
                       banks[:, (6, 4)[t] + half, :].rearrange("p (b c) -> p b c", b=4), ACT.Copy).then_inc(ht_ready, 1)

        tt, ts, stt = nc.vector.tensor_tensor, nc.vector.tensor_scalar, nc.vector.scalar_tensor_tensor

        def wide(ap, *dims):
            if len(dims) == 2:
                return ap.rearrange("p (a o) -> p a o", o=1).to_broadcast([P, *dims])
            return ap.rearrange("p (a b o) -> p a b o", b=dims[1], o=1).to_broadcast([P, *dims])

        def mod_vec(dve, m, j, cols):
            dve.wait_ge(mod_in, (m * MOD_UNITS + j) * 16 + 16)
            ts(mod_sum[:, cols], mod_w[:, 0, :], misc_col[:, 0:1], None, ALU.mult)
            for k in range(1, KD):
                dve.drain()
                stt(mod_sum[:, cols], mod_w[:, k, :], misc_col[:, k:k + 1], mod_sum[:, cols], ALU.mult, ALU.add)
            dve.drain().then_inc(mod_used, 1)

        def ffn_vec(dve, n, m=None, width=SEQ):
            def act_step(s):
                dve.wait_ge(silu_done, n + s + 2)
                dve.wait_ge(up_done, n + s + 2)
                tt(act_t[:, :, 0:width], v3(ffn_tmp, 0, FB, width), banks[:, 5, 0:FB * width].rearrange("p (f t) -> p f t", f=FB),
                   ALU.mult).then_inc(act_ready, 1)
            act_step(0)
            if m is not None:
                mod_vec(dve, m, 0, slice(0, MOD_COLS))
            with dve.Fori(1, NS) as s:
                act_step(s)
                if m is not None:
                    mod_vec(dve, m, s, bass.ds(s * MOD_COLS, MOD_COLS))
            if m is not None:
                mod_vec(dve, m, NS, slice(NS * MOD_COLS, 3 * D))
                dve.drain().then_inc(mod_summed, 1)

        def layer_norm(dve, m, scale, mod=None):
            for t in range(TT):
                stt(H[:, t, :], H[:, t, :], scale, acc[:, t, :], ALU.mult, ALU.add)
            if mod is not None:
                dve.wait_ge(mod_col_done, mod + 1)
                tt(mod_col[:, bass.ds(mod * 24, 24)], banks[:, 4, 0:24], mod_bias[:, bass.ds(mod * 24, 24)], ALU.add)
            dve.drain()
            for t in range(TT):
                for half in range(2):
                    nc.vector.bn_stats(stats[:, t, half, :], H[:, t, half * 512:(half + 1) * 512])
            dve.drain()
            for t in range(TT):
                nc.vector.bn_aggr(moments[:, t, :], stats[:, t, :, :])
            dve.drain().then_inc(var_ready, 1)
            dve.wait_ge(std_ready, m)
            nc.vector.reciprocal(spread[:, :, 1], spread[:, :, 0])
            dve.drain()
            dve.wait_ge(norm_in, m * 32)
            for t in range(TT):
                ts(H[:, t, :], H[:, t, :], moments[:, t, 0:1], spread[:, t, 1:2], ALU.subtract, ALU.mult)
                dve.drain()
                tt(H[:, t, :], H[:, t, :], row_g[:], ALU.mult)
                dve.drain()
                tt(H[:, t, :], H[:, t, :], row_b[:], ALU.add).then_inc(norm_done, 1)

        def mixer_pe(pe, l):
            def panel_ready(use):
                pe.wait_ge(panel_in[use % 2], l * LANDED_LAYER[use % 2] + landed(use))
                return panel[use % 2]

            def pair_bank(i):
                if i >= 4:
                    pe.wait_ge(pair_taken, l * 23 + i - 3)
                return banks[:, 4 + i % 4, :]

            def project(tile, c, bank, half):
                for k in range(KD):
                    last = mm(bank[:, half * SEQ:(half + 1) * SEQ], tile[:, k, c:c + P], HT[:, k, :], start=k == 0, stop=k == KD - 1)
                return last

            def projection(use, first_pair):
                tile = v3(panel_ready(use), 0, KD, PANEL)
                for j in range(2):
                    bank = pair_bank(first_pair + j)
                    for half in range(2):
                        last = project(tile, (2 * j + half) * P, bank, half)
                    last.then_inc(pair_done, 1)
                    if j == 1:
                        pe.drain().then_inc(panel_used, 1)

            pe.wait_ge(param_in, l * 208 + 208)
            pe.wait_ge(ht_ready, l * 12 + 8)
            turn(banks[:, 7, 0:ROWS], rows[0:ROWS, 0, :])
            turn(banks[:, 7, P:P + TAPS * CB], rows[0:TAPS * CB, 1, :]).then_inc(param_turned, 1)
            for use in range(3):
                projection(use, 2 * use)
                if use == 0:
                    pe.wait_ge(param_ready, l + 1)
            for use in range(2):
                projection(3 + use, 6 + 2 * use)
            tile = v3(panel_ready(5), 0, KD, 520)
            small_bank = pair_bank(10)
            for t in range(TT):
                for k in range(KD):
                    last = mm(banks[:, t, :], HT[:, k, t * P:(t + 1) * P], tile[:, k, 0:512], start=k == 0, stop=k == KD - 1)
            last.then_inc(z_done, 1)
            for t in range(TT):
                for k in range(KD):
                    mm(small_bank[:, 8 * t:8 * t + 8], HT[:, k, t * P:(t + 1) * P], tile[:, k, 512:520],
                       start=k == 0, stop=k == KD - 1)
            pe.drain().then_inc(panel_used, 1)
            tile = v3(panel_ready(6), 0, KD, PANEL)
            for t in range(TT):
                for k in range(KD):
                    mm(banks[:, 2 + t, :], HT[:, k, t * P:(t + 1) * P], tile[:, k, :], start=k == 0, stop=k == KD - 1)
            pe.drain().then_inc(panel_used, 1)
            tile = v3(panel_ready(7), 0, KD, 192)
            for t in range(TT):
                for k in range(KD):
                    last = mm(small_bank[:, 16 + 192 * t:208 + 192 * t], HT[:, k, t * P:(t + 1) * P], tile[:, k, :],
                              start=k == 0, stop=k == KD - 1)
            last.then_inc(lora_done, 1)
            pe.drain().then_inc(panel_used, 1)

            pe.wait_ge(qkv_silu, l + 1)
            pe.wait_ge(z_taken, l + 1)
            pe.wait_ge(lora_taken, l + 1)
            for which in range(2):
                for t in range(TT):
                    for h in range(HEADS):
                        last = turn(banks[:, 2 * which + t, h * HD:(h + 1) * HD], conv[:, 4 * which + h, t * P:(t + 1) * P])
            last.then_inc(tok_done, 1)
            projection(8, 11)
            pe.wait_ge(tok_scaled, l + 1)
            for t in range(TT):
                for h in range(HEADS):
                    last = turn(banks[:, t, h * HD:(h + 1) * HD], conv[:, 8 + h, t * P:(t + 1) * P])
            last.then_inc(v_done, 1)
            for h in range(HEADS):
                for t in range(TT):
                    last = turn(banks[:, 2 + h // 2, (h % 2) * SEQ + t * P:(h % 2) * SEQ + (t + 1) * P], q_tok[:, t, h, :])
            last.then_inc(back_done, 1)
            projection(9, 13)
            pe.wait_ge(v_copied, l + 1)
            for h in range(HEADS):
                for t in range(TT):
                    last = turn(banks[:, h // 2, (h % 2) * SEQ + t * P:(h % 2) * SEQ + (t + 1) * P], k_tok[:, t, h, :])
            last.then_inc(back_done, 1)
            pe.wait_ge(back_copied, l * 2 + 1)
            pe.wait_ge(decay_in, l + 1)
            for t in range(TT):
                for h in range(HEADS):
                    mm(banks[:, 2 + t, h * P:(h + 1) * P], g_wide[:, t, h, :], prefix[:], start=True, stop=True)
            pe.wait_ge(back_copied, l * 2 + 2)
            g = small[:, 0:8]
            for t in range(TT):
                gt = g[:, t * HEADS:(t + 1) * HEADS]
                mm(banks[:, 0, 4 * t:4 * t + 4], prefix[:], gt, start=True, stop=True)
                mm(banks[:, 0, 8 + 4 * t:12 + 4 * t], same[:], gt, start=True, stop=True)
                for half in range(2):
                    c = 2 * t + half
                    last = mm(banks[:, 0, 16 + 4 * c:20 + 4 * c], in_chunk[:, half, :], gt, start=True, stop=True)
            last.then_inc(cum_done, 1)
            projection(10, 15)
            pe.wait_ge(cum_taken, l + 1)
            for t in range(TT):
                for h in range(HEADS):
                    mm(banks[:, t, h * P:(h + 1) * P], kT[:, h, t * P:(t + 1) * P], kT[:, h, t * P:(t + 1) * P], start=True, stop=True)
            pe.wait_ge(e_row_ready, l + 1)
            for t in range(TT):
                for h in range(HEADS):
                    last = mm(banks[:, 2 + t, h * P:(h + 1) * P], kT[:, h, t * P:(t + 1) * P], qT[:, h, t * P:(t + 1) * P], start=True, stop=True)
            last.then_inc(kk_done, 1)
            projection(11, 17)
            pe.wait_ge(inv_start, l + 1)
            for t in range(TT):
                for h in range(HEADS):
                    last = turn(banks[:, t, h * P:(h + 1) * P], inv[:, t, h, :])
            last.then_inc(start_done, 1)
            for i in range(5):
                pe.wait_ge(part_ready, l * 5 + i + 1)
                for t in range(TT):
                    if i == 0:
                        pe.wait_ge(inv_ready, l + 1)
                    else:
                        pe.wait_ge(step_done, l * 10 + 2 * (i - 1) + t + 1)
                    for h in range(HEADS):
                        last = mm(banks[:, t, h * P:(h + 1) * P], part[:, t, h, :], inv_t[:, t, h, :], start=True, stop=True)
                    last.then_inc(turn_done, 1)
                if i < 2:
                    projection(12 + i, 19 + 2 * i)
                for t in range(TT):
                    pe.wait_ge(turn_copied, l * 10 + 2 * i + t + 1)
                    if i < 4:
                        for h in range(HEADS):
                            mm(banks[:, 2 + t, h * P:(h + 1) * P], turn_b[:, t, h, :], inv[:, t, h, :], start=True, stop=True)
                    for h in range(HEADS):
                        last = mm(banks[:, t, h * P:(h + 1) * P], inv[:, t, h, :], turn_b[:, t, h, :], start=True, stop=True)
                    last.then_inc(join_done, 1)
            pe.wait_ge(cv_conv, l + 1)
            pe.wait_ge(pair_taken, l * 23 + 23)
            for t in range(TT):
                for b in range(CB):
                    last = turn(banks[:, 4 + t, b * P:(b + 1) * P], cv_acc[:, b, t * P:(t + 1) * P])
            last.then_inc(cv_turned, 1)
            pe.wait_ge(step_done, l * 10 + 10)
            for t in range(TT):
                for h in range(HEADS):
                    mm(banks[:, t, h * HD:(h + 1) * HD], inv_t[:, t, h, :], v_beta[:, t, h, :], start=True, stop=True)
            for t in range(TT):
                for h in range(HEADS):
                    last = mm(banks[:, 2 + t, h * P:(h + 1) * P], k_beta[:, t, h, :], inv_t[:, t, h, :], start=True, stop=True)
            last.then_inc(uw_done, 1)
            pe.wait_ge(cv_norm, l + 1)
            for t in range(TT):
                for b in range(CB):
                    last = turn(banks[:, 6 + b // 2, (b % 2) * SEQ + t * P:(b % 2) * SEQ + (t + 1) * P], cv_tok[:, t, b * P:(b + 1) * P])
            last.then_inc(cv_back, 1)

            def out_pairs(tile, src, kb, j, y, need, count):
                pe.wait_ge(need, count)
                for half in range(2):
                    b = 2 * j + half
                    for k in range(kb):
                        last = mm(banks[:, 4 + j, half * SEQ:(half + 1) * SEQ], tile[:, k, b * P:(b + 1) * P], src[:, k, :],
                                  start=k == 0, stop=k == kb - 1)
                last.then_inc(y_done, 1)

            pe.wait_ge(uw_copied, l + 1)
            cv_tile = v3(panel_ready(14), 0, CB, D)
            for c in range(4):
                t, r = c // 2, slice((c % 2) * CHUNK, (c % 2 + 1) * CHUNK)
                state = states[(c + 1) % 2]
                if c:
                    pe.wait_ge(state_ready, l * 3 + c)
                    for h in range(HEADS):
                        last = mm(banks[:, 0, h * HD:(h + 1) * HD], wT[:, t, h, :], state[:, h, :], start=True, stop=True)
                    last.then_inc(read_done, 1)
                    pe.wait_ge(v_new_ready, l * 3 + c)
                    if c > 1:
                        pe.wait_ge(o_copied, l * 4 + c)
                src = v_new if c else u_tok
                if c < 3:
                    for h in range(HEADS):
                        last = mm(banks[:, 2, h * HD:(h + 1) * HD], k_dec[r, t, h, :], src[r, t, h, :], start=True, stop=True)
                    last.then_inc(write_done, 1)
                if c == 1:
                    pe.wait_ge(o_copied, l * 4 + c)
                for h in range(HEADS):
                    if c:
                        mm(banks[:, 1, h * HD:(h + 1) * HD], e_row[:, t, h, :], state[:, h, :], start=True, stop=False)
                    last = mm(banks[:, 1, h * HD:(h + 1) * HD], qk[r, t, h, :], src[r, t, h, :], start=not c, stop=True)
                last.then_inc(o_done, 1)
                if c == 0:
                    pe.wait_ge(cv_ready, l * 2 + 2)
                out_pairs(cv_tile, cvT, CB, c, 0, cv_ready, l * 2 + 2)
            pe.drain().then_inc(panel_used, 1)
            pe.wait_ge(o_ready, l + 1)
            for h in range(HEADS):
                for t in range(TT):
                    last = turn(banks[:, h // 2, (h % 2) * SEQ + t * P:(h % 2) * SEQ + (t + 1) * P], o_tok[:, t, h, :])
            last.then_inc(o_turned, 1)
            tile = v3(panel_ready(15), 0, HEADS, D)
            pe.wait_ge(oT_ready, l + 1)
            for j in range(4):
                out_pairs(tile, oT, HEADS, j, 1, y_merged, l * 12 + j + 1)
            pe.drain().then_inc(panel_used, 1)

            pe.wait_ge(lora_norm, l + 1)
            for b in range(QB + KVB):
                bank = (0, 0, 1, 2, 2)[b]
                at = (0, SEQ, 0, 0, SEQ)[b]
                for t in range(TT):
                    last = turn(banks[:, bank, at + t * P:at + (t + 1) * P], lora[:, t, b * P:(b + 1) * P])
            last.then_inc(lora_turned, 1)
            tile = panel_ready(16)
            uq = v3(tile, 0, QB, HEADS * (NOPE + ROPE))
            ukv = v3(tile, QB * HEADS * (NOPE + ROPE), KVB, HEADS * (NOPE + VD))
            uq_h = uq.rearrange("p k (h c) -> p k h c", h=HEADS)
            ukv_h = ukv.rearrange("p k (h c) -> p k h c", h=HEADS)
            pe.wait_ge(lora_ready, l + 1)
            for t in range(TT):
                for k in range(QB):
                    mm(banks[:, 3, t * SEQ:(t + 1) * SEQ].rearrange("p (h c) -> p h c", h=HEADS), cqT[:, k, t * P:(t + 1) * P],
                       uq_h[:, k, :, NOPE:], start=k == 0, stop=k == QB - 1)
            for t in range(TT):
                for k in range(KVB):
                    last = mm(banks[:, t, :].rearrange("p (h c) -> p h c", h=HEADS), ckvT[:, k, t * P:(t + 1) * P],
                              ukv_h[:, k, :, NOPE:], start=k == 0, stop=k == KVB - 1)
            last.then_inc(qv_done, 1)
            for j in range(4):
                pe.wait_ge(y_merged, l * 12 + 4 + j + 1)
                src, w, kb = (cqT, uq_h, QB) if j < 2 else (ckvT, ukv_h, KVB)
                for half in range(2):
                    h = 2 * (j % 2) + half
                    for k in range(kb):
                        last = mm(banks[:, 4 + j, half * SEQ:(half + 1) * SEQ], w[:, k, h, 0:NOPE], src[:, k, :],
                                  start=k == 0, stop=k == kb - 1)
                last.then_inc(up_pair, 1)
            pe.drain().then_inc(panel_used, 1)
            pe.wait_ge(q_rotated, l + 1)
            for j in range(2):
                for t in range(TT):
                    turn(banks[:, 2, j * SEQ + t * P:j * SEQ + (t + 1) * P],
                         q_rot[:, t, 2 * j:2 * j + 2, :].rearrange("p h c -> p (h c)"))
            for t in range(TT):
                last = turn(banks[:, 3, t * P:(t + 1) * P], k_rot[:, t, :, :].rearrange("p h c -> p (h c)"))
            last.then_inc(rot_turned, 1)
            pe.wait_ge(up_taken, l * 4 + 4)
            pe.wait_ge(rot_ready, l + 1)
            for h in range(HEADS):
                r = slice((h % 2) * ROPE, (h % 2 + 1) * ROPE)
                for t in range(TT):
                    n = (t + 1) * P
                    dst = banks[:, 4 + 3 * (h % 2), (h // 2) * P:(h // 2 + 1) * P] if t == 0 else banks[:, 5 + h % 2, (h // 2) * SEQ:(h // 2 + 1) * SEQ]
                    mm(dst, qnT[:, h, t * P:(t + 1) * P], knT[:, h, 0:n], start=True, stop=False)
                    last = mm(dst, qrT[r, h // 2, t * P:(t + 1) * P], krT[r, 0:n], start=False, stop=True)
            last.then_inc(score_done, 1)
            pe.wait_ge(v_taken, l + 1)
            pe.wait_ge(prob_ready, l + 1)
            for h in range(HEADS):
                for i in range(3):
                    src = first_s[:, h, :] if i == 0 else second_s[:, h, (i - 1) * P:i * P]
                    last = turn(banks[:, (h * 3 + i) // 4, ((h * 3 + i) % 4) * P:((h * 3 + i) % 4 + 1) * P], src)
            last.then_inc(probT_done, 1)
            pe.wait_ge(probT_ready, l + 1)
            for h in range(HEADS):
                dst = banks[:, 4 + h // 2, (h % 2) * SEQ:(h % 2 + 1) * SEQ]
                mm(dst[:, 0:P], v_tok[:, 0, h * VD:(h + 1) * VD], probT[:, h, 0, :], start=True, stop=True)
                for kt in range(TT):
                    last = mm(dst[:, P:], v_tok[:, kt, h * VD:(h + 1) * VD], probT[:, h, 1 + kt, :], start=kt == 0, stop=kt == TT - 1)
            last.then_inc(mo_done, 1)
            tile = v3(panel_ready(17), 0, HEADS, D)
            pe.wait_ge(mo_ready, l + 1)
            for j in range(4):
                out_pairs(tile, moT, HEADS, j, 2, mo_ready, l + 1)
            pe.drain().then_inc(panel_used, 1)
            for i in range(2):
                tile = v3(panel_ready(18 + i), 0, 4, D)
                for k in range(4):
                    if k % 2 == 0:
                        pe.wait_ge(y_merged, l * 12 + 8 + (4 * i + k) // 2 + 1)
                    for t in range(TT):
                        for c in range(2):
                            last = mm(banks[:, 2 * t + c, :], merged[:, 4 * i + k, t * P:(t + 1) * P], tile[:, k, c * 512:(c + 1) * 512],
                                      start=i == 0 and k == 0, stop=i == 1 and k == 3)
                pe.drain().then_inc(panel_used, 1)
            pe.drain().then_inc(mix_done, 1)

        def mixer_act(act, l):
            def copy(out, src):
                return act_fn(out, src, ACT.Copy)

            def flat(ap):
                return ap.rearrange("p a b -> p (a b)")

            def gate_pair(i):
                act.wait_ge(pair_done, l * 22 + i)
                for half in range(2):
                    b = 2 * (i - 11) + half
                    last = act_fn(gates[:, b, :], banks[:, 4 + i % 4, half * SEQ:(half + 1) * SEQ], ACT.Sigmoid,
                                  bias=pcol[:, ROW_GATE + b:ROW_GATE + b + 1])
                last.then_inc(pair_taken, 1)

            act.wait_ge(param_turned, l + 1)
            copy(pcol[:, 0:ROWS], banks[:, 7, 0:ROWS])
            copy(dwcol[:, 0:TAPS * CB], banks[:, 7, P:P + TAPS * CB]).then_inc(param_ready, 1)
            for i in range(6):
                act.wait_ge(pair_done, l * 22 + i + 1)
                copy(raw[:, 2 * i:2 * i + 2, 4:260], banks[:, 4 + i % 4, :].rearrange("p (a b) -> p a b", a=2)).then_inc(pair_taken, 1)
            act.drain()
            for i in range(6, 10):
                act.wait_ge(pair_done, l * 22 + i + 1)
                for half in range(2):
                    b = 2 * (i - 6) + half
                    dst = glu_a[:, b, :] if b < CB else glu_s[:, b - CB, :]
                    last = act_fn(dst, banks[:, 4 + i % 4, half * SEQ:(half + 1) * SEQ], ACT.Identity if b < CB else ACT.Sigmoid,
                                  bias=pcol[:, ROW_GLU + b:ROW_GLU + b + 1])
                last.then_inc(pair_taken, 1)
            act.wait_ge(qkv_conv, l + 1)
            for i in range(3):
                last = act_fn(flat(conv[:, 4 * i:4 * i + 4, :]), flat(conv[:, 4 * i:4 * i + 4, :]), ACT.Silu)
            last.then_inc(qkv_silu, 1)
            act.wait_ge(z_done, l + 1)
            for t in range(TT):
                last = act_fn(z_tok[:, t, :], banks[:, t, :], ACT.Silu)
            last.then_inc(z_taken, 1)
            act.wait_ge(lora_done, l + 1)
            copy(flat(logits), banks[:, 6, 0:16])
            copy(lora[:, :, 512:704], banks[:, 6, 16:400].rearrange("p (t c) -> p t c", t=TT)).then_inc(pair_taken, 1)
            for t in range(TT):
                last = copy(lora[:, t, 0:512], banks[:, 2 + t, :])
            last.then_inc(lora_taken, 1)
            act.wait_ge(tok_done, l + 1)
            for i in range(4):
                last = act_fn(qk_sq[:, i, :, :].rearrange("p h c -> p (h c)"), banks[:, i, :], ACT.Square)
            last.then_inc(tok_sq, 1)
            act.wait_ge(soft_ready, l + 1)
            act_fn(v3(small, 8, TT, HEADS), logits[:, :, HEADS:], ACT.Sigmoid)
            act_fn(neg_a, head_rows[:, 0:HEADS], ACT.Exp)
            act_fn(soft_n, soft_n, ACT.Exp)
            act.drain()
            act_fn(soft_n, soft_n, ACT.Ln, bias=1.0).then_inc(gate_log, 1)
            act.wait_ge(tok_var, l + 1)
            act_fn(tok_sum, tok_sum, ACT.Sqrt, bias=L2_EPS).then_inc(tok_std, 1)
            gate_pair(11)
            gate_pair(12)
            act.wait_ge(v_done, l + 1)
            for t in range(TT):
                last = copy(v_beta[:, t, :, :].rearrange("p h c -> p (h c)"), banks[:, t, :])
            last.then_inc(v_copied, 1)
            act.wait_ge(back_done, l * 2 + 1)
            for i in range(2):
                last = copy(flat(qT[:, 2 * i:2 * i + 2, :]), banks[:, 2 + i, :])
            last.then_inc(back_copied, 1)
            gate_pair(13)
            gate_pair(14)
            act.wait_ge(back_done, l * 2 + 2)
            for i in range(2):
                last = copy(flat(kT[:, 2 * i:2 * i + 2, :]), banks[:, i, :])
            last.then_inc(back_copied, 1)
            act.wait_ge(clamp_ready, l + 1)
            for tile, sign in ((lower, -1.0), (qk, 1.0)):
                f = tile.rearrange("p t h c -> p (t h c)")
                last = act_fn(f, f, ACT.Exp, scale=sign)
            last.then_inc(decay_ready, 1)
            for t in range(TT):
                act_fn(e_row[:, t, :, :].rearrange("p h c -> p (h c)"), banks[:, 2 + t, :], ACT.Exp)
            act_fn(cum_e, cum, ACT.Exp)
            act_fn(dec_scale, dec_scale, ACT.Exp)
            act_fn(chunk_e, chunk_total, ACT.Exp).then_inc(e_row_ready, 1)
            for i in range(15, 19):
                gate_pair(i)
            act.wait_ge(start_done, l + 1)
            for t in range(TT):
                last = copy(inv_t[:, t, :, :].rearrange("p h c -> p (h c)"), banks[:, t, :])
            last.then_inc(inv_ready, 1)
            for i in range(5):
                for t in range(TT):
                    act.wait_ge(turn_done, l * 10 + 2 * i + t + 1)
                    if i:
                        act.wait_ge(join_done, l * 10 + 2 * (i - 1) + t + 1)
                    copy(turn_b[:, t, :, :].rearrange("p h c -> p (h c)"), banks[:, t, :]).then_inc(turn_copied, 1)
                if i < 2:
                    gate_pair(19 + 2 * i)
                    gate_pair(20 + 2 * i)
            act.wait_ge(lora_var, l + 1)
            act_fn(lora_scale, lora_ms, ACT.Sqrt, bias=LN_EPS).then_inc(lora_std, 1)
            act.wait_ge(cv_var, l + 1)
            act_fn(cv_scale, cv_mom[:, :, 1], ACT.Sqrt, bias=LN_EPS).then_inc(cv_std, 1)
            act.wait_ge(uw_done, l + 1)
            for t in range(TT):
                copy(u_tok[:, t, :, :].rearrange("p h c -> p (h c)"), banks[:, t, :])
            for t in range(TT):
                last = copy(wT[:, t, :, :].rearrange("p h c -> p (h c)"), banks[:, 2 + t, :])
            last.then_inc(uw_copied, 1)
            act.wait_ge(cv_back, l + 1)
            for b in range(CB):
                last = act_fn(cvT[:, b, :], banks[:, 6 + b // 2, (b % 2) * SEQ:(b % 2 + 1) * SEQ], ACT.Silu,
                              scale=pcol[:, ROW_LNG + b:ROW_LNG + b + 1], bias=pcol[:, ROW_LNB + b:ROW_LNB + b + 1])
                if b % 2:
                    last.then_inc(cv_ready, 1)
            for c in range(4):
                r = slice((c % 2) * CHUNK, (c % 2 + 1) * CHUNK)
                act.wait_ge(o_done, l * 4 + c + 1)
                copy(o_tok[r, c // 2, :, :].rearrange("p h c -> p (h c)"), banks[r, 1, :]).then_inc(o_copied, 1)
            act.wait_ge(o_var, l + 1)
            act_fn(o_scale, o_sum, ACT.Sqrt, scale=1.0 / HD, bias=LN_EPS).then_inc(o_std, 1)
            act.wait_ge(o_turned, l + 1)
            for i in range(2):
                last = copy(flat(oT[:, 2 * i:2 * i + 2, :]), banks[:, i, :])
            last.then_inc(oT_ready, 1)
            act.wait_ge(lora_turned, l + 1)
            for b in range(QB + KVB):
                bank, at = (0, 0, 1, 2, 2)[b], (0, SEQ, 0, 0, SEQ)[b]
                dst = cqT[:, b, :] if b < QB else ckvT[:, b - QB, :]
                last = act_fn(dst, banks[:, bank, at:at + SEQ], ACT.Identity, scale=pcol[:, ROW_QN + b:ROW_QN + b + 1], bias=0.0)
            last.then_inc(lora_ready, 1)
            act.wait_ge(qv_done, l + 1)
            for t in range(TT):
                last = copy(v_tok[:, t, :], banks[:, t, :])
            last.then_inc(v_taken, 1)
            for j in range(4):
                act.wait_ge(up_pair, l * 4 + j + 1)
                dst = qnT if j < 2 else knT
                copy(flat(dst[:, 2 * (j % 2):2 * (j % 2) + 2, :]), banks[:, 4 + j, :]).then_inc(up_taken, 1)
            act.wait_ge(rot_turned, l + 1)
            copy(flat(qrT), banks[:, 2, :])
            copy(krT, banks[:, 3, 0:SEQ]).then_inc(rot_ready, 1)
            act.wait_ge(max_ready, l + 1)
            for h in range(HEADS):
                for i, tile in enumerate((first_s, second_s)):
                    c = 4 * i + h
                    last = act_fn(tile[:, h, :], tile[:, h, :], ACT.Exp, scale=MLA_SCALE, bias=s_max[:, c:c + 1], accum_out=s_sum[:, c:c + 1])
            act.drain().then_inc(exp_ready, 1)
            act.wait_ge(probT_done, l + 1)
            for i in range(3):
                last = copy(probT.rearrange("p h i c -> p (h i c)")[:, i * 512:(i + 1) * 512], banks[:, i, :])
            last.then_inc(probT_ready, 1)
            act.wait_ge(mo_done, l + 1)
            for i in range(2):
                last = copy(flat(moT[:, 2 * i:2 * i + 2, :]), banks[:, 4 + i, :])
            last.then_inc(mo_ready, 1)

        def mixer_vec(dve, l):
            def one(ap):
                return ap.rearrange("p (o c) -> p o c", o=1)

            def th(ap):
                return ap.rearrange("p (t h) -> p t h", t=TT)

            nc.vector.memset(raw[:, :, 0:4], 0.0)
            dve.drain()
            dve.wait_ge(param_ready, l + 1)
            dve.wait_ge(pair_taken, l * 23 + 6)
            for j in range(4):
                for b in range(12):
                    w = pcol[:, ROW_CONV + 12 * j + b:ROW_CONV + 12 * j + b + 1]
                    if j == 0:
                        ts(conv[:, b, :], raw[:, b, 1:1 + SEQ], w, None, ALU.mult)
                    else:
                        stt(conv[:, b, :], raw[:, b, 1 + j:1 + j + SEQ], w, conv[:, b, :], ALU.mult, ALU.add)
                if j < 3:
                    dve.drain()
            dve.drain().then_inc(qkv_conv, 1)
            dve.wait_ge(pair_taken, l * 23 + 10)
            tt(glu_pad[:, :, 32:32 + SEQ], glu_a, glu_s, ALU.mult)
            for j in range(TAPS):
                dve.drain()
                for b in range(CB):
                    w = dwcol[:, CB * j + b:CB * j + b + 1]
                    src = glu_pad[:, b, 2 + j:2 + j + SEQ]
                    if j == 0:
                        ts(cv_acc[:, b, :], src, w, pcol[:, ROW_DWB + b:ROW_DWB + b + 1], ALU.mult, ALU.add)
                    else:
                        stt(cv_acc[:, b, :], src, w, cv_acc[:, b, :], ALU.mult, ALU.add)
            dve.drain().then_inc(cv_conv, 1)
            dve.wait_ge(lora_taken, l + 1)
            for t in range(TT):
                tt(soft_x[:, 4 * t:4 * t + 4], logits[:, t, 0:HEADS], head_rows[:, HEADS:], ALU.add)
            dve.drain()
            ts(soft_n, soft_x, -1.0, None, ALU.mult)
            dve.drain()
            tt(soft_n, soft_n, soft_x, ALU.min).then_inc(soft_ready, 1)
            dve.wait_ge(tok_sq, l + 1)
            nc.vector.tensor_reduce(tok_sum, qk_sq.rearrange("p a h c -> p (a h) c"), AX.X, ALU.add).then_inc(tok_var, 1)
            dve.wait_ge(gate_log, l + 1)
            ts(soft_x, soft_x, 0.0, None, ALU.max)
            ts(neg_a, neg_a, -1.0, None, ALU.mult)
            dve.drain()
            tt(soft_x, soft_x, soft_n, ALU.add)
            dve.drain()
            for t in range(TT):
                tt(log_g[:, 4 * t:4 * t + 4], soft_x[:, 4 * t:4 * t + 4], neg_a, ALU.mult)
            dve.wait_ge(tok_std, l + 1)
            nc.vector.reciprocal(tok_scale, tok_sum)
            dve.drain()
            for i in range(4):
                dst = (q_tok if i < 2 else k_tok)[:, i % 2, :, :]
                last = tt(dst, banks[:, i, :].rearrange("p (h c) -> p h c", h=HEADS), wide(tok_scale[:, 4 * i:4 * i + 4], HEADS, HD), ALU.mult)
            last.then_inc(tok_scaled, 1)
            dve.wait_ge(v_done, l + 1)
            nc.vector.tensor_copy(g_wide.rearrange("p t h c -> p (t h) c"), wide(log_g, TT * HEADS, P)).then_inc(decay_in, 1)
            dve.wait_ge(v_copied, l + 1)
            tt(v_beta.rearrange("p t h c -> p (t h) c"), v_beta.rearrange("p t h c -> p (t h) c"), wide(beta, TT * HEADS, HD), ALU.mult)
            dve.wait_ge(cum_done, l + 1)
            nc.vector.tensor_copy(small[:, 16:48], banks[:, 0, 0:32]).then_inc(cum_taken, 1)
            dve.drain()
            for t in range(TT):
                for h in range(HEADS):
                    row = banks[:, 2 + t, h * P:(h + 1) * P]
                    col = cum[:, 4 * t + h:4 * t + h + 1]
                    ts(lower[:, t, h, :], row, col, 0.0, ALU.subtract, ALU.max)
                    ts(qk[:, t, h, :], row, col, 0.0, ALU.subtract, ALU.min)
            tt(dec_scale, total, cum, ALU.subtract)
            dve.drain().then_inc(clamp_ready, 1)
            dve.wait_ge(decay_ready, l + 1)
            tt(lower.rearrange("p t h c -> p (t h) c"), lower.rearrange("p t h c -> p (t h) c"),
               one(strict[:]).to_broadcast([P, TT * HEADS, P]), ALU.mult)
            tt(qk.rearrange("p t h c -> p (t h) c"), qk.rearrange("p t h c -> p (t h) c"),
               one(prefix[:]).to_broadcast([P, TT * HEADS, P]), ALU.mult)
            dve.wait_ge(e_row_ready, l + 1)
            tt(k_scale, beta, cum_e, ALU.mult)
            dve.drain()
            k8 = k_tok.rearrange("p t h c -> p (t h) c")
            tt(k_beta.rearrange("p t h c -> p (t h) c"), k8, wide(k_scale, TT * HEADS, HD), ALU.mult)
            tt(k_dec.rearrange("p t h c -> p (t h) c"), k8, wide(dec_scale, TT * HEADS, HD), ALU.mult)
            dve.wait_ge(back_copied, l * 2 + 1)
            for t in range(TT):
                stt(e_row[:, t, :, :], e_row[:, t, :, :], DN_SCALE, qT[:, :, t * P:(t + 1) * P], ALU.mult, ALU.mult)
            dve.wait_ge(kk_done, l + 1)
            for t in range(TT):
                for h in range(HEADS):
                    stt(lower[:, t, h, :], banks[:, t, h * P:(h + 1) * P], beta[:, 4 * t + h:4 * t + h + 1], lower[:, t, h, :], ALU.mult, ALU.mult)
            for t in range(TT):
                f = qk[:, t, :, :].rearrange("p h c -> p (h c)")
                stt(f, banks[:, 2 + t, :], DN_SCALE, f, ALU.mult, ALU.mult)
            dve.drain().then_inc(lower_ready, 1)
            inv8 = inv.rearrange("p t h c -> p (t h) c")
            tt(inv8, lower.rearrange("p t h c -> p (t h) c"), level[:, 0:1, :].to_broadcast([P, TT * HEADS, P]), ALU.mult)
            dve.drain()
            tt(inv8, one(ident[:]).to_broadcast([P, TT * HEADS, P]), inv8, ALU.subtract).then_inc(inv_start, 1)
            for t in range(TT):
                nc.vector.bn_stats(lora_stats[:, t, 0, :], lora[:, t, 0:QL])
                nc.vector.bn_stats(lora_stats[:, t, 1, :], lora[:, t, QL:QL + KVL])
            dve.drain()
            for t in range(TT):
                for i in range(2):
                    nc.vector.bn_aggr(lora_mom[:, t, i, :], lora_stats[:, t, i, :])
            dve.drain()
            ms = v3(small, 224, TT, 2)
            tt(ms, lora_mom[:, :, :, 0], lora_mom[:, :, :, 0], ALU.mult)
            dve.drain()
            tt(ms, ms, lora_mom[:, :, :, 1], ALU.add).then_inc(lora_var, 1)
            for i in range(5):
                for t in range(TT):
                    dve.wait_ge(join_done, l * 10 + 2 * i + t + 1)
                    if i < 4:
                        f = inv[:, t, :, :].rearrange("p h c -> p (h c)")
                        tt(f, f, banks[:, 2 + t, :], ALU.subtract)
                    f = inv_t[:, t, :, :].rearrange("p h c -> p (h c)")
                    tt(f, f, banks[:, t, :], ALU.subtract).then_inc(step_done, 1)
                if i < 4:
                    dve.drain()
            dve.wait_ge(cv_turned, l + 1)
            for t in range(TT):
                nc.vector.bn_stats(cv_stats[:, t, :], banks[:, 4 + t, :])
            dve.drain()
            for t in range(TT):
                nc.vector.bn_aggr(cv_mom[:, t, :], cv_stats[:, t, :])
            dve.drain().then_inc(cv_var, 1)
            dve.wait_ge(lora_std, l + 1)
            dve.wait_ge(cv_std, l + 1)
            nc.vector.reciprocal(lora_scale, lora_scale)
            nc.vector.reciprocal(cv_scale, cv_scale)
            dve.drain()
            for t in range(TT):
                last = ts(cv_tok[:, t, :], banks[:, 4 + t, :], cv_mom[:, t, 0:1], cv_scale[:, t:t + 1], ALU.subtract, ALU.mult)
            last.then_inc(cv_norm, 1)
            for t in range(TT):
                ts(lora[:, t, 0:QL], lora[:, t, 0:QL], lora_scale[:, 2 * t:2 * t + 1], None, ALU.mult)
                last = ts(lora[:, t, QL:QL + KVL], lora[:, t, QL:QL + KVL], lora_scale[:, 2 * t + 1:2 * t + 2], None, ALU.mult)
            last.then_inc(lora_norm, 1)
            for c in range(4):
                t, r = c // 2, slice((c % 2) * CHUNK, (c % 2 + 1) * CHUNK)
                if c:
                    dve.wait_ge(read_done, l * 3 + c)
                    tt(v_new[r, t, :, :].rearrange("p h c -> p (h c)"), u_tok[r, t, :, :].rearrange("p h c -> p (h c)"),
                       banks[r, 0, :], ALU.subtract).then_inc(v_new_ready, 1)
                if c < 3:
                    dve.wait_ge(write_done, l * 3 + c + 1)
                    if c == 0:
                        nc.vector.tensor_copy(states[0].rearrange("p h c -> p (h c)"), banks[:, 2, :]).then_inc(state_ready, 1)
                    else:
                        for h in range(HEADS):
                            last = stt(states[c % 2][:, h, :], states[(c + 1) % 2][:, h, :], chunk_e[:, 4 * c + h:4 * c + h + 1], banks[:, 2, h * HD:(h + 1) * HD],
                                       ALU.mult, ALU.add)
                        last.then_inc(state_ready, 1)
                    dve.drain()
                dve.wait_ge(y_done, l * 12 + c + 1)
                for half in range(2):
                    b = 2 * c + half
                    last = stt(merged[:, b, :], banks[:, 4 + c, half * SEQ:(half + 1) * SEQ], pcol[:, ROW_PW + b:ROW_PW + b + 1],
                               gates[:, KD + b, :], ALU.add, ALU.mult)
                last.then_inc(y_merged, 1)
            dve.wait_ge(o_copied, l * 4 + 4)
            o8 = o_tok.rearrange("p t h c -> p (t h) c")
            sq8 = square.rearrange("p t (h c) -> p (t h) c", h=HEADS)
            tt(sq8, o8, o8, ALU.mult)
            dve.drain()
            nc.vector.tensor_reduce(o_sum, sq8, AX.X, ALU.add).then_inc(o_var, 1)
            dve.wait_ge(o_std, l + 1)
            nc.vector.reciprocal(o_scale, o_scale)
            dve.drain()
            tt(o8, o8, wide(o_scale, TT * HEADS, HD), ALU.mult)
            dve.drain()
            dve.wait_ge(z_scaled, l + 1)
            tt(o8, o8, z_tok.rearrange("p t (h c) -> p (t h) c", h=HEADS), ALU.mult).then_inc(o_ready, 1)

            def merge(j, first_y, first_gate):
                dve.wait_ge(y_done, l * 12 + first_y + j + 1)
                tt(branch, banks[:, 4 + j, :].rearrange("p (a b) -> p a b", a=2), gates[:, first_gate + 2 * j:first_gate + 2 * j + 2, :], ALU.mult)
                dve.drain()
                m = merged[:, 2 * j:2 * j + 2, :]
                tt(m, m, branch, ALU.add).then_inc(y_merged, 1)
                dve.drain()

            for j in range(4):
                merge(j, 4, 0)
            dve.wait_ge(qv_done, l + 1)
            for t in range(TT):
                q = banks[:, 3, t * SEQ:(t + 1) * SEQ].rearrange("p (h c) -> p h c", h=HEADS)
                k = lora[:, t, QL + KVL:704].rearrange("p (o c) -> p o c", o=1)
                for heads, src, dsts in ((HEADS, q, (q_rot[:, t, :, :],)), (1, k, (k_rot[:, t, 0:1, :], k_rot[:, t, 1:2, :]))):
                    cos = cosine[:, 0, t:t + 1, :].to_broadcast([P, heads, HALF])
                    sin = sine[:, 0, t:t + 1, :].to_broadcast([P, heads, HALF])
                    at = (t * 5 + (0 if heads > 1 else 4)) * HALF
                    part_ = [rope_t[:, i, at:at + heads * HALF].rearrange("p (h c) -> p h c", h=heads) for i in range(4)]
                    x1, x2 = src[:, :, 0:HALF], src[:, :, HALF:]
                    tt(part_[0], x1, cos, ALU.mult)
                    tt(part_[1], x2, sin, ALU.mult)
                    tt(part_[2], x2, cos, ALU.mult)
                    tt(part_[3], x1, sin, ALU.mult)
                    dve.drain()
                    for dst in dsts:
                        tt(dst[:, :, 0:HALF], part_[0], part_[1], ALU.subtract)
                        tt(dst[:, :, HALF:], part_[2], part_[3], ALU.add)
            dve.drain().then_inc(q_rotated, 1)
            dve.wait_ge(score_done, l + 1)
            mask = one(causal[:]).to_broadcast([P, 2, P])
            for j in range(2):
                src = banks[:, 4 + 3 * j, 0:SEQ].rearrange("p (h c) -> p h c", h=2)
                tt(first_s[:, j::2, :], src, mask, ALU.add)
                src = banks[:, 5 + j, :].rearrange("p (h c) -> p h c", h=2)
                nc.vector.tensor_copy(second_s[:, j::2, 0:P], src[:, :, 0:P])
                tt(second_s[:, j::2, P:], src[:, :, P:], mask, ALU.add)
            dve.drain()
            nc.vector.tensor_reduce(s_max[:, 0:4], first_s, AX.X, ALU.max)
            nc.vector.tensor_reduce(s_max[:, 4:8], second_s, AX.X, ALU.max)
            dve.drain()
            ts(s_max, s_max, -MLA_SCALE, None, ALU.mult).then_inc(max_ready, 1)
            dve.wait_ge(exp_ready, l + 1)
            nc.vector.reciprocal(s_sum, s_sum)
            dve.drain()
            tt(first_s, first_s, wide(s_sum[:, 0:4], HEADS, P), ALU.mult)
            tt(second_s, second_s, wide(s_sum[:, 4:8], HEADS, SEQ), ALU.mult).then_inc(prob_ready, 1)
            for j in range(4):
                merge(j, 8, 2 * KD)
            dve.wait_ge(mix_done, l + 1)

        NORMS = DEPTH * LN_LAYER
        FFN2 = DEPTH * FFN_LAYER
        PAIRS, TAKEN = DEPTH * 22, DEPTH * 23

        @block.tensor
        def _(pe):
            for s in (gate_done, up_done, down_done):
                pe.drain().then_inc(s, 1)
            pe.drain().then_inc(panel_used, 2)
            pe.wait_ge(const_ready, 1)
            pe.wait_ge(setup_in, 16)
            turn_h(pe)
            pe.wait_ge(setup_row, 112)
            pe.wait_ge(pos_ready, 1)
            turn(banks[:, 0, 0:P], rows[:, 0, :])
            turn(banks[:, 0, P:P + 32], rows[0:32, 1, :])
            turn(banks[:, 0, 160:164], small[0:2 * TT, 192:192 + P]).then_inc(setup_turned, 1)
            pe.wait_ge(col_ready, 1)

            with pe.Fori(0, DEPTH) as l:
                n = l * FFN_LAYER
                ffn_pe(pe, n, l * 12 + 4)
                mod_pe(pe, l * 2)
                turn_h(pe, l * 6)
                mixer_pe(pe, l)
                turn_h(pe, l * 6 + 2)
                ffn_pe(pe, n + NS, l * 12 + 12)
                mod_pe(pe, l * 2 + 1)
                turn_h(pe, l * 6 + 4)

            def norm_pe(j):
                pe.wait_ge(norm_done, 2 * (NORMS + 1 + j))
                for q in range(4):
                    for half in range(2):
                        b = 2 * q + half
                        for t in range(TT):
                            last = turn(banks[:, 4 + q, half * SEQ + t * P:half * SEQ + (t + 1) * P], x_norm[:, t, b * P:(b + 1) * P])
                    last.then_inc(turned, 1)
                pe.wait_ge(diag_ready, j + 1)
                for i in range(2):
                    last = mm(banks[:, i, :], ones[:], diag[:, 4 * i:4 * i + 4, :].rearrange("p b c -> p (b c)"), start=True, stop=True)
                last.then_inc(grow_done, 1)
                pe.wait_ge(ht_ready, 4 * (NORMS + 2 + j))
                pe.wait_ge(grow_ready, j + 1)

            def panel_ready(use):
                pe.wait_ge(panel_in[use % 2], landed_second(use))
                return panel[use % 2]

            norm_pe(0)
            for use in range(6):
                tile = v3(panel_ready(use), 0, KD, PANEL)
                for j in range(2):
                    i = 2 * use + j
                    if i >= 4:
                        pe.wait_ge(pair_taken, TAKEN + i - 3)
                    for half in range(2):
                        c = (2 * j + half) * P
                        for k in range(KD):
                            last = mm(banks[:, 4 + i % 4, half * SEQ:(half + 1) * SEQ], tile[:, k, c:c + P], HT[:, k, :],
                                      start=k == 0, stop=k == KD - 1)
                    last.then_inc(pair_done, 1)
                pe.drain().then_inc(panel_used, 1)
            pe.wait_ge(conv_ready, 1)
            for i in range(2):
                tile = v3(panel_ready(6 + i), 0, 4, D)
                for k in range(4):
                    for t in range(TT):
                        for c in range(2):
                            mm(banks[:, 2 * t + c, :], conv_o[:, 4 * i + k, t * P:(t + 1) * P], tile[:, k, c * 512:(c + 1) * 512],
                               start=i == 0 and k == 0, stop=i == 1 and k == 3)
                pe.drain().then_inc(panel_used, 1)
            pe.drain().then_inc(mix_done, 1)

            norm_pe(1)
            ffn_pe(pe, FFN2, 4 * (NORMS + 3))

            norm_pe(2)
            for i in range(12):
                use, t = 8 + i // 2, i % 2
                cols = min(PANEL, 2 * AW - PANEL * (i // 2)) if i < 8 else AW // 2
                tile = v3(panel_ready(use), 0, KD, cols)
                if i >= 4:
                    pe.wait_ge(pair_taken, TAKEN + 8 + i - 3)
                for k in range(KD):
                    last = mm(banks[:, 4 + i % 4, 0:cols], HT[:, k, t * P:(t + 1) * P], tile[:, k, :], start=k == 0, stop=k == KD - 1)
                last.then_inc(pair_done, 1)
                if t == 1:
                    pe.drain().then_inc(panel_used, 1)
            pe.wait_ge(a_rotated, TT)
            pe.wait_ge(pair_taken, TAKEN + 8 + 12)
            for q in range(8):
                for half in range(2):
                    b = 2 * (q % 4) + half
                    n = min(P, AW - b * P)
                    c = (q // 4) * AW + b * P
                    for t in range(TT):
                        last = turn(banks[0:n, q, half * SEQ + t * P:half * SEQ + (t + 1) * P], a_rot[:, t, c:c + n])
                last.then_inc(a_turned, 1)
            pe.wait_ge(a_qk_ready, 8)
            for h in range(AH):
                if h >= 8:
                    pe.wait_ge(a_masked, h - 7)
                r, b = slice((h % 2) * AD, (h % 2 + 1) * AD), h // 2
                mm(banks[:, h % 8, 0:P], a_qT[r, b, 0:P], a_kT[r, b, 0:P], start=True, stop=True)
                mm(banks[:, h % 8, P:3 * P], a_qT[r, b, P:], a_kT[r, b, :], start=True, stop=True).then_inc(a_scored, 1)
            pe.wait_ge(a_masked, AH)
            for h in range(AH + 1):
                if h < AH:
                    pe.wait_ge(a_exp, h + 1)
                    if h >= 4:
                        pe.wait_ge(a_pT_ready, h - 3)
                    for i in range(3):
                        last = turn(banks[:, 4 + h % 4, i * P:(i + 1) * P], a_s[:, h, i * P:(i + 1) * P])
                    last.then_inc(a_pT_done, 1)
                if h:
                    g = h - 1
                    pe.wait_ge(a_pT_ready, g + 1)
                    c = (g % 8) * AD
                    v = a_v[:, :, g * AD:(g + 1) * AD]
                    mm(banks[:, g // 8, c:c + AD], a_pT[:, g, 0, :], v[:, 0, :], start=True, stop=True)
                    mm(banks[:, 2 + g // 8, c:c + AD], a_pT[:, g, 1, :], v[:, 0, :], start=True, stop=False)
                    last = mm(banks[:, 2 + g // 8, c:c + AD], a_pT[:, g, 2, :], v[:, 1, :], start=False, stop=True)
            last.then_inc(a_o_done, 1)
            pe.wait_ge(a_o_ready, 1)
            for q in range(4):
                for half in range(2):
                    b = 2 * q + half
                    n = min(P, AW - b * P)
                    for t in range(TT):
                        last = turn(banks[0:n, 4 + q, half * SEQ + t * P:half * SEQ + (t + 1) * P], a_o[:, t, b * P:b * P + n])
                last.then_inc(a_oT_done, 1)
            pe.wait_ge(a_oT_ready, 4)
            for i in range(2):
                tile = v3(panel_ready(14 + i), 0, 4, D)
                for k in range(4):
                    n = min(P, AW - (4 * i + k) * P)
                    for t in range(TT):
                        for c in range(2):
                            mm(banks[:, 2 * t + c, :], a_oT[0:n, 4 * i + k, t * P:(t + 1) * P], tile[0:n, k, c * 512:(c + 1) * 512],
                               start=i == 0 and k == 0, stop=i == 1 and k == 3)
                pe.drain().then_inc(panel_used, 1)
            pe.drain().then_inc(mix_done, 1)

            norm_pe(3)
            for t in range(TT):
                for k in range(KD):
                    last = mm(banks[:, 6, t * NE:(t + 1) * NE], HT[:, k, t * P:(t + 1) * P], router[:, k, :], start=k == 0, stop=k == KD - 1)
            last.then_inc(route_done, 1)
            pe.wait_ge(chosen_ready, 1)
            for t in range(TT):
                mm(banks[:, 7, t * NE:(t + 1) * NE], prefix[:], chosen[:, t, :], start=True, stop=t == 0)
                if t:
                    mm(banks[:, 7, t * NE:(t + 1) * NE], ones[:], chosen[:, 0, :], start=False, stop=True)
            for t in range(TT):
                mm(banks[:, 7, 16:16 + NE], ones[:], chosen[:, t, :], start=t == 0, stop=t == TT - 1)
            mm(banks[:, 6, 0:P], ones[:], prefix[:], start=True, stop=True).then_inc(counted, 1)
            pe.wait_ge(plan_ready, 1)
            items = pe.value_load(plan[0:1, ITEMS:ITEMS + 1], min_val=1, max_val=ITEMS - 1)
            gather_pe(pe, 0)
            with pe.Fori(0, items) as i:
                expert_pe(pe, FFN2 + NS + i * NS, i)

        @block.scalar
        def _(act):
            act.drain().then_inc(silu_done, 1)
            ht_act(act, 0)
            act.wait_ge(setup_turned, 1)
            act_fn(mod_bias[:], banks[:, 0, 0:P], ACT.Copy)
            act_fn(misc_col[:, 0:8], banks[:, 0, P:P + 8], ACT.Silu)
            act_fn(misc_col[:, 8:32], banks[:, 0, P + 8:P + 32], ACT.Copy)
            act_fn(small[:, 320:324], banks[:, 0, 160:164], ACT.Copy).then_inc(col_ready, 1)
            act.wait_ge(angle_ready, 1)
            act_fn(sine.rearrange("p s t c -> p (s t c)"), arena[:, 0:P], ACT.Sin)
            act_fn(cosine.rearrange("p s t c -> p (s t c)"), arena[:, P:2 * P], ACT.Sin).then_inc(rope_ready, 1)

            with act.Fori(0, DEPTH) as l:
                n = l * FFN_LAYER
                ffn_act(act, n)
                std_act(act, l * LN_LAYER + 1, 4 * LN_EPS)
                ht_act(act, l * 12 + 4)
                mixer_act(act, l)
                std_act(act, l * LN_LAYER + 2, LN_EPS)
                ht_act(act, l * 12 + 8)
                ffn_act(act, n + NS)
                std_act(act, l * LN_LAYER + 3, 4 * LN_EPS)
                ht_act(act, l * 12 + 12)

            def rms_act(j):
                act.wait_ge(var_ready, NORMS + 1 + j)
                for t in range(TT):
                    act_fn(x_norm[:, t, :], H[:, t, :], ACT.Square, accum_out=moments[:, t, 1:2])
                act.drain()
                act_fn(spread[:, :, 0], moments[:, :, 1], ACT.Sqrt, scale=1.0 / D, bias=RMS_EPS).then_inc(std_ready, 1)

            def norm_act(j):
                rms_act(j)
                for q in range(4):
                    act.wait_ge(turned, 4 * (NORMS + 1 + j) + q + 1)
                    for half in range(2):
                        b = 2 * q + half
                        last = act_fn(HT[:, b, :], banks[:, 4 + q, half * SEQ:(half + 1) * SEQ], ACT.Identity,
                                      scale=mod_scale[:, b:b + 1], bias=mod_col[:, 24 * j + b:24 * j + b + 1])
                    last.then_inc(ht_ready, 1)
                act.wait_ge(grow_done, j + 1)
                for i in range(2):
                    last = act_fn(gate_row[:, i * 512:(i + 1) * 512], banks[:, i, :], ACT.Copy)
                last.then_inc(grow_ready, 1)

            norm_act(0)
            for i in range(8):
                act.wait_ge(pair_done, PAIRS + i + 1)
                dst = b_conv if i < 4 else c_conv
                act_fn(dst[:, 2 * (i % 4):2 * (i % 4) + 2, :], banks[:, 4 + i % 4, :].rearrange("p (a b) -> p a b", a=2), ACT.Copy).then_inc(pair_taken, 1)
            norm_act(1)
            ffn_act(act, FFN2)
            norm_act(2)
            for i in range(12):
                act.wait_ge(pair_done, PAIRS + 12 + i + 1)
                use, t = i // 2, i % 2
                cols = min(PANEL, 2 * AW - PANEL * use) if i < 8 else AW // 2
                dst = a_qk[:, t, use * PANEL:use * PANEL + cols] if i < 8 else a_v[:, t, (use - 4) * cols:(use - 3) * cols]
                act_fn(dst, banks[:, 4 + i % 4, 0:cols], ACT.Copy).then_inc(pair_taken, 1)

            def blocks_act(dst, bank, q):
                if q < 3:
                    return act_fn(dst[:, 2 * q:2 * q + 2, :], banks[:, bank, :].rearrange("p (a b) -> p a b", a=2), ACT.Copy)
                act_fn(dst[:, 6, :], banks[:, bank, 0:SEQ], ACT.Copy)
                return act_fn(dst[0:AW % P, 7, :], banks[0:AW % P, bank, SEQ:], ACT.Copy)

            for q in range(8):
                act.wait_ge(a_turned, q + 1)
                blocks_act(a_qT if q < 4 else a_kT, q, q % 4).then_inc(a_qk_ready, 1)
            act.wait_ge(a_max, 1)
            act_fn(a_up, a_up, ACT.Exp)
            for h in range(AH):
                for t in range(TT):
                    i = t * AH + h
                    s = a_s[:, h, 0:P] if t == 0 else a_s[:, h, P:]
                    act_fn(s, s, ACT.Exp, scale=A_SCALE, bias=a_neg[:, i:i + 1], accum_out=a_sum[:, i:i + 1])
                act.drain().then_inc(a_exp, 1)
            for q in range(4):
                act.wait_ge(a_oT_done, q + 1)
                blocks_act(a_oT, 4 + q, q).then_inc(a_oT_ready, 1)
            norm_act(3)
            act.wait_ge(route_exp, 1)
            act_fn(r_exp, r_exp, ACT.Exp).then_inc(route_exp, 1)

            def gathered_act(i):
                act.wait_ge(gathered, i + 1)
                for b in range(KD):
                    last = act_fn(HT[:, b, 0:P], banks[:, 6 + b // 4, (b % 4) * P:(b % 4 + 1) * P], ACT.Identity,
                                  scale=mod_scale[:, b:b + 1], bias=mod_col[:, 72 + b:73 + b])
                last.then_inc(x_ready, 1)

            act.wait_ge(plan_ready, 1)
            items = act.value_load(plan[0:1, ITEMS:ITEMS + 1], min_val=1, max_val=ITEMS - 1)
            gathered_act(0)
            with act.Fori(0, items) as i:
                def weigh_act():
                    act.wait_ge(weigh_turned, i + 1)
                    act_fn(weighT.rearrange("p t c -> p (t c)"), banks[:, 2, 0:SEQ], ACT.Copy).then_inc(weigh_taken, 1)
                n = FFN2 + NS + i * NS
                ffn_act(act, n, P, weigh_act)
                gathered_act(i + 1)
                act.wait_ge(down_done, n + NS + 1)
                for c in range(2):
                    last = act_fn(slot_out[:, c * 512:(c + 1) * 512], banks[:, c, :], ACT.Copy)
                last.then_inc(slots_taken, 1)
            rms_act(4)

        @block.vector
        def _(dve):
            for s in (act_ready, mod_used):
                dve.drain().then_inc(s, 1)
            dve.wait_ge(setup_row, 112)
            nc.vector.tensor_copy(small[0:2 * TT, 192:192 + P], small[0:2 * TT, 0:P].bitcast(I32)).then_inc(pos_ready, 1)
            dve.wait_ge(const_ready, 1)
            dve.wait_ge(col_ready, 1)
            angle, other, turns = arena[:, 0:P], arena[:, P:2 * P], arena[:, 2 * P:3 * P]
            for i in range(2 * TT):
                ts(angle[:, i * HALF:(i + 1) * HALF], inv_freq, small[:, 320 + i:321 + i], None, ALU.mult)
            dve.drain()
            ts(turns, angle, float(1 / TWO_PI), None, ALU.mult)
            dve.drain()
            ts(turns, turns, ROUND, None, ALU.add)
            dve.drain()
            ts(turns, turns, ROUND, None, ALU.subtract)
            for part_ in (PI_A, PI_B, PI_C):
                dve.drain()
                stt(angle, turns, -part_, angle, ALU.mult, ALU.add)
            dve.drain()
            ts(other, angle, float(np.pi / 2), None, ALU.add)
            dve.drain()
            ts(turns, other, float(np.pi), -TWO_PI, ALU.is_gt, ALU.mult)
            dve.drain()
            tt(other, other, turns, ALU.add)
            dve.drain()
            ts(arena[:, 0:2 * P], arena[:, 0:2 * P], PI_SAFE, -PI_SAFE, ALU.min, ALU.max)
            for g in (1, 2):
                r = DILATIONS[g]
                hot = arena[:, 3 * P + 16 * g:3 * P + 16 * g + r]
                nc.vector.tensor_reduce(hot, ident[:].rearrange("p (m r) -> p r m", r=r), AX.X, ALU.add)
                dve.drain()
                ts(hot, hot, 1.0, -MASKED, ALU.subtract, ALU.mult)
                dve.drain()
                nc.vector.tensor_copy(band[:, g, :, :].rearrange("p i (m r) -> p (i m) r", r=r),
                                      hot.rearrange("p (o r) -> p o r", o=1).to_broadcast([P, 3 * P // r, r]))
            dve.drain().then_inc(angle_ready, 1)
            dve.wait_ge(rope_ready, 1)

            with dve.Fori(0, DEPTH) as l:
                n = l * FFN_LAYER
                ffn_vec(dve, n, l * 2)
                dve.wait_ge(down_done, n + NS + 1)
                layer_norm(dve, l * LN_LAYER + 1, 2 * ALPHA, l * 2)
                mixer_vec(dve, l)
                layer_norm(dve, l * LN_LAYER + 2, ALPHA)
                ffn_vec(dve, n + NS, l * 2 + 1)
                dve.wait_ge(down_done, n + 2 * NS + 1)
                layer_norm(dve, l * LN_LAYER + 3, 2 * ALPHA, l * 2 + 1)

            def norm_vec(j):
                m = NORMS + 1 + j
                dve.drain()
                stt(mod_scale, mod_col[:, 24 * j + 8:24 * j + 16], 1.0, mod_bias[:, 96 + 8 * j:104 + 8 * j], ALU.add, ALU.mult)
                dve.drain().then_inc(var_ready, 1)
                for b in range(KD):
                    last = ts(diag[:, b, :], ident[:], mod_col[:, 24 * j + 16 + b:24 * j + 17 + b], None, ALU.mult)
                last.then_inc(diag_ready, 1)
                dve.wait_ge(std_ready, m)
                nc.vector.reciprocal(spread[:, :, 1], spread[:, :, 0])
                dve.drain()
                for t in range(TT):
                    ts(x_norm[:, t, :], H[:, t, :], spread[:, t, 1:2], None, ALU.mult).then_inc(norm_done, 1)

            def residual(j, src):
                dve.wait_ge(grow_ready, j + 1)
                for t in range(TT):
                    tt(x_norm[:, t, :], src[:, t, :], gate_row[:], ALU.mult)
                dve.drain()
                for t in range(TT):
                    tt(H[:, t, :], H[:, t, :], x_norm[:, t, :], ALU.add)

            norm_vec(0)
            nc.vector.memset(v_pad[:, :, 0:4], 0.0)
            dve.wait_ge(pair_taken, TAKEN + 8)
            for i in range(4):
                dve.wait_ge(pair_done, PAIRS + 8 + i + 1)
                tt(v_pad[:, 2 * i:2 * i + 2, 4:260], banks[:, 4 + i, :].rearrange("p (a b) -> p a b", a=2), c_conv[:, 2 * i:2 * i + 2, :], ALU.mult)
            for j in range(3):
                dve.drain()
                for b in range(KD):
                    w = misc_col[:, 8 + 8 * j + b:9 + 8 * j + b]
                    if j == 0:
                        ts(conv_o[:, b, :], v_pad[:, b, 2:2 + SEQ], w, None, ALU.mult)
                    else:
                        stt(conv_o[:, b, :], v_pad[:, b, 2 + j:2 + j + SEQ], w, conv_o[:, b, :], ALU.mult, ALU.add)
            dve.drain()
            tt(conv_o, conv_o, b_conv, ALU.mult).then_inc(conv_ready, 1)
            dve.wait_ge(mix_done, DEPTH + 1)
            residual(0, acc)

            norm_vec(1)
            ffn_vec(dve, FFN2)
            dve.wait_ge(down_done, FFN2 + NS + 1)
            residual(1, acc)

            norm_vec(2)
            dve.wait_ge(pair_taken, TAKEN + 8 + 8)
            for t in range(TT):
                src = a_qk[:, t, :].rearrange("p (h c) -> p h c", c=AD)
                dst = a_rot[:, t, :].rearrange("p (h c) -> p h c", c=AD)
                cos = cosine[:, 1, t:t + 1, :].to_broadcast([P, 2 * AH, HALF])
                sin = sine[:, 1, t:t + 1, :].to_broadcast([P, 2 * AH, HALF])
                p0, p1, p2, p3 = [x.rearrange("p (h c) -> p h c", c=HALF) for x in (a_t[:, 0, :], a_t[:, 1, :], a_t2[:, 0, :], a_t2[:, 1, :])]
                x1, x2 = src[:, :, 0:HALF], src[:, :, HALF:]
                dve.drain()
                tt(p0, x1, cos, ALU.mult)
                tt(p1, x2, sin, ALU.mult)
                tt(p2, x2, cos, ALU.mult)
                tt(p3, x1, sin, ALU.mult)
                dve.drain()
                tt(dst[:, :, 0:HALF], p0, p1, ALU.subtract)
                tt(dst[:, :, HALF:], p2, p3, ALU.add).then_inc(a_rotated, 1)
            dve.wait_ge(setup_done, 1)
            for h in range(AH):
                dve.wait_ge(a_scored, h + 1)
                tt(a_s[:, h, :], banks[:, h % 8, 0:3 * P], band[:, h // AJ, :, :].rearrange("p i c -> p (i c)"), ALU.add).then_inc(a_masked, 1)
            dve.drain()
            nc.vector.tensor_reduce(a_neg[:, 0:AH], a_s[:, :, 0:P], AX.X, ALU.max)
            nc.vector.tensor_reduce(a_neg[:, AH:], a_s[:, :, P:], AX.X, ALU.max)
            dve.drain()
            ts(a_neg, a_neg, -A_SCALE, None, ALU.mult)
            dve.drain()
            for t in range(TT):
                own = a_neg[:, t * AH:(t + 1) * AH]
                low = a_low[:, t * AJ:(t + 1) * AJ]
                nc.vector.tensor_reduce(low, own.rearrange("p (g j) -> p j g", g=AG), AX.X, ALU.min)
                dve.drain()
                tt(a_up[:, t * AH:(t + 1) * AH].rearrange("p (g j) -> p g j", g=AG), low.rearrange("p (o j) -> p o j", o=1).to_broadcast([P, AG, AJ]),
                   own.rearrange("p (g j) -> p g j", g=AG), ALU.subtract)
            dve.drain().then_inc(a_max, 1)
            for h in range(AH):
                dve.wait_ge(a_pT_done, h + 1)
                nc.vector.tensor_copy(a_pT[:, h, :, :].rearrange("p i c -> p (i c)"), banks[:, 4 + h % 4, 0:3 * P]).then_inc(a_pT_ready, 1)
            tt(a_coef, a_up, a_sum, ALU.mult)
            dve.drain()
            for t in range(TT):
                nc.vector.tensor_reduce(a_low[:, t * AJ:(t + 1) * AJ], a_coef[:, t * AH:(t + 1) * AH].rearrange("p (g j) -> p j g", g=AG), AX.X, ALU.add)
            dve.drain()
            nc.vector.reciprocal(a_low, a_low)
            dve.drain()
            for t in range(TT):
                tt(a_coef[:, t * AH:(t + 1) * AH].rearrange("p (g j) -> p g j", g=AG), a_up[:, t * AH:(t + 1) * AH].rearrange("p (g j) -> p g j", g=AG),
                   a_low[:, t * AJ:(t + 1) * AJ].rearrange("p (o j) -> p o j", o=1).to_broadcast([P, AG, AJ]), ALU.mult)
            dve.drain()
            dve.wait_ge(a_o_done, 1)
            for t in range(TT):
                for i, heads in enumerate((8, AH - 8)):
                    c = slice(8 * i * AD, (8 * i + heads) * AD)
                    last = tt(a_o[:, t, c].rearrange("p (h c) -> p h c", c=AD), banks[:, 2 * t + i, 0:heads * AD].rearrange("p (h c) -> p h c", c=AD),
                              wide(a_coef[:, t * AH + 8 * i:t * AH + 8 * i + heads], heads, AD), ALU.mult)
            last.then_inc(a_o_ready, 1)
            dve.wait_ge(mix_done, DEPTH + 2)
            residual(2, acc)

            norm_vec(3)
            for e in range(NE):
                nc.vector.memset(r_rank[:, e:e + 1], float(NE - e))
            nc.vector.memset(experts_sum, 0.0)
            dve.wait_ge(route_done, 1)
            nc.vector.tensor_copy(r_log.rearrange("p t e -> p (t e)"), banks[:, 6, 0:TT * NE])
            dve.drain()
            rank = r_rank.rearrange("p (o e) -> p o e", o=1).to_broadcast([P, TT, NE])

            def first_largest(src, top, hot):
                nc.vector.tensor_reduce(top, src, AX.X, ALU.max)
                dve.drain()
                tt(r_eq, src, wide(top, TT, NE), ALU.is_equal)
                dve.drain()
                tt(r_eq, r_eq, rank, ALU.mult)
                dve.drain()
                nc.vector.tensor_reduce(r_top, r_eq, AX.X, ALU.max)
                dve.drain()
                tt(hot, r_eq, wide(r_top, TT, NE), ALU.is_equal)
                dve.drain()

            first_largest(r_log, r_first, r_hot1)
            stt(r_rest, r_hot1, -3e38, r_log, ALU.mult, ALU.add)
            dve.drain()
            first_largest(r_rest, r_second, r_hot2)
            tt(r_exp, r_second, r_first, ALU.subtract).then_inc(route_exp, 1)
            nc.vector.memset(prefix[0:CHUNK, CHUNK:], 1.0)
            tt(chosen, r_hot1, r_hot2, ALU.add)
            dve.drain().then_inc(chosen_ready, 1)
            dve.wait_ge(route_exp, 2)
            ts(r_w1, r_exp, 1.0, None, ALU.add)
            dve.drain()
            nc.vector.reciprocal(r_w1, r_w1)
            dve.drain()
            tt(r_exp, r_exp, r_w1, ALU.mult)
            tt(r_hot1, r_hot1, wide(r_w1, TT, NE), ALU.mult)
            dve.drain()
            tt(r_hot2, r_hot2, wide(r_exp, TT, NE), ALU.mult)
            dve.drain()
            tt(v3(small, 256, TT, NE), r_hot1, r_hot2, ALU.add)
            dve.drain()
            dve.wait_ge(counted, 1)
            nc.vector.tensor_copy(count_up, banks[:, 6, 0:P])
            nc.vector.tensor_copy(counts, banks[:, 7, 16:16 + NE])
            tt(token_rank.rearrange("p t e -> p (t e)"), banks[:, 7, 0:TT * NE], chosen.rearrange("p t e -> p (t e)"), ALU.mult)
            dve.drain()
            ts(passes, counts, 0.0, None, ALU.is_gt)
            ts(more, counts, float(P), None, ALU.is_gt)
            dve.drain()
            tt(passes, passes, more, ALU.add)
            dve.drain()
            nc.vector.tensor_copy(end_item, passes)
            for e in range(1, NE):
                dve.drain()
                tt(end_item[:, e:e + 1], end_item[:, e:e + 1], end_item[:, e - 1:e], ALU.add)
            dve.drain()
            tt(first_item, end_item, passes, ALU.subtract)

            def by_item(ap):
                return ap.rearrange("p (i o) -> p i o", o=1).to_broadcast([P, ITEMS, NE])

            def by_expert(ap):
                return ap.rearrange("p (o e) -> p o e", o=1).to_broadcast([P, ITEMS, NE])

            def pick_expert(out_, src):
                tt(item_tmp, item_hot, by_expert(src), ALU.mult)
                dve.drain()
                nc.vector.tensor_reduce(out_, item_tmp, AX.X, ALU.add)
                dve.drain()

            tt(item_tmp, by_item(count_up[:, 0:ITEMS]), by_expert(end_item), ALU.is_gt)
            dve.drain()
            nc.vector.tensor_reduce(item_expert, item_tmp, AX.X, ALU.add)
            dve.drain()
            nc.vector.tensor_copy(plan[:, 0:ITEMS], item_expert)
            nc.vector.tensor_copy(plan[:, ITEMS:], end_item[:, NE - 1:])
            dve.drain().then_inc(plan_ready, 1)
            ts(item_expert, item_expert, 1.0, None, ALU.add)
            dve.drain()
            tt(item_hot, by_item(item_expert), by_expert(count_up[:, 0:NE]), ALU.is_equal)
            dve.drain()
            pick_expert(item_pass, first_item)
            tt(item_pass, count_up[:, 0:ITEMS], item_pass, ALU.subtract)
            dve.drain()
            ts(item_pass, item_pass, -1.0, -float(P), ALU.add, ALU.mult)
            for t in range(TT):
                pick_expert(item_slot[:, t, :], token_rank[:, t, :])
                tt(item_slot[:, t, :], item_slot[:, t, :], item_pass, ALU.add)
                pick_expert(item_gate[:, t, :], route[:, t * NE:(t + 1) * NE])

            def pick_vec(i):
                for t in range(TT):
                    last = ts(pick[:, t, :], count_up, mod_sum[:, bass.ds(256 + t * ITEMS + i, 1)], None, ALU.is_equal)
                last.then_inc(pick_ready, 1)

            dve.drain().then_inc(sum_done, 2)
            items = dve.value_load(plan[0:1, ITEMS:ITEMS + 1], min_val=1, max_val=ITEMS - 1)
            pick_vec(0)
            with dve.Fori(0, items) as i:
                n = FFN2 + NS + i * NS
                gate_col = [mod_sum[:, bass.ds(288 + t * ITEMS + i, 1)] for t in range(TT)]
                dve.wait_ge(x_ready, i + 1)
                for t in range(TT):
                    last = ts(weigh[:, t, :], count_up, mod_sum[:, bass.ds(256 + t * ITEMS + i, 1)], gate_col[t], ALU.is_equal, ALU.mult)
                last.then_inc(weigh_ready, 1)
                pick_vec(i + 1)
                ffn_vec(dve, n, width=P)
                for t in range(TT):
                    dve.wait_ge(scattered, i * 2 + t + 1)
                    b = (2, 6)[t]
                    tt(experts_sum[:, t, :], experts_sum[:, t, :], banks[:, b:b + 2, :].rearrange("p b c -> p (b c)"), ALU.add).then_inc(sum_done, 1)
                dve.drain()
            residual(3, experts_sum)

            dve.drain().then_inc(var_ready, 1)
            dve.wait_ge(std_ready, NORMS + 5)
            nc.vector.reciprocal(spread[:, :, 1], spread[:, :, 0])
            dve.wait_ge(norm_in, NORMS * 32 + 16)
            dve.drain()
            for t in range(TT):
                stt(H[:, t, :], H[:, t, :], spread[:, t, 1:2], row_b[:], ALU.mult, ALU.mult).then_inc(out_ready, 1)


_INS = ['x', 'positions', 'ln1_g', 'ln1_b', 'ffn1_w_gate', 'ffn1_w_up', 'ffn1_w_down', 'w_in', 'b_gate', 'dn_conv_w',
        'dn_a_log', 'dn_dt_bias', 'dn_norm_w', 'dn_w_o', 'cv_glu_b', 'cv_dw_w', 'cv_dw_b', 'cv_ln_g', 'cv_ln_b',
        'cv_w_pw2', 'cv_b_pw2', 'mla_q_norm_w', 'mla_w_uq', 'mla_kv_norm_w', 'mla_w_ukv', 'mla_w_o', 'w_out', 'ln2_g',
        'ln2_b', 'ffn2_w_gate', 'ffn2_w_up', 'ffn2_w_down', 'ln3_g', 'ln3_b', 'c_2', 'positions_2', 'mod_w_2',
        'mod_b_2', 'norm_g_2', 'conv_w_in_2', 'conv_w_2', 'conv_w_out_2', 'ffn_w_gate_2', 'ffn_w_up_2', 'ffn_w_down_2',
        'attn_w_qkv_2', 'attn_w_o_2', 'router_w_2', 'moe_w_gate_2', 'moe_w_up_2', 'moe_w_down_2', 'final_g_2']


def kernel(**inputs):
    import numpy as _np
    import concourse.bacc as _bacc
    from concourse import mybir as _mybir
    from concourse.bass_utils import run_bass_kernel_spmd as _run

    nc = _bacc.Bacc("TRN2", target_bir_lowering=False, num_devices=1)
    arrays, args = {}, {}
    for name in _INS:
        v = _np.ascontiguousarray(inputs[name])
        arrays[f"in_{name}_dram"] = v
        args[name] = nc.dram_tensor(f"in_{name}_dram", v.shape, _mybir.dt.from_np(v.dtype), kind="ExternalInput").ap()
    out = nc.dram_tensor("out_0_dram", (1, SEQ, D), F32, kind="ExternalOutput").ap()
    build(nc, args, out)
    r = _run(nc, [arrays], core_ids=[0])
    return r.results[0]["out_0_dram"]
```

```python
from contextlib import ExitStack

import numpy as np

import concourse.bass as bass
from concourse import mybir

F32 = mybir.dt.float32
F32R = mybir.dt.float32r
I32 = mybir.dt.int32
ALU = mybir.AluOpType
ACT = mybir.ActivationFunctionType
AX = mybir.AxisListType

P = 128
SEQ, D, DEPTH = 256, 1024, 2
TT = SEQ // P
KD = D // P
FF, FSTEP = 2816, 256
NS = FF // FSTEP
FB = FSTEP // P
HEADS, HD, CHUNK = 4, 128, 64
CV, TAPS = 512, 31
CB = CV // P
QL, KVL, NOPE, ROPE, VD = 384, 256, 128, 64, 128
HALF = ROPE // 2
QB, KVB = QL // P, KVL // P
ALPHA = (2 * DEPTH) ** 0.25
LN_EPS, RMS_EPS, L2_EPS = 1e-5, 1e-6, 1e-6
MLA_SCALE = (NOPE + ROPE) ** -0.5
DN_SCALE = HD ** -0.5
MASKED = -1e30
C_Z, C_GLU, C_CQ, C_KR, C_GATE = 1536, 2056, 3080, 3720, 3784
PANEL = 512
GATE_PANELS = 3 * D // PANEL
AH, AD, AG, AJ = 15, 64, 3, 5
AW = AH * AD
A_SCALE = AD ** -0.5
DILATIONS = (1, 4, 16)
NE = 8
ITEMS = 16
MOD_UNITS = 12
MOD_COLS = 3 * D // MOD_UNITS
FFN_LAYER = 2 * NS
MIX_USES = 20
LN_LAYER = 3

ROW_GATE, ROW_CONV, ROW_GLU, ROW_DWB, ROW_LNG, ROW_LNB, ROW_PW, ROW_QN, ROW_KVN, ROWS = (
    0, 24, 72, 80, 84, 88, 92, 100, 103, 105)
TWO_PI = 2 * np.pi
ROUND = 1.5 * 2.0 ** 23
PI_A = 6.28125
PI_B = float((np.array(TWO_PI - PI_A, np.float32).view(np.int32) & np.int32(-4096)).view(np.float32))
PI_C = float(np.float32(TWO_PI - PI_A - PI_B))
PI_SAFE = 3.1415925

MIXER_PANELS = (
    [("qkv", [("w_in", 0, D, PANEL * i, PANEL)]) for i in range(3)]
    + [("glu", [("w_in", 0, D, C_GLU + PANEL * i, PANEL)]) for i in range(2)]
    + [("z", [("w_in", 0, D, C_Z, 520)]),
       ("lora", [("w_in", 0, D, C_CQ, PANEL)]),
       ("lora", [("w_in", 0, D, C_CQ + PANEL, C_GATE - C_CQ - PANEL)])]
    + [("gate", [("w_in", 0, D, C_GATE + PANEL * i, PANEL)]) for i in range(GATE_PANELS)]
    + [("cv_out", [("cv_w_pw2", 0, CV, 0, D)]),
       ("dn_out", [("dn_w_o", 0, HEADS * HD, 0, D)]),
       ("mla_up", [("mla_w_uq", 0, QL, 0, HEADS * (NOPE + ROPE)), ("mla_w_ukv", 0, KVL, 0, HEADS * (NOPE + VD))]),
       ("mla_out", [("mla_w_o", 0, HEADS * VD, 0, D)]),
       ("out", [("w_out", 0, D // 2, 0, D)]),
       ("out", [("w_out", D // 2, D // 2, 0, D)])])
SECOND_PANELS = (
    [("conv_in", [("conv_w_in_2", 0, D, PANEL * i, PANEL)]) for i in range(6)]
    + [("conv_out", [("conv_w_out_2", 0, D // 2, 0, D)]), ("conv_out", [("conv_w_out_2", D // 2, D // 2, 0, D)])]
    + [("qk", [("attn_w_qkv_2", 0, D, PANEL * i, min(PANEL, 2 * AW - PANEL * i))]) for i in range(4)]
    + [("v", [("attn_w_qkv_2", 0, D, 2 * AW + 480 * i, 480)]) for i in range(2)]
    + [("attn_out", [("attn_w_o_2", 0, PANEL, 0, D)]),
       ("attn_out", [("attn_w_o_2", PANEL, 384, 0, D), ("attn_w_o_2", 896, 64, 0, D)])])
assert len(MIXER_PANELS) == MIX_USES
PANEL_WORDS = max(sum(-(-rows // P) * cols for _, rows, cols in [(m, r, c) for m, _, r, _, c in pieces])
                  for _, pieces in MIXER_PANELS + SECOND_PANELS)


def landed(use):
    return 16 * sum(len(MIXER_PANELS[u][1]) for u in range(use % 2, use + 1, 2))


LANDED_LAYER = [landed(MIX_USES - 2), landed(MIX_USES - 1)]


def landed_second(use):
    return DEPTH * LANDED_LAYER[use % 2] + 16 * sum(len(SECOND_PANELS[u][1]) for u in range(use % 2, use + 1, 2))


def build(nc, a, out):
    with ExitStack() as ctx:
        def sb(name, shape, dt=F32):
            return ctx.enter_context(nc.sbuf_tensor(name, shape, dt))

        def sem(name):
            return ctx.enter_context(nc.semaphore(name))

        def v3(tile, at, *dims):
            n = int(np.prod(dims))
            piece = tile[:, at:at + n]
            if len(dims) == 1:
                return piece
            names = "abcd"[:len(dims)]
            return piece.rearrange(f"p ({' '.join(names)}) -> p {' '.join(names)}", **dict(zip(names, dims)))

        gate_w = sb("gate_w", [P, KD, FSTEP])
        up_w = sb("up_w", [P, KD, FSTEP])
        down_w = sb("down_w", [P, FB, D])
        panel = [sb(f"panel{i}", [P, PANEL_WORDS]) for i in range(2)]
        mod_unit = sb("mod_unit", [P, KD * MOD_COLS])
        mod_sum = sb("mod_sum", [P, 3 * D])
        H = sb("H", [P, TT, D])
        HT = sb("HT", [P, KD, SEQ])
        ffn_tmp = sb("ffn_tmp", [P, 2 * FB * SEQ])
        row_g = sb("row_g", [P, D])
        row_b = sb("row_b", [P, D])
        rows = sb("rows", [P, 2, P])
        pcol = sb("pcol", [P, ROWS])
        dwcol = sb("dwcol", [P, TAPS * CB])
        ident = sb("ident", [P, P])
        ones = sb("ones", [P, P])
        causal = sb("causal", [P, P])
        prefix = sb("prefix", [P, P])
        strict = sb("strict", [P, P])
        same = sb("same", [P, P])
        in_chunk = sb("in_chunk", [P, 2, P])
        level = sb("level", [P, 6, P])
        band = sb("band", [P, AG, 3, P])
        cosine = sb("cosine", [P, 2, TT, HALF])
        sine = sb("sine", [P, 2, TT, HALF])
        mod_col = sb("mod_col", [P, 2 * DEPTH * 24])
        mod_bias = sb("mod_bias", [P, P])
        misc_col = sb("misc_col", [P, 32])
        norm_row = sb("norm_row", [P, HD])
        head_rows = sb("head_rows", [P, 2 * HEADS])
        router = sb("router", [P, KD, NE])
        stats = sb("stats", [P, TT, 2, 6])
        moments = sb("moments", [P, TT, 2])
        spread = sb("spread", [P, TT, 2])
        small = sb("small", [P, 328])
        arena_at = nc.sbuf_base
        arena = sb("arena", [P, 21552])
        ffn_arena = nc.alloc_sbuf_tensor_at("ffn_arena", [P, 21552], F32R, offset=arena_at)
        banks = ctx.enter_context(nc.psum_tensor("banks", [P, 8, 512], F32))
        acc = banks[:, 0:4, :].rearrange("p (t n) c -> p t (n c)", t=TT)

        act_t = v3(ffn_tmp, FB * SEQ, FB, SEQ)
        mod_w = v3(mod_unit, 0, KD, MOD_COLS)
        def parts(at, step, *dims):
            return [v3(ffn_arena, at + j * step, *dims) for j in range(2)]

        gate_parts, up_parts, down_parts = parts(6144, 2048, KD, FSTEP), parts(10240, 2048, KD, FSTEP), parts(14336, 2048, FB, D)
        x_parts, unit_parts = parts(2048, 2048, KD, SEQ), parts(0, 512, FB, SEQ)
        last_down_parts, last_unit_parts = parts(6144, 2048, FB, D), parts(10240, 512, FB, SEQ)
        slot_x_parts, slot_unit_parts = parts(18432, 1024, KD, P), parts(20480, 256, FB, P)
        gates = v3(arena, 0, 3 * KD, SEQ)
        raw = v3(arena, 6144, 12, 260)
        q_tok = v3(arena, 6144, TT, HEADS, HD)
        k_tok = v3(arena, 7168, TT, HEADS, HD)
        inv = v3(arena, 6144, TT, HEADS, P)
        inv_t = v3(arena, 7168, TT, HEADS, P)
        v_beta = v3(arena, 8192, TT, HEADS, HD)
        v_new = v_beta
        conv = v3(arena, 9264, 12, SEQ)
        lower = v3(arena, 9264, TT, HEADS, P)
        qk = v3(arena, 10288, TT, HEADS, P)
        g_wide = v3(arena, 11312, TT, HEADS, P)
        e_row = v3(arena, 11312, TT, HEADS, P)
        square = v3(arena, 9264, TT, HEADS * HD)
        qT = v3(arena, 12336, HEADS, SEQ)
        kT = v3(arena, 13360, HEADS, SEQ)
        part = v3(arena, 12336, TT, HEADS, P)
        turn_b = v3(arena, 13360, TT, HEADS, P)
        k_beta = v3(arena, 14384, TT, HEADS, HD)
        o_tok = k_beta
        k_dec = v3(arena, 15408, TT, HEADS, HD)
        oT = v3(arena, 15408, HEADS, SEQ)
        qk_sq = v3(arena, 16432, 4, HEADS, HD)
        u_tok = v3(arena, 16432, TT, HEADS, HD)
        wT = v3(arena, 17456, TT, HEADS, P)
        states = [v3(arena, 18480, HEADS, HD), v3(arena, 13360, HEADS, HD)]
        glu_pad = v3(arena, 18992, CB, 288)
        z_tok = v3(mod_sum, 2048, TT, HEADS * HD)
        lora = v3(arena, 20144, TT, 704)
        glu_a = v3(mod_unit, 0, CB, SEQ)
        glu_s = v3(mod_unit, 1024, CB, SEQ)
        cv_tok = v3(mod_unit, 0, TT, CV)
        cvT = v3(mod_unit, 1024, CB, SEQ)
        cv_acc = v3(ffn_tmp, 0, CB, SEQ)
        merged = v3(mod_sum, 0, KD, SEQ)
        branch = v3(ffn_tmp, 0, 2, SEQ)
        cqT = v3(arena, 6144, QB, SEQ)
        ckvT = v3(arena, 6912, KVB, SEQ)
        qnT = v3(arena, 7424, HEADS, SEQ)
        knT = v3(arena, 8448, HEADS, SEQ)
        q_rot = v3(arena, 9472, TT, HEADS, ROPE)
        qrT = v3(arena, 9984, 2, SEQ)
        k_rot = v3(arena, 10496, TT, 2, ROPE)
        krT = v3(arena, 10752, SEQ)
        v_tok = v3(arena, 11008, TT, HEADS * VD)
        first_s = v3(arena, 12032, HEADS, P)
        second_s = v3(arena, 12544, HEADS, SEQ)
        probT = v3(arena, 13568, HEADS, 3, P)
        moT = v3(arena, 15104, HEADS, SEQ)
        rope_t = v3(arena, 16128, 4, TT * (HEADS + 1) * HALF)
        x_norm = v3(arena, 0, TT, D)
        b_conv = v3(arena, 2048, KD, SEQ)
        c_conv = v3(arena, 4096, KD, SEQ)
        v_pad = v3(arena, 6144, KD, 260)
        conv_o = v3(arena, 8224, KD, SEQ)
        a_v = v3(arena, 0, TT, AW)
        a_qk = v3(arena, 2048, TT, 2 * AW)
        a_rot = v3(arena, 5888, TT, 2 * AW)
        a_pT = v3(arena, 2048, AH, 3, P)
        a_qT = v3(arena, 9728, KD, SEQ)
        a_kT = v3(arena, 11776, KD, SEQ)
        a_s = v3(arena, 13824, AH, 3 * P)
        a_o = v3(arena, 19584, TT, AW)
        a_oT = v3(arena, 9728, KD, SEQ)
        a_t = v3(mod_sum, 0, 2, AW)
        a_t2 = v3(mod_unit, 0, 2, AW)
        diag = v3(mod_unit, 0, KD, P)
        experts_sum = v3(arena, 2048, TT, D)
        pick = v3(arena, 4096, TT, P)
        weigh = v3(arena, 4352, TT, P)
        weighT = v3(arena, 4608, TT, P)
        slot_out = v3(arena, 4864, D)
        item_hot, item_tmp = v3(mod_sum, 0, ITEMS, NE), v3(mod_sum, 128, ITEMS, NE)
        item_slot, item_gate = v3(mod_sum, 256, TT, ITEMS), v3(mod_sum, 288, TT, ITEMS)
        item_expert, item_pass = mod_sum[:, 320:336], mod_sum[:, 360:376]
        passes, first_item, end_item = mod_sum[:, 336:344], mod_sum[:, 344:352], mod_sum[:, 352:360]
        count_up = mod_sum[:, 384:512]
        token_rank = v3(mod_sum, 512, TT, NE)
        counts, more = mod_sum[:, 528:536], mod_sum[:, 536:544]
        plan = mod_sum[:, 544:544 + ITEMS + 1].bitcast(I32)
        gate_row = row_g

        log_g, beta = small[:, 0:8], small[:, 8:16]
        cum, total, chunk_total = small[:, 16:24], small[:, 24:32], small[:, 32:48]
        logits = v3(small, 48, TT, 8)
        soft_x, soft_n = small[:, 64:72], small[:, 72:80]
        tok_sum, tok_scale = small[:, 80:96], small[:, 96:112]
        k_scale, dec_scale, chunk_e = small[:, 112:120], small[:, 120:128], small[:, 128:144]
        o_sum, o_scale = small[:, 144:152], small[:, 152:160]
        inv_freq = small[:, 160:192]
        lora_stats, lora_mom, lora_ms, lora_scale = v3(small, 192, TT, 2, 6), v3(small, 216, TT, 2, 2), small[:, 224:228], small[:, 228:232]
        s_max, s_sum = small[:, 240:248], small[:, 248:256]
        cum_e = small[:, 264:272]
        cv_stats, cv_mom, cv_scale = v3(small, 272, TT, 6), v3(small, 284, TT, 2), small[:, 288:290]
        neg_a = small[:, 292:296]

        mod_scale = small[:, 300:308]
        a_neg, a_sum, a_up, a_coef, a_low = small[:, 0:30], small[:, 32:62], small[:, 64:94], small[:, 96:126], small[:, 126:136]
        r_log, r_first, r_eq, r_second = v3(small, 136, TT, NE), small[:, 152:154], v3(small, 156, TT, NE), small[:, 172:174]
        r_top, r_hot1, r_hot2 = small[:, 174:176], v3(small, 176, TT, NE), v3(small, 192, TT, NE)
        r_exp, r_w1, r_rest, r_rank = small[:, 208:210], small[:, 210:212], v3(small, 212, TT, NE), small[:, 232:240]
        route = small[:, 256:272]
        chosen = v3(small, 272, TT, NE)

        setup_in, setup_row = sem("setup_in"), sem("setup_row")
        const_ready, setup_done, setup_turned = sem("const_ready"), sem("setup_done"), sem("setup_turned")
        pos_ready, col_ready, angle_ready, rope_ready = sem("pos_ready"), sem("col_ready"), sem("angle_ready"), sem("rope_ready")
        gate_in, up_in, down_in, mod_in = sem("gate_in"), sem("up_in"), sem("down_in"), sem("mod_in")
        gate_done, up_done, down_done = sem("gate_done"), sem("up_done"), sem("down_done")
        gate_high, up_high, down_high = sem("gate_high"), sem("up_high"), sem("down_high")
        gate_low, up_low, down_low = sem("gate_low"), sem("up_low"), sem("down_low")
        x_high, x_low = sem("x_high"), sem("x_low")
        unit_ready, unit_turned, unit_high = sem("unit_ready"), sem("unit_turned"), sem("unit_high")
        silu_done, act_ready, mod_used = sem("silu_done"), sem("act_ready"), sem("mod_used")
        mod_summed, mod_col_done = sem("mod_summed"), sem("mod_col_done")
        panel_in = [sem("panel0_in"), sem("panel1_in")]
        panel_used = sem("panel_used")
        norm_in, param_in = sem("norm_in"), sem("param_in")
        var_ready, std_ready, norm_done = sem("var_ready"), sem("std_ready"), sem("norm_done")
        turned, ht_ready = sem("turned"), sem("ht_ready")
        param_turned, param_ready = sem("param_turned"), sem("param_ready")
        pair_done, pair_taken = sem("pair_done"), sem("pair_taken")
        z_done, z_taken, lora_done, lora_taken = sem("z_done"), sem("z_taken"), sem("lora_done"), sem("lora_taken")
        qkv_conv, qkv_silu = sem("qkv_conv"), sem("qkv_silu")
        soft_ready, decay_in, gate_log = sem("soft_ready"), sem("decay_in"), sem("gate_log")
        tok_done, tok_sq, tok_var, tok_std = sem("tok_done"), sem("tok_sq"), sem("tok_var"), sem("tok_std")
        tok_scaled, v_done, v_copied = sem("tok_scaled"), sem("v_done"), sem("v_copied")
        back_done, back_copied = sem("back_done"), sem("back_copied")
        cum_done, cum_taken, clamp_ready, decay_ready = sem("cum_done"), sem("cum_taken"), sem("clamp_ready"), sem("decay_ready")
        e_row_ready, kk_done, lower_ready = sem("e_row_ready"), sem("kk_done"), sem("lower_ready")
        inv_start, start_done, inv_ready = sem("inv_start"), sem("start_done"), sem("inv_ready")
        part_ready, turn_done, turn_copied, step_done = sem("part_ready"), sem("turn_done"), sem("turn_copied"), sem("step_done")
        join_done, uw_done, uw_copied = sem("join_done"), sem("uw_done"), sem("uw_copied")
        read_done, v_new_ready, o_done, o_copied = sem("read_done"), sem("v_new_ready"), sem("o_done"), sem("o_copied")
        write_done, state_ready = sem("write_done"), sem("state_ready")
        o_var, o_std, o_ready, o_turned, oT_ready = sem("o_var"), sem("o_std"), sem("o_ready"), sem("o_turned"), sem("oT_ready")
        z_scaled = sem("z_scaled")
        cv_conv, cv_turned, cv_var, cv_std, cv_norm = sem("cv_conv"), sem("cv_turned"), sem("cv_var"), sem("cv_std"), sem("cv_norm")
        cv_back, cv_ready = sem("cv_back"), sem("cv_ready")
        y_done, y_merged = sem("y_done"), sem("y_merged")
        lora_var, lora_std, lora_norm, lora_turned, lora_ready = (
            sem("lora_var"), sem("lora_std"), sem("lora_norm"), sem("lora_turned"), sem("lora_ready"))
        up_pair, up_taken, qv_done, v_taken, q_rotated = sem("up_pair"), sem("up_taken"), sem("qv_done"), sem("v_taken"), sem("q_rotated")
        rot_turned, rot_ready = sem("rot_turned"), sem("rot_ready")
        score_done, max_ready, exp_ready, prob_ready = sem("score_done"), sem("max_ready"), sem("exp_ready"), sem("prob_ready")
        probT_done, probT_ready, mo_done, mo_ready = sem("probT_done"), sem("probT_ready"), sem("mo_done"), sem("mo_ready")
        mix_done = sem("mix_done")
        diag_ready, grow_done, grow_ready, conv_ready = sem("diag_ready"), sem("grow_done"), sem("grow_ready"), sem("conv_ready")
        a_rotated, a_turned, a_qk_ready = sem("a_rotated"), sem("a_turned"), sem("a_qk_ready")
        a_scored, a_masked, a_max, a_exp = sem("a_scored"), sem("a_masked"), sem("a_max"), sem("a_exp")
        a_pT_done, a_pT_ready, a_o_done, a_o_ready = sem("a_pT_done"), sem("a_pT_ready"), sem("a_o_done"), sem("a_o_ready")
        a_oT_done, a_oT_ready = sem("a_oT_done"), sem("a_oT_ready")
        route_done, route_exp = sem("route_done"), sem("route_exp")
        chosen_ready, counted, plan_ready = sem("chosen_ready"), sem("counted"), sem("plan_ready")
        pick_ready, gathered, x_ready = sem("pick_ready"), sem("gathered"), sem("x_ready")
        weigh_ready, weigh_turned, weigh_taken = sem("weigh_ready"), sem("weigh_turned"), sem("weigh_taken")
        slots_taken, scattered, sum_done = sem("slots_taken"), sem("scattered"), sem("sum_done")
        out_ready, stored = sem("out_ready"), sem("stored")

        block = ctx.enter_context(nc.Block())

        @block.sync
        def _(sp):
            def row(ap):
                return ap.to_broadcast([P, ap.shape[-1]])

            def columns(s):
                return slice(s * FSTEP, (s + 1) * FSTEP) if isinstance(s, int) else bass.ds(s * FSTEP, FSTEP)

            def gate_load(gate, n, s):
                sp.wait_ge(gate_low, n + s + 1)
                sp.dma_start(gate_w[:], gate[:, :, columns(s % NS if isinstance(s, int) else s)]).then_inc(gate_in, 16)

            def up_load(up, n, s):
                sp.wait_ge(up_low, n + s + 1)
                sp.dma_start(up_w[:], up[:, :, columns(s % NS if isinstance(s, int) else s)]).then_inc(up_in, 16)

            def down_load(down, n, s):
                sp.wait_ge(down_low, n + s + 1)
                blocks = slice(s * FB, (s + 1) * FB) if isinstance(s, int) else bass.ds(s * FB, FB)
                sp.dma_start(down_w[:], down[:, blocks, :]).then_inc(down_in, 16)

            def ffn_loads(gate, up, down, n, mod=None, extra=None):
                def mod_load(s):
                    if mod is not None:
                        source, m = mod
                        sp.wait_ge(mod_used, m * MOD_UNITS + s + 1)
                        sp.dma_start(mod_w, source[:, :, columns(s)]).then_inc(mod_in, 16)

                gate_load(gate, n, 0)
                up_load(up, n, 0)
                down_load(down, n, 0)
                mod_load(0)
                gate_load(gate, n, 1)
                up_load(up, n, 1)
                mod_load(1)
                if extra is not None:
                    extra()
                with sp.Fori(2, NS) as s:
                    gate_load(gate, n, s)
                    mod_load(s)
                    up_load(up, n, s)
                    down_load(down, n, s - 1)
                mod_load(NS)
                down_load(down, n, NS - 1)

            def by_k(ap):
                return ap.rearrange("(k p) n -> p k n", p=P)

            def of_layer(name, l):
                w = a[name][bass.ds(l, 1)]
                return w.rearrange("o (k p) n -> p (o k) n", p=P)

            def panel_load(pieces, use, parity, l=None):
                sp.wait_ge(panel_used, use + 1)
                at = 0
                for name, r0, nr, c0, cols in pieces:
                    k = -(-nr // P)
                    src = a[name][bass.ds(l, 1), r0:r0 + nr, c0:c0 + cols] if l is not None else a[name][0:1, r0:r0 + nr, c0:c0 + cols]
                    if nr % P:
                        dst = panel[parity][0:nr, at:at + cols]
                        src = src.rearrange("o p n -> p (o n)")
                    else:
                        dst = v3(panel[parity], at, k, cols)
                        src = src.rearrange("o (k p) n -> p (o k) n", p=P)
                    sp.dma_start(dst, src).then_inc(panel_in[parity], 16)
                    at += k * cols

            def norm_loads(which, l):
                sp.dma_start(row_g[:], row(a[which + "_g"][bass.ds(l, 1), :])).then_inc(norm_in, 16)
                sp.dma_start(row_b[:], row(a[which + "_b"][bass.ds(l, 1), :])).then_inc(norm_in, 16)

            def param_loads(l):
                def to(at, n, name, pat, **kw):
                    sp.dma_start(rows[at:at + n, 0, :], a[name][bass.ds(l, 1)].rearrange(pat, **kw)).then_inc(param_in, 16)
                to(ROW_GATE, 24, "b_gate", "o (b p) -> (o b) p", p=P)
                to(ROW_CONV, 48, "dn_conv_w", "o j (b p) -> (o j b) p", p=P)
                to(ROW_GLU, 8, "cv_glu_b", "o (b p) -> (o b) p", p=P)
                to(ROW_DWB, 4, "cv_dw_b", "o (b p) -> (o b) p", p=P)
                to(ROW_LNG, 4, "cv_ln_g", "o (b p) -> (o b) p", p=P)
                to(ROW_LNB, 4, "cv_ln_b", "o (b p) -> (o b) p", p=P)
                to(ROW_PW, 8, "cv_b_pw2", "o (b p) -> (o b) p", p=P)
                to(ROW_QN, QB, "mla_q_norm_w", "o (b p) -> (o b) p", p=P)
                to(ROW_KVN, KVB, "mla_kv_norm_w", "o (b p) -> (o b) p", p=P)
                sp.dma_start(rows[0:TAPS * CB, 1, :],
                             a["cv_dw_w"][bass.ds(l, 1)].rearrange("o j (b p) -> (o j b) p", p=P)).then_inc(param_in, 16)
                sp.dma_start(norm_row[:], row(a["dn_norm_w"][bass.ds(l, 1), :])).then_inc(param_in, 16)
                sp.dma_start(head_rows[:, 0:HEADS], row(a["dn_a_log"][bass.ds(l, 1), :])).then_inc(param_in, 16)
                sp.dma_start(head_rows[:, HEADS:], row(a["dn_dt_bias"][bass.ds(l, 1), :])).then_inc(param_in, 16)

            sp.dma_start(H[:], a["x"][0].rearrange("(t p) d -> p t d", p=P)).then_inc(setup_in, 16)
            sp.dma_start(rows[0:96, 0, :], a["mod_b_2"].rearrange("i j (b p) -> (i j b) p", p=P)).then_inc(setup_row, 16)
            sp.dma_start(rows[96:128, 0, :], a["norm_g_2"].rearrange("i j (b p) -> (i j b) p", p=P)).then_inc(setup_row, 16)
            sp.dma_start(rows[0:8, 1, :], a["c_2"].rearrange("o (b p) -> (o b) p", p=P)).then_inc(setup_row, 16)
            sp.dma_start(rows[8:32, 1, :], a["conv_w_2"][0].rearrange("j (b p) -> (j b) p", p=P)).then_inc(setup_row, 16)
            pos = small[0:2 * TT, 0:P].bitcast(I32)
            sp.dma_start(pos[0:TT, :], a["positions"].rearrange("o (t p) -> (o t) p", p=P)).then_inc(setup_row, 16)
            sp.dma_start(pos[TT:2 * TT, :], a["positions_2"].rearrange("o (t p) -> (o t) p", p=P)).then_inc(setup_row, 16)
            sp.dma_start(router[:], by_k(a["router_w_2"][0])).then_inc(setup_row, 16)

            with sp.Fori(0, DEPTH) as l:
                n = l * FFN_LAYER
                mod = a["mod_w_2"][bass.ds(l, 1)]

                def first_extra():
                    param_loads(l)
                    norm_loads("ln1", l)
                ffn_loads(of_layer("ffn1_w_gate", l), of_layer("ffn1_w_up", l), of_layer("ffn1_w_down", l), n,
                          (mod[:, 0].rearrange("o (k p) n -> p (o k) n", p=P), l * 2), first_extra)
                for use, (_, pieces) in enumerate(MIXER_PANELS):
                    panel_load(pieces, l * MIX_USES + use, use % 2, l)
                    if use == 4:
                        norm_loads("ln2", l)
                ffn_loads(of_layer("ffn2_w_gate", l), of_layer("ffn2_w_up", l), of_layer("ffn2_w_down", l), n + NS,
                          (mod[:, 1].rearrange("o (k p) n -> p (o k) n", p=P), l * 2 + 1), lambda: norm_loads("ln3", l))

            for use, (name, pieces) in enumerate(SECOND_PANELS):
                panel_load(pieces, DEPTH * MIX_USES + use, use % 2)
                if name == "conv_out" and use == 7:
                    ffn_loads(by_k(a["ffn_w_gate_2"][0]), by_k(a["ffn_w_up_2"][0]), by_k(a["ffn_w_down_2"][0]), DEPTH * FFN_LAYER)
            sp.wait_ge(plan_ready, 1)
            items = sp.value_load(plan[0:1, ITEMS:ITEMS + 1], min_val=1, max_val=ITEMS - 1)

            def expert(i):
                e = sp.value_load(plan[0:1, i:i + 1] if isinstance(i, int) else plan[0:1, bass.ds(i, 1)], min_val=0, max_val=NE - 1)
                return [a[name][0, bass.ds(e, 1)].rearrange("o (k p) n -> p (o k) n", p=P)
                        for name in ("moe_w_gate_2", "moe_w_up_2", "moe_w_down_2")]

            first = DEPTH * FFN_LAYER + NS
            gate, up, _ = expert(0)
            for s in range(2):
                gate_load(gate, first, s)
                up_load(up, first, s)
            with sp.Fori(0, items) as i:
                n = first + i * NS
                gate, up, down = expert(i)
                down_load(down, n, 0)
                with sp.Fori(2, NS) as s:
                    gate_load(gate, n, s)
                    up_load(up, n, s)
                    down_load(down, n, s - 1)
                gate, up, _ = expert(i + 1)
                gate_load(gate, n, NS)
                up_load(up, n, NS)
                down_load(down, n, NS - 1)
                gate_load(gate, n, NS + 1)
                up_load(up, n, NS + 1)
            sp.wait_ge(norm_done, (DEPTH * LN_LAYER + 1) * TT)
            sp.dma_start(row_b[:], row(a["final_g_2"].rearrange("(o d) -> o d", o=1))).then_inc(norm_in, 16)
            for t in range(TT):
                sp.wait_ge(out_ready, t + 1)
                sp.dma_start(out[0, t * P:(t + 1) * P, :], H[:, t, :]).then_inc(stored, 16)
            sp.wait_ge(stored, 16 * TT)

        @block.gpsimd
        def _(pool):
            def keep(tile, op, pattern, base, step, fill):
                pool.drain()
                nc.gpsimd.affine_select(out=tile, in_=tile, pattern=pattern, compare_op=op, fill=fill, base=base,
                                        channel_multiplier=step)

            for tile, value in ((ident, 0.0), (ones, 1.0), (causal, 0.0), (prefix, 1.0), (strict, 1.0), (same, 1.0),
                                (in_chunk, 0.0), (level, 1.0)):
                nc.gpsimd.memset(tile[:], value)
            nc.gpsimd.memset(glu_pad[:, :, 0:32], 0.0)
            for j in range(HALF):
                nc.gpsimd.memset(small[:, 160 + j:161 + j], float(np.float32(10000.0) ** np.float32(-j / HALF)))
            keep(ident[:], ALU.not_equal, [[-1, P]], 0, 1, 1.0)
            pool.drain().then_inc(const_ready, 1)
            keep(causal[:], ALU.is_ge, [[-1, P]], 0, 1, MASKED)
            keep(prefix[:], ALU.is_ge, [[1, P]], 0, -1, 0.0)
            keep(strict[:], ALU.is_ge, [[-1, P]], -1, 1, 0.0)
            for i in range(6):
                b = 1 << i
                m = P // (2 * b)
                tile = level[:, i, :].rearrange("p (m s r) -> p m s r", s=2, r=b)
                keep(tile, ALU.is_ge, [[-2 * b, m], [0, 2], [0, b]], -b, 1, 0.0)
                keep(tile, ALU.is_ge, [[2 * b, m], [0, 2], [0, b]], 2 * b - 1, -1, 0.0)
            pool.drain()
            nc.gpsimd.memset(prefix[0:CHUNK, CHUNK:], 0.0)
            pool.drain()
            nc.gpsimd.memset(strict[CHUNK:, 0:CHUNK], 0.0)
            pool.drain()
            nc.gpsimd.memset(same[0:CHUNK, CHUNK:], 0.0)
            pool.drain()
            nc.gpsimd.memset(same[CHUNK:, 0:CHUNK], 0.0)
            for half in range(2):
                pool.drain()
                nc.gpsimd.memset(in_chunk[half * CHUNK:(half + 1) * CHUNK, half, :], 1.0)
            pool.drain()
            for i in range(6):
                b = 1 << i
                nc.gpsimd.memset(level[:, i, :].rearrange("p (m s r) -> p m s r", s=2, r=b)[:, :, 1, :], 0.0)
            pool.drain().then_inc(const_ready, 1)
            pool.wait_ge(angle_ready, 1)
            nc.gpsimd.memset(band[:, 0, :, :], 0.0)
            keep(band[:, 0, 1, :], ALU.is_ge, [[1, P]], 0, -1, MASKED)
            for g in range(AG):
                for i in (0, 2):
                    keep(band[:, g, i, :], ALU.is_ge, [[-1, P]], 0, 1, MASKED)
            pool.drain().then_inc(setup_done, 1)

            with pool.Fori(0, DEPTH) as l:
                pool.wait_ge(z_taken, l + 1)
                z = z_tok.rearrange("p t (h v) -> p (t h) v", h=HEADS)
                nc.gpsimd.tensor_tensor(z, z, norm_row[:].rearrange("p (o v) -> p o v", o=1).to_broadcast([P, TT * HEADS, HD]),
                                        ALU.mult).then_inc(z_scaled, 1)
                pool.wait_ge(lower_ready, l + 1)
                for i in range(1, 6):
                    if i > 1:
                        pool.wait_ge(turn_done, l * 10 + 2 * (i - 1))
                    nc.gpsimd.tensor_tensor(part.rearrange("p t h c -> p (t h) c"), lower.rearrange("p t h c -> p (t h) c"),
                                            level[:, i:i + 1, :].to_broadcast([P, TT * HEADS, P]), ALU.mult).then_inc(part_ready, 1)

        EXPERTS_AT = DEPTH * FFN_LAYER + NS

        mm = nc.tensor.matmul

        def turn(out, tile):
            k = tile.shape[0]
            return nc.tensor.transpose(out, tile, ident[0:k, 0:k])

        def split_mm(out, w, x, start, stop):
            mm(out, w[0], x[0], start=start, stop=False)
            mm(out, w[0], x[1], start=False, stop=False)
            return mm(out, w[1], x[0], start=False, stop=stop)

        def ffn_in(bank, weights):
            for f in range(FB):
                for k in range(KD):
                    last = split_mm(banks[:, bank, f * SEQ:(f + 1) * SEQ], [w[:, k, f * P:(f + 1) * P] for w in weights],
                                    [v[:, k, :] for v in x_parts], k == 0, k == KD - 1)
            return last

        def slots_in(bank, weights):
            for k in range(KD):
                last = split_mm(banks[:, bank, 0:FSTEP], [v[:, k, :] for v in slot_x_parts], [w[:, k, :] for w in weights], k == 0, k == KD - 1)
            return last

        def ffn_gate(pe, n, s, ffn_in=ffn_in):
            pe.wait_ge(gate_low, n + s + 2)
            pe.wait_ge(silu_done, n + s + 1)
            ffn_in(4, gate_parts).then_inc(gate_done, 1)

        def ffn_up(pe, n, s, ffn_in=ffn_in):
            pe.wait_ge(up_low, n + s + 2)
            pe.wait_ge(unit_ready, n + s + 1)
            ffn_in(5, up_parts).then_inc(up_done, 1)

        def ffn_down(pe, n, s, first=False, final=False, units=unit_parts, weights=down_parts, width=SEQ):
            pe.wait_ge(down_low, n + s + 2)
            pe.wait_ge(act_ready, n + s + 1)
            for f in range(FB):
                for t in range(width // P):
                    for c in range(2):
                        last = split_mm(banks[:, 2 * t + c, :], [u[:, f, t * P:(t + 1) * P] for u in units],
                                        [w[:, f, c * 512:(c + 1) * 512] for w in weights],
                                        first and f == 0, final and f == FB - 1)
            last.then_inc(down_done, 1)

        def ffn_pe(pe, n, f):
            pe.wait_ge(x_low, f * 2 + 2)
            ffn_gate(pe, n, 0)
            ffn_up(pe, n, 0)
            ffn_gate(pe, n, 1)
            ffn_up(pe, n, 1)
            ffn_down(pe, n, 0, first=True)
            with pe.Fori(2, NS) as s:
                ffn_gate(pe, n, s)
                ffn_up(pe, n, s)
                ffn_down(pe, n, s - 1)
            ffn_down(pe, n, NS - 1, final=True, units=last_unit_parts, weights=last_down_parts)

        def gather_pe(pe, i):
            pe.wait_ge(pick_ready, i + 1)
            for b in range(KD):
                for t in range(TT):
                    last = mm(banks[:, 6 + b // 4, (b % 4) * P:(b % 4 + 1) * P], x_norm[:, t, b * P:(b + 1) * P], pick[:, t, :],
                              start=t == 0, stop=t == TT - 1)
            last.then_inc(gathered, 1)

        def first_step(pe, n, i):
            pe.wait_ge(x_low, (i + FFNS) * 2 + 2)
            ffn_gate(pe, n, 0, slots_in)
            ffn_up(pe, n, 0, slots_in)

        def expert_pe(pe, n, i):
            to = dict(units=slot_unit_parts, width=P)

            def turn_units(s):
                pe.wait_ge(unit_ready, n + s + 2)
                for f in range(FB):
                    last = turn(banks[:, 3, f * P:(f + 1) * P], act_t[:, 0, f * P:(f + 1) * P])
                last.then_inc(unit_turned, 1)

            ffn_gate(pe, n, 1, slots_in)
            pe.wait_ge(weigh_ready, i + 1)
            pe.wait_ge(sum_done, i * 2 + 2)
            for t in range(TT):
                last = turn(banks[:, 2, t * P:(t + 1) * P], weigh[:, t, :])
            last.then_inc(weigh_turned, 1)
            turn_units(0)
            ffn_up(pe, n, 1, slots_in)
            ffn_down(pe, n, 0, first=True, **to)
            with pe.Fori(2, NS) as s:
                ffn_gate(pe, n, s, slots_in)
                turn_units(s - 1)
                ffn_up(pe, n, s, slots_in)
                ffn_down(pe, n, s - 1, **to)
            turn_units(NS - 1)
            gather_pe(pe, i + 1)
            ffn_down(pe, n, NS - 1, final=True, **to)
            first_step(pe, n + NS, i + 1)
            pe.wait_ge(slots_taken, i + 1)
            pe.wait_ge(weigh_taken, i + 1)
            pe.wait_ge(x_ready, i + 2)
            for t in range(TT):
                for c in range(2):
                    last = mm(banks[:, (2, 6)[t] + c, :], weighT[:, t, :], slot_out[:, c * 512:(c + 1) * 512], start=True, stop=True)
                last.then_inc(scattered, 1)

        def mod_pe(pe, m):
            pe.wait_ge(mod_summed, m + 1)
            for b in range(24):
                last = mm(banks[:, 4, b:b + 1], mod_sum[:, b * P:(b + 1) * P], ones[:, 0:1], start=True, stop=True)
            last.then_inc(mod_col_done, 1)

        def turn_h(pe, done):
            for t in range(TT):
                pe.wait_ge(norm_done, done + t + 1)
                for half in range(2):
                    for j in range(4):
                        b = 4 * half + j
                        last = turn(banks[:, (6, 4)[t] + half, j * P:(j + 1) * P], H[:, t, b * P:(b + 1) * P])
                    last.then_inc(turned, 1)

        act_fn = nc.scalar.activation

        def panel_high(act, n, s, landed_, done, tile, weights, high):
            act.wait_ge(landed_, (n + s) * 16 + 16)
            act.wait_ge(done, n + s + 1)
            for half in halves(tile):
                act_fn(weights[0][:, half, :], tile[:, half, :], ACT.Copy).then_inc(high, 1)

        def halves(tile):
            k = tile.shape[1] // 2
            return slice(0, k), slice(k, 2 * k)

        def gate_act(act, n, s):
            panel_high(act, n, s, gate_in, gate_done, gate_w, gate_parts, gate_high)

        def up_act(act, n, s):
            panel_high(act, n, s, up_in, up_done, up_w, up_parts, up_high)

        def down_act(act, n, s):
            panel_high(act, n, s, down_in, down_done, down_w, down_parts, down_high)

        def turned_tile(t):
            bank = (6, 4)[t]
            return banks[:, bank:bank + 2, :].rearrange("p h (j c) -> p (h j) c", j=4)

        def turned_act(act, before):
            for t in range(TT):
                act.wait_ge(turned, before + 2 * t + 2)
                act_fn(x_parts[0][:, :, t * P:(t + 1) * P], turned_tile(t), ACT.Copy).then_inc(x_high, 1)

        def x_high_act(act, x=x_parts, width=SEQ):
            act.drain()
            for half in halves(HT):
                act_fn(x[0][:, half, :], HT[:, half, 0:width], ACT.Copy).then_inc(x_high, 1)

        def silu_act(act, n, s, width):
            act.wait_ge(gate_done, n + s + 2)
            act.wait_ge(unit_ready, n + s + 1)
            act_fn(ffn_tmp[:, 0:width], banks[:, 4, 0:width], ACT.Silu).then_inc(silu_done, 1)

        def ffn_act(act, n):
            def step(s, final=False):
                silu_act(act, n, s, FB * SEQ)
                if final:
                    panel_high(act, n, s, down_in, gate_done, down_w, last_down_parts, down_high)
                else:
                    gate_act(act, n, s + 1)
                    up_act(act, n, s + 1)
                    down_act(act, n, s)
                act.wait_ge(unit_ready, n + s + 2)
                act_fn((last_unit_parts if final else unit_parts)[0], act_t, ACT.Copy).then_inc(unit_high, 1)

            up_act(act, n, 0)
            with act.Fori(0, NS - 1) as s:
                step(s)
            step(NS - 1, True)

        def first_step_act(act, n):
            silu_act(act, n, 0, FSTEP)
            gate_act(act, n, 1)
            up_act(act, n, 1)

        def expert_act(act, n, weigh_act):
            def unit_act(s):
                act.wait_ge(unit_turned, n + s - EXPERTS_AT + 1)
                act_fn(slot_unit_parts[0], banks[:, 3, 0:FSTEP].rearrange("p (f c) -> p f c", f=FB), ACT.Copy).then_inc(unit_high, 1)

            def step(s):
                silu_act(act, n, s, FSTEP)
                unit_act(s - 1)
                gate_act(act, n, s + 1)
                up_act(act, n, s + 1)
                down_act(act, n, s)

            down_act(act, n, 0)
            weigh_act()
            with act.Fori(1, NS) as s:
                step(s)
            unit_act(NS - 1)

        def std_act(act, m, eps):
            act.wait_ge(var_ready, m)
            act_fn(spread[:, :, 0], moments[:, :, 1], ACT.Sqrt, bias=eps).then_inc(std_ready, 1)

        def ht_act(act, before):
            for i in range(4):
                t, half = i // 2, i % 2
                act.wait_ge(turned, before + i + 1)
                act_fn(HT[:, 4 * half:4 * half + 4, t * P:(t + 1) * P],
                       banks[:, (6, 4)[t] + half, :].rearrange("p (b c) -> p b c", b=4), ACT.Copy).then_inc(ht_ready, 1)

        tt, ts, stt = nc.vector.tensor_tensor, nc.vector.tensor_scalar, nc.vector.scalar_tensor_tensor

        def wide(ap, *dims):
            if len(dims) == 2:
                return ap.rearrange("p (a o) -> p a o", o=1).to_broadcast([P, *dims])
            return ap.rearrange("p (a b o) -> p a b o", b=dims[1], o=1).to_broadcast([P, *dims])

        def mod_vec(dve, m, j, cols):
            dve.wait_ge(mod_in, (m * MOD_UNITS + j) * 16 + 16)
            ts(mod_sum[:, cols], mod_w[:, 0, :], misc_col[:, 0:1], None, ALU.mult)
            for k in range(1, KD):
                dve.drain()
                stt(mod_sum[:, cols], mod_w[:, k, :], misc_col[:, k:k + 1], mod_sum[:, cols], ALU.mult, ALU.add)
            dve.drain().then_inc(mod_used, 1)

        def panel_low(dve, n, s, high, tile, weights, low):
            for i, half in enumerate(halves(tile)):
                dve.wait_ge(high, (n + s) * 2 + i + 1)
                last = tt(weights[1][:, half, :], tile[:, half, :], weights[0][:, half, :].bitcast(F32), ALU.subtract)
            last.then_inc(low, 1)

        def gate_vec(dve, n, s):
            panel_low(dve, n, s, gate_high, gate_w, gate_parts, gate_low)

        def up_vec(dve, n, s):
            panel_low(dve, n, s, up_high, up_w, up_parts, up_low)

        def down_vec(dve, n, s):
            panel_low(dve, n, s, down_high, down_w, down_parts, down_low)

        def x_low_vec(dve, f, x=x_parts, width=SEQ):
            for i, half in enumerate(halves(HT)):
                dve.wait_ge(x_high, f * 2 + i + 1)
                tt(x[1][:, half, :], HT[:, half, 0:width], x[0][:, half, :].bitcast(F32), ALU.subtract).then_inc(x_low, 1)

        def turned_vec(dve, f):
            for t in range(TT):
                c = slice(t * P, (t + 1) * P)
                dve.wait_ge(x_high, f * 2 + t + 1)
                tt(x_parts[1][:, :, c], turned_tile(t), x_parts[0][:, :, c].bitcast(F32), ALU.subtract).then_inc(x_low, 1)

        def unit_vec(dve, n, s, width):
            dve.wait_ge(silu_done, n + s + 2)
            dve.wait_ge(up_done, n + s + 2)
            tt(v3(ffn_tmp, FB * SEQ, width), ffn_tmp[:, 0:width], banks[:, 5, 0:width], ALU.mult).then_inc(unit_ready, 1)

        def ffn_vec(dve, n, m=None):
            def step(s, final=False):
                if not final:
                    gate_vec(dve, n, s + 1)
                if m is not None and not final:
                    mod_vec(dve, m, s + 1, bass.ds(s * MOD_COLS + MOD_COLS, MOD_COLS))
                elif m is not None:
                    mod_vec(dve, m, NS, slice(NS * MOD_COLS, 3 * D))
                    dve.drain().then_inc(mod_summed, 1)
                dve.drain()
                unit_vec(dve, n, s, FB * SEQ)
                if final:
                    panel_low(dve, n, s, down_high, down_w, last_down_parts, down_low)
                else:
                    up_vec(dve, n, s + 1)
                    down_vec(dve, n, s)
                units = last_unit_parts if final else unit_parts
                dve.wait_ge(unit_high, n + s + 1)
                tt(units[1], act_t, units[0].bitcast(F32), ALU.subtract).then_inc(act_ready, 1)

            up_vec(dve, n, 0)
            if m is not None:
                mod_vec(dve, m, 0, slice(0, MOD_COLS))
            with dve.Fori(0, NS - 1) as s:
                step(s)
            step(NS - 1, True)

        def first_step_vec(dve, n):
            gate_vec(dve, n, 1)
            unit_vec(dve, n, 0, FSTEP)
            up_vec(dve, n, 1)

        def expert_vec(dve, n):
            def low_units(s):
                dve.wait_ge(unit_high, n + s + 1)
                tt(slot_unit_parts[1], banks[:, 3, 0:FSTEP].rearrange("p (f c) -> p f c", f=FB), slot_unit_parts[0].bitcast(F32),
                   ALU.subtract).then_inc(act_ready, 1)

            def step(s):
                low_units(s - 1)
                gate_vec(dve, n, s + 1)
                unit_vec(dve, n, s, FSTEP)
                up_vec(dve, n, s + 1)
                down_vec(dve, n, s)

            down_vec(dve, n, 0)
            with dve.Fori(1, NS) as s:
                step(s)
            low_units(NS - 1)

        def layer_norm(dve, m, scale, mod=None):
            for t in range(TT):
                stt(H[:, t, :], H[:, t, :], scale, acc[:, t, :], ALU.mult, ALU.add)
            dve.drain()
            for t in range(TT):
                for half in range(2):
                    nc.vector.bn_stats(stats[:, t, half, :], H[:, t, half * 512:(half + 1) * 512])
            dve.drain()
            for t in range(TT):
                nc.vector.bn_aggr(moments[:, t, :], stats[:, t, :, :])
            dve.drain().then_inc(var_ready, 1)
            dve.wait_ge(norm_in, m * 32)
            for t in range(TT):
                stt(H[:, t, :], H[:, t, :], moments[:, t, 0:1], row_g[:], ALU.subtract, ALU.mult)
            dve.wait_ge(std_ready, m)
            nc.vector.reciprocal(spread[:, :, 1], spread[:, :, 0])
            dve.drain()
            for t in range(TT):
                stt(H[:, t, :], H[:, t, :], spread[:, t, 1:2], row_b[:], ALU.mult, ALU.add).then_inc(norm_done, 1)
                if t == 0 and mod is not None:
                    dve.wait_ge(mod_col_done, mod + 1)
                    tt(mod_col[:, bass.ds(mod * 24, 24)], banks[:, 4, 0:24], mod_bias[:, bass.ds(mod * 24, 24)], ALU.add)

        def mixer_pe(pe, l):
            def panel_ready(use):
                pe.wait_ge(panel_in[use % 2], l * LANDED_LAYER[use % 2] + landed(use))
                return panel[use % 2]

            def pair_bank(i):
                if i >= 4:
                    pe.wait_ge(pair_taken, l * 23 + i - 3)
                return banks[:, 4 + i % 4, :]

            def project(tile, c, bank, half):
                for k in range(KD):
                    last = mm(bank[:, half * SEQ:(half + 1) * SEQ], tile[:, k, c:c + P], HT[:, k, :], start=k == 0, stop=k == KD - 1)
                return last

            def projection(use, first_pair):
                tile = v3(panel_ready(use), 0, KD, PANEL)
                for j in range(2):
                    bank = pair_bank(first_pair + j)
                    for half in range(2):
                        last = project(tile, (2 * j + half) * P, bank, half)
                    last.then_inc(pair_done, 1)
                    if j == 1:
                        pe.drain().then_inc(panel_used, 1)

            pe.wait_ge(param_in, l * 208 + 208)
            pe.wait_ge(ht_ready, l * 4 + 4)
            turn(banks[:, 7, 0:ROWS], rows[0:ROWS, 0, :])
            turn(banks[:, 7, P:P + TAPS * CB], rows[0:TAPS * CB, 1, :]).then_inc(param_turned, 1)
            for use in range(3):
                projection(use, 2 * use)
                if use == 0:
                    pe.wait_ge(param_ready, l + 1)
            for use in range(2):
                projection(3 + use, 6 + 2 * use)
            tile = v3(panel_ready(5), 0, KD, 520)
            small_bank = pair_bank(10)
            for t in range(TT):
                for k in range(KD):
                    last = mm(banks[:, t, :], HT[:, k, t * P:(t + 1) * P], tile[:, k, 0:512], start=k == 0, stop=k == KD - 1)
            last.then_inc(z_done, 1)
            for t in range(TT):
                for k in range(KD):
                    mm(small_bank[:, 8 * t:8 * t + 8], HT[:, k, t * P:(t + 1) * P], tile[:, k, 512:520],
                       start=k == 0, stop=k == KD - 1)
            pe.drain().then_inc(panel_used, 1)
            tile = v3(panel_ready(6), 0, KD, PANEL)
            for t in range(TT):
                for k in range(KD):
                    mm(banks[:, 2 + t, :], HT[:, k, t * P:(t + 1) * P], tile[:, k, :], start=k == 0, stop=k == KD - 1)
            pe.drain().then_inc(panel_used, 1)
            tile = v3(panel_ready(7), 0, KD, 192)
            for t in range(TT):
                for k in range(KD):
                    last = mm(small_bank[:, 16 + 192 * t:208 + 192 * t], HT[:, k, t * P:(t + 1) * P], tile[:, k, :],
                              start=k == 0, stop=k == KD - 1)
            last.then_inc(lora_done, 1)
            pe.drain().then_inc(panel_used, 1)

            pe.wait_ge(qkv_silu, l + 1)
            pe.wait_ge(z_taken, l + 1)
            pe.wait_ge(lora_taken, l + 1)
            for which in range(2):
                for t in range(TT):
                    for h in range(HEADS):
                        last = turn(banks[:, 2 * which + t, h * HD:(h + 1) * HD], conv[:, 4 * which + h, t * P:(t + 1) * P])
            last.then_inc(tok_done, 1)
            projection(8, 11)
            pe.wait_ge(tok_scaled, l + 1)
            for t in range(TT):
                for h in range(HEADS):
                    last = turn(banks[:, t, h * HD:(h + 1) * HD], conv[:, 8 + h, t * P:(t + 1) * P])
            last.then_inc(v_done, 1)
            for h in range(HEADS):
                for t in range(TT):
                    last = turn(banks[:, 2 + h // 2, (h % 2) * SEQ + t * P:(h % 2) * SEQ + (t + 1) * P], q_tok[:, t, h, :])
            last.then_inc(back_done, 1)
            projection(9, 13)
            pe.wait_ge(v_copied, l + 1)
            for h in range(HEADS):
                for t in range(TT):
                    last = turn(banks[:, h // 2, (h % 2) * SEQ + t * P:(h % 2) * SEQ + (t + 1) * P], k_tok[:, t, h, :])
            last.then_inc(back_done, 1)
            pe.wait_ge(back_copied, l * 2 + 1)
            pe.wait_ge(decay_in, l + 1)
            for t in range(TT):
                for h in range(HEADS):
                    mm(banks[:, 2 + t, h * P:(h + 1) * P], g_wide[:, t, h, :], prefix[:], start=True, stop=True)
            pe.wait_ge(back_copied, l * 2 + 2)
            g = small[:, 0:8]
            for t in range(TT):
                gt = g[:, t * HEADS:(t + 1) * HEADS]
                mm(banks[:, 0, 4 * t:4 * t + 4], prefix[:], gt, start=True, stop=True)
                mm(banks[:, 0, 8 + 4 * t:12 + 4 * t], same[:], gt, start=True, stop=True)
                for half in range(2):
                    c = 2 * t + half
                    last = mm(banks[:, 0, 16 + 4 * c:20 + 4 * c], in_chunk[:, half, :], gt, start=True, stop=True)
            last.then_inc(cum_done, 1)
            projection(10, 15)
            pe.wait_ge(cum_taken, l + 1)
            for t in range(TT):
                for h in range(HEADS):
                    mm(banks[:, t, h * P:(h + 1) * P], kT[:, h, t * P:(t + 1) * P], kT[:, h, t * P:(t + 1) * P], start=True, stop=True)
            pe.wait_ge(e_row_ready, l + 1)
            for t in range(TT):
                for h in range(HEADS):
                    last = mm(banks[:, 2 + t, h * P:(h + 1) * P], kT[:, h, t * P:(t + 1) * P], qT[:, h, t * P:(t + 1) * P], start=True, stop=True)
            last.then_inc(kk_done, 1)
            projection(11, 17)
            pe.wait_ge(inv_start, l + 1)
            for t in range(TT):
                for h in range(HEADS):
                    last = turn(banks[:, t, h * P:(h + 1) * P], inv[:, t, h, :])
            last.then_inc(start_done, 1)
            for i in range(5):
                pe.wait_ge(part_ready, l * 5 + i + 1)
                for t in range(TT):
                    if i == 0:
                        pe.wait_ge(inv_ready, l + 1)
                    else:
                        pe.wait_ge(step_done, l * 10 + 2 * (i - 1) + t + 1)
                    for h in range(HEADS):
                        last = mm(banks[:, t, h * P:(h + 1) * P], part[:, t, h, :], inv_t[:, t, h, :], start=True, stop=True)
                    last.then_inc(turn_done, 1)
                if i < 2:
                    projection(12 + i, 19 + 2 * i)
                for t in range(TT):
                    pe.wait_ge(turn_copied, l * 10 + 2 * i + t + 1)
                    if i < 4:
                        for h in range(HEADS):
                            mm(banks[:, 2 + t, h * P:(h + 1) * P], turn_b[:, t, h, :], inv[:, t, h, :], start=True, stop=True)
                    for h in range(HEADS):
                        last = mm(banks[:, t, h * P:(h + 1) * P], inv[:, t, h, :], turn_b[:, t, h, :], start=True, stop=True)
                    last.then_inc(join_done, 1)
            pe.wait_ge(cv_conv, l + 1)
            pe.wait_ge(pair_taken, l * 23 + 23)
            for t in range(TT):
                for b in range(CB):
                    last = turn(banks[:, 4 + t, b * P:(b + 1) * P], cv_acc[:, b, t * P:(t + 1) * P])
            last.then_inc(cv_turned, 1)
            pe.wait_ge(step_done, l * 10 + 10)
            for t in range(TT):
                for h in range(HEADS):
                    mm(banks[:, t, h * HD:(h + 1) * HD], inv_t[:, t, h, :], v_beta[:, t, h, :], start=True, stop=True)
            for t in range(TT):
                for h in range(HEADS):
                    last = mm(banks[:, 2 + t, h * P:(h + 1) * P], k_beta[:, t, h, :], inv_t[:, t, h, :], start=True, stop=True)
            last.then_inc(uw_done, 1)
            pe.wait_ge(cv_norm, l + 1)
            for t in range(TT):
                for b in range(CB):
                    last = turn(banks[:, 6 + b // 2, (b % 2) * SEQ + t * P:(b % 2) * SEQ + (t + 1) * P], cv_tok[:, t, b * P:(b + 1) * P])
            last.then_inc(cv_back, 1)

            def out_pairs(tile, src, kb, j, y, need, count):
                pe.wait_ge(need, count)
                for half in range(2):
                    b = 2 * j + half
                    for k in range(kb):
                        last = mm(banks[:, 4 + j, half * SEQ:(half + 1) * SEQ], tile[:, k, b * P:(b + 1) * P], src[:, k, :],
                                  start=k == 0, stop=k == kb - 1)
                last.then_inc(y_done, 1)

            pe.wait_ge(uw_copied, l + 1)
            cv_tile = v3(panel_ready(14), 0, CB, D)
            for c in range(4):
                t, r = c // 2, slice((c % 2) * CHUNK, (c % 2 + 1) * CHUNK)
                state = states[(c + 1) % 2]
                if c:
                    pe.wait_ge(state_ready, l * 3 + c)
                    for h in range(HEADS):
                        last = mm(banks[:, 0, h * HD:(h + 1) * HD], wT[:, t, h, :], state[:, h, :], start=True, stop=True)
                    last.then_inc(read_done, 1)
                    pe.wait_ge(v_new_ready, l * 3 + c)
                    if c > 1:
                        pe.wait_ge(o_copied, l * 4 + c)
                src = v_new if c else u_tok
                if c < 3:
                    for h in range(HEADS):
                        last = mm(banks[:, 2, h * HD:(h + 1) * HD], k_dec[r, t, h, :], src[r, t, h, :], start=True, stop=True)
                    last.then_inc(write_done, 1)
                if c == 1:
                    pe.wait_ge(o_copied, l * 4 + c)
                for h in range(HEADS):
                    if c:
                        mm(banks[:, 1, h * HD:(h + 1) * HD], e_row[:, t, h, :], state[:, h, :], start=True, stop=False)
                    last = mm(banks[:, 1, h * HD:(h + 1) * HD], qk[r, t, h, :], src[r, t, h, :], start=not c, stop=True)
                last.then_inc(o_done, 1)
                if c == 0:
                    pe.wait_ge(cv_ready, l * 2 + 2)
                out_pairs(cv_tile, cvT, CB, c, 0, cv_ready, l * 2 + 2)
            pe.drain().then_inc(panel_used, 1)
            pe.wait_ge(o_ready, l + 1)
            for h in range(HEADS):
                for t in range(TT):
                    last = turn(banks[:, h // 2, (h % 2) * SEQ + t * P:(h % 2) * SEQ + (t + 1) * P], o_tok[:, t, h, :])
            last.then_inc(o_turned, 1)
            tile = v3(panel_ready(15), 0, HEADS, D)
            pe.wait_ge(oT_ready, l + 1)
            for j in range(4):
                out_pairs(tile, oT, HEADS, j, 1, y_merged, l * 12 + j + 1)
            pe.drain().then_inc(panel_used, 1)

            pe.wait_ge(lora_norm, l + 1)
            for b in range(QB + KVB):
                bank = (0, 0, 1, 2, 2)[b]
                at = (0, SEQ, 0, 0, SEQ)[b]
                for t in range(TT):
                    last = turn(banks[:, bank, at + t * P:at + (t + 1) * P], lora[:, t, b * P:(b + 1) * P])
            last.then_inc(lora_turned, 1)
            tile = panel_ready(16)
            uq = v3(tile, 0, QB, HEADS * (NOPE + ROPE))
            ukv = v3(tile, QB * HEADS * (NOPE + ROPE), KVB, HEADS * (NOPE + VD))
            uq_h = uq.rearrange("p k (h c) -> p k h c", h=HEADS)
            ukv_h = ukv.rearrange("p k (h c) -> p k h c", h=HEADS)
            pe.wait_ge(lora_ready, l + 1)
            for t in range(TT):
                for k in range(QB):
                    mm(banks[:, 3, t * SEQ:(t + 1) * SEQ].rearrange("p (h c) -> p h c", h=HEADS), cqT[:, k, t * P:(t + 1) * P],
                       uq_h[:, k, :, NOPE:], start=k == 0, stop=k == QB - 1)
            for t in range(TT):
                for k in range(KVB):
                    last = mm(banks[:, t, :].rearrange("p (h c) -> p h c", h=HEADS), ckvT[:, k, t * P:(t + 1) * P],
                              ukv_h[:, k, :, NOPE:], start=k == 0, stop=k == KVB - 1)
            last.then_inc(qv_done, 1)
            for j in range(4):
                pe.wait_ge(y_merged, l * 12 + 4 + j + 1)
                src, w, kb = (cqT, uq_h, QB) if j < 2 else (ckvT, ukv_h, KVB)
                for half in range(2):
                    h = 2 * (j % 2) + half
                    for k in range(kb):
                        last = mm(banks[:, 4 + j, half * SEQ:(half + 1) * SEQ], w[:, k, h, 0:NOPE], src[:, k, :],
                                  start=k == 0, stop=k == kb - 1)
                last.then_inc(up_pair, 1)
            pe.drain().then_inc(panel_used, 1)
            pe.wait_ge(q_rotated, l + 1)
            for j in range(2):
                for t in range(TT):
                    turn(banks[:, 2, j * SEQ + t * P:j * SEQ + (t + 1) * P],
                         q_rot[:, t, 2 * j:2 * j + 2, :].rearrange("p h c -> p (h c)"))
            for t in range(TT):
                last = turn(banks[:, 3, t * P:(t + 1) * P], k_rot[:, t, :, :].rearrange("p h c -> p (h c)"))
            last.then_inc(rot_turned, 1)
            pe.wait_ge(up_taken, l * 4 + 4)
            pe.wait_ge(rot_ready, l + 1)
            for h in range(HEADS):
                r = slice((h % 2) * ROPE, (h % 2 + 1) * ROPE)
                for t in range(TT):
                    n = (t + 1) * P
                    dst = banks[:, 4 + 3 * (h % 2), (h // 2) * P:(h // 2 + 1) * P] if t == 0 else banks[:, 5 + h % 2, (h // 2) * SEQ:(h // 2 + 1) * SEQ]
                    mm(dst, qnT[:, h, t * P:(t + 1) * P], knT[:, h, 0:n], start=True, stop=False)
                    last = mm(dst, qrT[r, h // 2, t * P:(t + 1) * P], krT[r, 0:n], start=False, stop=True)
            last.then_inc(score_done, 1)
            pe.wait_ge(v_taken, l + 1)
            pe.wait_ge(prob_ready, l + 1)
            for h in range(HEADS):
                for i in range(3):
                    src = first_s[:, h, :] if i == 0 else second_s[:, h, (i - 1) * P:i * P]
                    last = turn(banks[:, (h * 3 + i) // 4, ((h * 3 + i) % 4) * P:((h * 3 + i) % 4 + 1) * P], src)
            last.then_inc(probT_done, 1)
            pe.wait_ge(probT_ready, l + 1)
            for h in range(HEADS):
                dst = banks[:, 4 + h // 2, (h % 2) * SEQ:(h % 2 + 1) * SEQ]
                mm(dst[:, 0:P], v_tok[:, 0, h * VD:(h + 1) * VD], probT[:, h, 0, :], start=True, stop=True)
                for kt in range(TT):
                    last = mm(dst[:, P:], v_tok[:, kt, h * VD:(h + 1) * VD], probT[:, h, 1 + kt, :], start=kt == 0, stop=kt == TT - 1)
            last.then_inc(mo_done, 1)
            tile = v3(panel_ready(17), 0, HEADS, D)
            pe.wait_ge(mo_ready, l + 1)
            for j in range(4):
                out_pairs(tile, moT, HEADS, j, 2, mo_ready, l + 1)
            pe.drain().then_inc(panel_used, 1)
            for i in range(2):
                tile = v3(panel_ready(18 + i), 0, 4, D)
                for k in range(4):
                    if k % 2 == 0:
                        pe.wait_ge(y_merged, l * 12 + 8 + (4 * i + k) // 2 + 1)
                    for t in range(TT):
                        for c in range(2):
                            last = mm(banks[:, 2 * t + c, :], merged[:, 4 * i + k, t * P:(t + 1) * P], tile[:, k, c * 512:(c + 1) * 512],
                                      start=i == 0 and k == 0, stop=i == 1 and k == 3)
                pe.drain().then_inc(panel_used, 1)
            pe.drain().then_inc(mix_done, 1)

        def mixer_act(act, l):
            def copy(out, src):
                return act_fn(out, src, ACT.Copy)

            def flat(ap):
                return ap.rearrange("p a b -> p (a b)")

            def gate_pair(i):
                act.wait_ge(pair_done, l * 22 + i)
                for half in range(2):
                    b = 2 * (i - 11) + half
                    last = act_fn(gates[:, b, :], banks[:, 4 + i % 4, half * SEQ:(half + 1) * SEQ], ACT.Sigmoid,
                                  bias=pcol[:, ROW_GATE + b:ROW_GATE + b + 1])
                last.then_inc(pair_taken, 1)

            act.wait_ge(param_turned, l + 1)
            copy(pcol[:, 0:ROWS], banks[:, 7, 0:ROWS])
            copy(dwcol[:, 0:TAPS * CB], banks[:, 7, P:P + TAPS * CB]).then_inc(param_ready, 1)
            for i in range(6):
                act.wait_ge(pair_done, l * 22 + i + 1)
                copy(raw[:, 2 * i:2 * i + 2, 4:260], banks[:, 4 + i % 4, :].rearrange("p (a b) -> p a b", a=2)).then_inc(pair_taken, 1)
            act.drain()
            for i in range(6, 10):
                act.wait_ge(pair_done, l * 22 + i + 1)
                for half in range(2):
                    b = 2 * (i - 6) + half
                    dst = glu_a[:, b, :] if b < CB else glu_s[:, b - CB, :]
                    last = act_fn(dst, banks[:, 4 + i % 4, half * SEQ:(half + 1) * SEQ], ACT.Identity if b < CB else ACT.Sigmoid,
                                  bias=pcol[:, ROW_GLU + b:ROW_GLU + b + 1])
                last.then_inc(pair_taken, 1)
            act.wait_ge(qkv_conv, l + 1)
            for i in range(3):
                last = act_fn(flat(conv[:, 4 * i:4 * i + 4, :]), flat(conv[:, 4 * i:4 * i + 4, :]), ACT.Silu)
            last.then_inc(qkv_silu, 1)
            act.wait_ge(z_done, l + 1)
            for t in range(TT):
                last = act_fn(z_tok[:, t, :], banks[:, t, :], ACT.Silu)
            last.then_inc(z_taken, 1)
            act.wait_ge(lora_done, l + 1)
            copy(flat(logits), banks[:, 6, 0:16])
            copy(lora[:, :, 512:704], banks[:, 6, 16:400].rearrange("p (t c) -> p t c", t=TT)).then_inc(pair_taken, 1)
            for t in range(TT):
                last = copy(lora[:, t, 0:512], banks[:, 2 + t, :])
            last.then_inc(lora_taken, 1)
            act.wait_ge(tok_done, l + 1)
            for i in range(4):
                last = act_fn(qk_sq[:, i, :, :].rearrange("p h c -> p (h c)"), banks[:, i, :], ACT.Square)
            last.then_inc(tok_sq, 1)
            act.wait_ge(soft_ready, l + 1)
            act_fn(v3(small, 8, TT, HEADS), logits[:, :, HEADS:], ACT.Sigmoid)
            act_fn(neg_a, head_rows[:, 0:HEADS], ACT.Exp)
            act_fn(soft_n, soft_n, ACT.Exp)
            act.drain()
            act_fn(soft_n, soft_n, ACT.Ln, bias=1.0).then_inc(gate_log, 1)
            act.wait_ge(tok_var, l + 1)
            act_fn(tok_sum, tok_sum, ACT.Sqrt, bias=L2_EPS).then_inc(tok_std, 1)
            gate_pair(11)
            gate_pair(12)
            act.wait_ge(v_done, l + 1)
            for t in range(TT):
                last = copy(v_beta[:, t, :, :].rearrange("p h c -> p (h c)"), banks[:, t, :])
            last.then_inc(v_copied, 1)
            act.wait_ge(back_done, l * 2 + 1)
            for i in range(2):
                last = copy(flat(qT[:, 2 * i:2 * i + 2, :]), banks[:, 2 + i, :])
            last.then_inc(back_copied, 1)
            gate_pair(13)
            gate_pair(14)
            act.wait_ge(back_done, l * 2 + 2)
            for i in range(2):
                last = copy(flat(kT[:, 2 * i:2 * i + 2, :]), banks[:, i, :])
            last.then_inc(back_copied, 1)
            act.wait_ge(clamp_ready, l + 1)
            for tile, sign in ((lower, -1.0), (qk, 1.0)):
                f = tile.rearrange("p t h c -> p (t h c)")
                last = act_fn(f, f, ACT.Exp, scale=sign)
            last.then_inc(decay_ready, 1)
            for t in range(TT):
                act_fn(e_row[:, t, :, :].rearrange("p h c -> p (h c)"), banks[:, 2 + t, :], ACT.Exp)
            act_fn(cum_e, cum, ACT.Exp)
            act_fn(dec_scale, dec_scale, ACT.Exp)
            act_fn(chunk_e, chunk_total, ACT.Exp).then_inc(e_row_ready, 1)
            for i in range(15, 19):
                gate_pair(i)
            act.wait_ge(start_done, l + 1)
            for t in range(TT):
                last = copy(inv_t[:, t, :, :].rearrange("p h c -> p (h c)"), banks[:, t, :])
            last.then_inc(inv_ready, 1)
            for i in range(5):
                for t in range(TT):
                    act.wait_ge(turn_done, l * 10 + 2 * i + t + 1)
                    if i:
                        act.wait_ge(join_done, l * 10 + 2 * (i - 1) + t + 1)
                    copy(turn_b[:, t, :, :].rearrange("p h c -> p (h c)"), banks[:, t, :]).then_inc(turn_copied, 1)
                if i < 2:
                    gate_pair(19 + 2 * i)
                    gate_pair(20 + 2 * i)
            act.wait_ge(lora_var, l + 1)
            act_fn(lora_scale, lora_ms, ACT.Sqrt, bias=LN_EPS).then_inc(lora_std, 1)
            act.wait_ge(cv_var, l + 1)
            act_fn(cv_scale, cv_mom[:, :, 1], ACT.Sqrt, bias=LN_EPS).then_inc(cv_std, 1)
            act.wait_ge(uw_done, l + 1)
            for t in range(TT):
                copy(u_tok[:, t, :, :].rearrange("p h c -> p (h c)"), banks[:, t, :])
            for t in range(TT):
                last = copy(wT[:, t, :, :].rearrange("p h c -> p (h c)"), banks[:, 2 + t, :])
            last.then_inc(uw_copied, 1)
            act.wait_ge(cv_back, l + 1)
            for b in range(CB):
                last = act_fn(cvT[:, b, :], banks[:, 6 + b // 2, (b % 2) * SEQ:(b % 2 + 1) * SEQ], ACT.Silu,
                              scale=pcol[:, ROW_LNG + b:ROW_LNG + b + 1], bias=pcol[:, ROW_LNB + b:ROW_LNB + b + 1])
                if b % 2:
                    last.then_inc(cv_ready, 1)
            for c in range(4):
                r = slice((c % 2) * CHUNK, (c % 2 + 1) * CHUNK)
                act.wait_ge(o_done, l * 4 + c + 1)
                copy(o_tok[r, c // 2, :, :].rearrange("p h c -> p (h c)"), banks[r, 1, :]).then_inc(o_copied, 1)
            act.wait_ge(o_var, l + 1)
            act_fn(o_scale, o_sum, ACT.Sqrt, scale=1.0 / HD, bias=LN_EPS).then_inc(o_std, 1)
            act.wait_ge(o_turned, l + 1)
            for i in range(2):
                last = copy(flat(oT[:, 2 * i:2 * i + 2, :]), banks[:, i, :])
            last.then_inc(oT_ready, 1)
            act.wait_ge(lora_turned, l + 1)
            for b in range(QB + KVB):
                bank, at = (0, 0, 1, 2, 2)[b], (0, SEQ, 0, 0, SEQ)[b]
                dst = cqT[:, b, :] if b < QB else ckvT[:, b - QB, :]
                last = act_fn(dst, banks[:, bank, at:at + SEQ], ACT.Identity, scale=pcol[:, ROW_QN + b:ROW_QN + b + 1], bias=0.0)
            last.then_inc(lora_ready, 1)
            act.wait_ge(qv_done, l + 1)
            for t in range(TT):
                last = copy(v_tok[:, t, :], banks[:, t, :])
            last.then_inc(v_taken, 1)
            for j in range(4):
                act.wait_ge(up_pair, l * 4 + j + 1)
                dst = qnT if j < 2 else knT
                copy(flat(dst[:, 2 * (j % 2):2 * (j % 2) + 2, :]), banks[:, 4 + j, :]).then_inc(up_taken, 1)
            act.wait_ge(rot_turned, l + 1)
            copy(flat(qrT), banks[:, 2, :])
            copy(krT, banks[:, 3, 0:SEQ]).then_inc(rot_ready, 1)
            act.wait_ge(max_ready, l + 1)
            for h in range(HEADS):
                for i, tile in enumerate((first_s, second_s)):
                    c = 4 * i + h
                    last = act_fn(tile[:, h, :], tile[:, h, :], ACT.Exp, scale=MLA_SCALE, bias=s_max[:, c:c + 1], accum_out=s_sum[:, c:c + 1])
            act.drain().then_inc(exp_ready, 1)
            act.wait_ge(probT_done, l + 1)
            for i in range(3):
                last = copy(probT.rearrange("p h i c -> p (h i c)")[:, i * 512:(i + 1) * 512], banks[:, i, :])
            last.then_inc(probT_ready, 1)
            act.wait_ge(mo_done, l + 1)
            for i in range(2):
                last = copy(flat(moT[:, 2 * i:2 * i + 2, :]), banks[:, 4 + i, :])
            last.then_inc(mo_ready, 1)

        def mixer_vec(dve, l):
            def one(ap):
                return ap.rearrange("p (o c) -> p o c", o=1)

            def th(ap):
                return ap.rearrange("p (t h) -> p t h", t=TT)

            nc.vector.memset(raw[:, :, 0:4], 0.0)
            dve.drain()
            dve.wait_ge(param_ready, l + 1)
            dve.wait_ge(pair_taken, l * 23 + 6)
            for j in range(4):
                for b in range(12):
                    w = pcol[:, ROW_CONV + 12 * j + b:ROW_CONV + 12 * j + b + 1]
                    if j == 0:
                        ts(conv[:, b, :], raw[:, b, 1:1 + SEQ], w, None, ALU.mult)
                    else:
                        stt(conv[:, b, :], raw[:, b, 1 + j:1 + j + SEQ], w, conv[:, b, :], ALU.mult, ALU.add)
                if j < 3:
                    dve.drain()
            dve.drain().then_inc(qkv_conv, 1)
            dve.wait_ge(pair_taken, l * 23 + 10)
            tt(glu_pad[:, :, 32:32 + SEQ], glu_a, glu_s, ALU.mult)
            for j in range(TAPS):
                dve.drain()
                for b in range(CB):
                    w = dwcol[:, CB * j + b:CB * j + b + 1]
                    src = glu_pad[:, b, 2 + j:2 + j + SEQ]
                    if j == 0:
                        ts(cv_acc[:, b, :], src, w, pcol[:, ROW_DWB + b:ROW_DWB + b + 1], ALU.mult, ALU.add)
                    else:
                        stt(cv_acc[:, b, :], src, w, cv_acc[:, b, :], ALU.mult, ALU.add)
            dve.drain().then_inc(cv_conv, 1)
            dve.wait_ge(lora_taken, l + 1)
            for t in range(TT):
                tt(soft_x[:, 4 * t:4 * t + 4], logits[:, t, 0:HEADS], head_rows[:, HEADS:], ALU.add)
            dve.drain()
            ts(soft_n, soft_x, -1.0, None, ALU.mult)
            dve.drain()
            tt(soft_n, soft_n, soft_x, ALU.min).then_inc(soft_ready, 1)
            dve.wait_ge(tok_sq, l + 1)
            nc.vector.tensor_reduce(tok_sum, qk_sq.rearrange("p a h c -> p (a h) c"), AX.X, ALU.add).then_inc(tok_var, 1)
            dve.wait_ge(gate_log, l + 1)
            ts(soft_x, soft_x, 0.0, None, ALU.max)
            ts(neg_a, neg_a, -1.0, None, ALU.mult)
            dve.drain()
            tt(soft_x, soft_x, soft_n, ALU.add)
            dve.drain()
            for t in range(TT):
                tt(log_g[:, 4 * t:4 * t + 4], soft_x[:, 4 * t:4 * t + 4], neg_a, ALU.mult)
            dve.wait_ge(tok_std, l + 1)
            nc.vector.reciprocal(tok_scale, tok_sum)
            dve.drain()
            for i in range(4):
                dst = (q_tok if i < 2 else k_tok)[:, i % 2, :, :]
                last = tt(dst, banks[:, i, :].rearrange("p (h c) -> p h c", h=HEADS), wide(tok_scale[:, 4 * i:4 * i + 4], HEADS, HD), ALU.mult)
            last.then_inc(tok_scaled, 1)
            dve.wait_ge(v_done, l + 1)
            nc.vector.tensor_copy(g_wide.rearrange("p t h c -> p (t h) c"), wide(log_g, TT * HEADS, P)).then_inc(decay_in, 1)
            dve.wait_ge(v_copied, l + 1)
            tt(v_beta.rearrange("p t h c -> p (t h) c"), v_beta.rearrange("p t h c -> p (t h) c"), wide(beta, TT * HEADS, HD), ALU.mult)
            dve.wait_ge(cum_done, l + 1)
            nc.vector.tensor_copy(small[:, 16:48], banks[:, 0, 0:32]).then_inc(cum_taken, 1)
            dve.drain()
            for t in range(TT):
                for h in range(HEADS):
                    row = banks[:, 2 + t, h * P:(h + 1) * P]
                    col = cum[:, 4 * t + h:4 * t + h + 1]
                    ts(lower[:, t, h, :], row, col, 0.0, ALU.subtract, ALU.max)
                    ts(qk[:, t, h, :], row, col, 0.0, ALU.subtract, ALU.min)
            tt(dec_scale, total, cum, ALU.subtract)
            dve.drain().then_inc(clamp_ready, 1)
            dve.wait_ge(decay_ready, l + 1)
            tt(lower.rearrange("p t h c -> p (t h) c"), lower.rearrange("p t h c -> p (t h) c"),
               one(strict[:]).to_broadcast([P, TT * HEADS, P]), ALU.mult)
            tt(qk.rearrange("p t h c -> p (t h) c"), qk.rearrange("p t h c -> p (t h) c"),
               one(prefix[:]).to_broadcast([P, TT * HEADS, P]), ALU.mult)
            dve.wait_ge(e_row_ready, l + 1)
            tt(k_scale, beta, cum_e, ALU.mult)
            dve.drain()
            k8 = k_tok.rearrange("p t h c -> p (t h) c")
            tt(k_beta.rearrange("p t h c -> p (t h) c"), k8, wide(k_scale, TT * HEADS, HD), ALU.mult)
            tt(k_dec.rearrange("p t h c -> p (t h) c"), k8, wide(dec_scale, TT * HEADS, HD), ALU.mult)
            dve.wait_ge(back_copied, l * 2 + 1)
            for t in range(TT):
                stt(e_row[:, t, :, :], e_row[:, t, :, :], DN_SCALE, qT[:, :, t * P:(t + 1) * P], ALU.mult, ALU.mult)
            dve.wait_ge(kk_done, l + 1)
            for t in range(TT):
                for h in range(HEADS):
                    stt(lower[:, t, h, :], banks[:, t, h * P:(h + 1) * P], beta[:, 4 * t + h:4 * t + h + 1], lower[:, t, h, :], ALU.mult, ALU.mult)
            for t in range(TT):
                f = qk[:, t, :, :].rearrange("p h c -> p (h c)")
                stt(f, banks[:, 2 + t, :], DN_SCALE, f, ALU.mult, ALU.mult)
            dve.drain().then_inc(lower_ready, 1)
            inv8 = inv.rearrange("p t h c -> p (t h) c")
            tt(inv8, lower.rearrange("p t h c -> p (t h) c"), level[:, 0:1, :].to_broadcast([P, TT * HEADS, P]), ALU.mult)
            dve.drain()
            tt(inv8, one(ident[:]).to_broadcast([P, TT * HEADS, P]), inv8, ALU.subtract).then_inc(inv_start, 1)
            for t in range(TT):
                nc.vector.bn_stats(lora_stats[:, t, 0, :], lora[:, t, 0:QL])
                nc.vector.bn_stats(lora_stats[:, t, 1, :], lora[:, t, QL:QL + KVL])
            dve.drain()
            for t in range(TT):
                for i in range(2):
                    nc.vector.bn_aggr(lora_mom[:, t, i, :], lora_stats[:, t, i, :])
            dve.drain()
            ms = v3(small, 224, TT, 2)
            tt(ms, lora_mom[:, :, :, 0], lora_mom[:, :, :, 0], ALU.mult)
            dve.drain()
            tt(ms, ms, lora_mom[:, :, :, 1], ALU.add).then_inc(lora_var, 1)
            for i in range(5):
                for t in range(TT):
                    dve.wait_ge(join_done, l * 10 + 2 * i + t + 1)
                    if i < 4:
                        f = inv[:, t, :, :].rearrange("p h c -> p (h c)")
                        tt(f, f, banks[:, 2 + t, :], ALU.subtract)
                    f = inv_t[:, t, :, :].rearrange("p h c -> p (h c)")
                    tt(f, f, banks[:, t, :], ALU.subtract).then_inc(step_done, 1)
                if i < 4:
                    dve.drain()
            dve.wait_ge(cv_turned, l + 1)
            for t in range(TT):
                nc.vector.bn_stats(cv_stats[:, t, :], banks[:, 4 + t, :])
            dve.drain()
            for t in range(TT):
                nc.vector.bn_aggr(cv_mom[:, t, :], cv_stats[:, t, :])
            dve.drain().then_inc(cv_var, 1)
            dve.wait_ge(lora_std, l + 1)
            dve.wait_ge(cv_std, l + 1)
            nc.vector.reciprocal(lora_scale, lora_scale)
            nc.vector.reciprocal(cv_scale, cv_scale)
            dve.drain()
            for t in range(TT):
                last = ts(cv_tok[:, t, :], banks[:, 4 + t, :], cv_mom[:, t, 0:1], cv_scale[:, t:t + 1], ALU.subtract, ALU.mult)
            last.then_inc(cv_norm, 1)
            for t in range(TT):
                ts(lora[:, t, 0:QL], lora[:, t, 0:QL], lora_scale[:, 2 * t:2 * t + 1], None, ALU.mult)
                last = ts(lora[:, t, QL:QL + KVL], lora[:, t, QL:QL + KVL], lora_scale[:, 2 * t + 1:2 * t + 2], None, ALU.mult)
            last.then_inc(lora_norm, 1)
            for c in range(4):
                t, r = c // 2, slice((c % 2) * CHUNK, (c % 2 + 1) * CHUNK)
                if c:
                    dve.wait_ge(read_done, l * 3 + c)
                    tt(v_new[r, t, :, :].rearrange("p h c -> p (h c)"), u_tok[r, t, :, :].rearrange("p h c -> p (h c)"),
                       banks[r, 0, :], ALU.subtract).then_inc(v_new_ready, 1)
                if c < 3:
                    dve.wait_ge(write_done, l * 3 + c + 1)
                    if c == 0:
                        nc.vector.tensor_copy(states[0].rearrange("p h c -> p (h c)"), banks[:, 2, :]).then_inc(state_ready, 1)
                    else:
                        for h in range(HEADS):
                            last = stt(states[c % 2][:, h, :], states[(c + 1) % 2][:, h, :], chunk_e[:, 4 * c + h:4 * c + h + 1], banks[:, 2, h * HD:(h + 1) * HD],
                                       ALU.mult, ALU.add)
                        last.then_inc(state_ready, 1)
                    dve.drain()
                dve.wait_ge(y_done, l * 12 + c + 1)
                for half in range(2):
                    b = 2 * c + half
                    last = stt(merged[:, b, :], banks[:, 4 + c, half * SEQ:(half + 1) * SEQ], pcol[:, ROW_PW + b:ROW_PW + b + 1],
                               gates[:, KD + b, :], ALU.add, ALU.mult)
                last.then_inc(y_merged, 1)
            dve.wait_ge(o_copied, l * 4 + 4)
            o8 = o_tok.rearrange("p t h c -> p (t h) c")
            sq8 = square.rearrange("p t (h c) -> p (t h) c", h=HEADS)
            tt(sq8, o8, o8, ALU.mult)
            dve.drain()
            nc.vector.tensor_reduce(o_sum, sq8, AX.X, ALU.add).then_inc(o_var, 1)
            dve.wait_ge(o_std, l + 1)
            nc.vector.reciprocal(o_scale, o_scale)
            dve.drain()
            tt(o8, o8, wide(o_scale, TT * HEADS, HD), ALU.mult)
            dve.drain()
            dve.wait_ge(z_scaled, l + 1)
            tt(o8, o8, z_tok.rearrange("p t (h c) -> p (t h) c", h=HEADS), ALU.mult).then_inc(o_ready, 1)

            def merge(j, first_y, first_gate):
                dve.wait_ge(y_done, l * 12 + first_y + j + 1)
                tt(branch, banks[:, 4 + j, :].rearrange("p (a b) -> p a b", a=2), gates[:, first_gate + 2 * j:first_gate + 2 * j + 2, :], ALU.mult)
                dve.drain()
                m = merged[:, 2 * j:2 * j + 2, :]
                tt(m, m, branch, ALU.add).then_inc(y_merged, 1)
                dve.drain()

            for j in range(4):
                merge(j, 4, 0)
            dve.wait_ge(qv_done, l + 1)
            for t in range(TT):
                q = banks[:, 3, t * SEQ:(t + 1) * SEQ].rearrange("p (h c) -> p h c", h=HEADS)
                k = lora[:, t, QL + KVL:704].rearrange("p (o c) -> p o c", o=1)
                for heads, src, dsts in ((HEADS, q, (q_rot[:, t, :, :],)), (1, k, (k_rot[:, t, 0:1, :], k_rot[:, t, 1:2, :]))):
                    cos = cosine[:, 0, t:t + 1, :].to_broadcast([P, heads, HALF])
                    sin = sine[:, 0, t:t + 1, :].to_broadcast([P, heads, HALF])
                    at = (t * 5 + (0 if heads > 1 else 4)) * HALF
                    part_ = [rope_t[:, i, at:at + heads * HALF].rearrange("p (h c) -> p h c", h=heads) for i in range(4)]
                    x1, x2 = src[:, :, 0:HALF], src[:, :, HALF:]
                    tt(part_[0], x1, cos, ALU.mult)
                    tt(part_[1], x2, sin, ALU.mult)
                    tt(part_[2], x2, cos, ALU.mult)
                    tt(part_[3], x1, sin, ALU.mult)
                    dve.drain()
                    for dst in dsts:
                        tt(dst[:, :, 0:HALF], part_[0], part_[1], ALU.subtract)
                        tt(dst[:, :, HALF:], part_[2], part_[3], ALU.add)
            dve.drain().then_inc(q_rotated, 1)
            dve.wait_ge(score_done, l + 1)
            mask = one(causal[:]).to_broadcast([P, 2, P])
            for j in range(2):
                src = banks[:, 4 + 3 * j, 0:SEQ].rearrange("p (h c) -> p h c", h=2)
                tt(first_s[:, j::2, :], src, mask, ALU.add)
                src = banks[:, 5 + j, :].rearrange("p (h c) -> p h c", h=2)
                nc.vector.tensor_copy(second_s[:, j::2, 0:P], src[:, :, 0:P])
                tt(second_s[:, j::2, P:], src[:, :, P:], mask, ALU.add)
            dve.drain()
            nc.vector.tensor_reduce(s_max[:, 0:4], first_s, AX.X, ALU.max)
            nc.vector.tensor_reduce(s_max[:, 4:8], second_s, AX.X, ALU.max)
            dve.drain()
            ts(s_max, s_max, -MLA_SCALE, None, ALU.mult).then_inc(max_ready, 1)
            dve.wait_ge(exp_ready, l + 1)
            nc.vector.reciprocal(s_sum, s_sum)
            dve.drain()
            tt(first_s, first_s, wide(s_sum[:, 0:4], HEADS, P), ALU.mult)
            tt(second_s, second_s, wide(s_sum[:, 4:8], HEADS, SEQ), ALU.mult).then_inc(prob_ready, 1)
            for j in range(4):
                merge(j, 8, 2 * KD)
            dve.wait_ge(mix_done, l + 1)

        NORMS = DEPTH * LN_LAYER
        FFN2 = DEPTH * FFN_LAYER
        FFNS = 2 * DEPTH + 1
        PAIRS, TAKEN = DEPTH * 22, DEPTH * 23

        @block.tensor
        def _(pe):
            for s in (gate_done, up_done, down_done):
                pe.drain().then_inc(s, 1)
            pe.drain().then_inc(panel_used, 2)
            pe.wait_ge(const_ready, 1)
            pe.wait_ge(setup_row, 112)
            pe.wait_ge(pos_ready, 1)
            turn(banks[:, 0, 0:P], rows[:, 0, :])
            turn(banks[:, 0, P:P + 32], rows[0:32, 1, :])
            turn(banks[:, 0, 160:164], small[0:2 * TT, 192:192 + P]).then_inc(setup_turned, 1)
            pe.wait_ge(col_ready, 1)

            pe.wait_ge(const_ready, 2)
            with pe.Fori(0, DEPTH) as l:
                n = l * FFN_LAYER
                turn_h(pe, l * 6)
                ffn_pe(pe, n, l * 2)
                mod_pe(pe, l * 2)
                turn_h(pe, l * 6 + 2)
                mixer_pe(pe, l)
                turn_h(pe, l * 6 + 4)
                ffn_pe(pe, n + NS, l * 2 + 1)
                mod_pe(pe, l * 2 + 1)

            def norm_pe(j):
                pe.wait_ge(norm_done, 2 * (NORMS + 2 + j))
                for q in range(4):
                    for half in range(2):
                        b = 2 * q + half
                        for t in range(TT):
                            last = turn(banks[:, 4 + q, half * SEQ + t * P:half * SEQ + (t + 1) * P], x_norm[:, t, b * P:(b + 1) * P])
                    last.then_inc(turned, 1)
                pe.wait_ge(diag_ready, j + 1)
                for i in range(2):
                    last = mm(banks[:, i, :], ones[:], diag[:, 4 * i:4 * i + 4, :].rearrange("p b c -> p (b c)"), start=True, stop=True)
                last.then_inc(grow_done, 1)
                pe.wait_ge(ht_ready, 4 * (DEPTH + 1 + j))
                pe.wait_ge(grow_ready, j + 1)

            def panel_ready(use):
                pe.wait_ge(panel_in[use % 2], landed_second(use))
                return panel[use % 2]

            norm_pe(0)
            for use in range(6):
                tile = v3(panel_ready(use), 0, KD, PANEL)
                for j in range(2):
                    i = 2 * use + j
                    if i >= 4:
                        pe.wait_ge(pair_taken, TAKEN + i - 3)
                    for half in range(2):
                        c = (2 * j + half) * P
                        for k in range(KD):
                            last = mm(banks[:, 4 + i % 4, half * SEQ:(half + 1) * SEQ], tile[:, k, c:c + P], HT[:, k, :],
                                      start=k == 0, stop=k == KD - 1)
                    last.then_inc(pair_done, 1)
                pe.drain().then_inc(panel_used, 1)
            pe.wait_ge(conv_ready, 1)
            for i in range(2):
                tile = v3(panel_ready(6 + i), 0, 4, D)
                for k in range(4):
                    for t in range(TT):
                        for c in range(2):
                            mm(banks[:, 2 * t + c, :], conv_o[:, 4 * i + k, t * P:(t + 1) * P], tile[:, k, c * 512:(c + 1) * 512],
                               start=i == 0 and k == 0, stop=i == 1 and k == 3)
                pe.drain().then_inc(panel_used, 1)
            pe.drain().then_inc(mix_done, 1)

            norm_pe(1)
            ffn_pe(pe, FFN2, FFNS - 1)

            norm_pe(2)
            for i in range(12):
                use, t = 8 + i // 2, i % 2
                cols = min(PANEL, 2 * AW - PANEL * (i // 2)) if i < 8 else AW // 2
                tile = v3(panel_ready(use), 0, KD, cols)
                if i >= 4:
                    pe.wait_ge(pair_taken, TAKEN + 8 + i - 3)
                for k in range(KD):
                    last = mm(banks[:, 4 + i % 4, 0:cols], HT[:, k, t * P:(t + 1) * P], tile[:, k, :], start=k == 0, stop=k == KD - 1)
                last.then_inc(pair_done, 1)
                if t == 1:
                    pe.drain().then_inc(panel_used, 1)
            pe.wait_ge(a_rotated, TT)
            pe.wait_ge(pair_taken, TAKEN + 8 + 12)
            for q in range(8):
                for half in range(2):
                    b = 2 * (q % 4) + half
                    n = min(P, AW - b * P)
                    c = (q // 4) * AW + b * P
                    for t in range(TT):
                        last = turn(banks[0:n, q, half * SEQ + t * P:half * SEQ + (t + 1) * P], a_rot[:, t, c:c + n])
                last.then_inc(a_turned, 1)
            pe.wait_ge(a_qk_ready, 8)
            for h in range(AH):
                if h >= 8:
                    pe.wait_ge(a_masked, h - 7)
                r, b = slice((h % 2) * AD, (h % 2 + 1) * AD), h // 2
                mm(banks[:, h % 8, 0:P], a_qT[r, b, 0:P], a_kT[r, b, 0:P], start=True, stop=True)
                mm(banks[:, h % 8, P:3 * P], a_qT[r, b, P:], a_kT[r, b, :], start=True, stop=True).then_inc(a_scored, 1)
            pe.wait_ge(a_masked, AH)
            for h in range(AH + 1):
                if h < AH:
                    pe.wait_ge(a_exp, h + 1)
                    if h >= 4:
                        pe.wait_ge(a_pT_ready, h - 3)
                    for i in range(3):
                        last = turn(banks[:, 4 + h % 4, i * P:(i + 1) * P], a_s[:, h, i * P:(i + 1) * P])
                    last.then_inc(a_pT_done, 1)
                if h:
                    g = h - 1
                    pe.wait_ge(a_pT_ready, g + 1)
                    c = (g % 8) * AD
                    v = a_v[:, :, g * AD:(g + 1) * AD]
                    mm(banks[:, g // 8, c:c + AD], a_pT[:, g, 0, :], v[:, 0, :], start=True, stop=True)
                    mm(banks[:, 2 + g // 8, c:c + AD], a_pT[:, g, 1, :], v[:, 0, :], start=True, stop=False)
                    last = mm(banks[:, 2 + g // 8, c:c + AD], a_pT[:, g, 2, :], v[:, 1, :], start=False, stop=True)
            last.then_inc(a_o_done, 1)
            pe.wait_ge(a_o_ready, 1)
            for q in range(4):
                for half in range(2):
                    b = 2 * q + half
                    n = min(P, AW - b * P)
                    for t in range(TT):
                        last = turn(banks[0:n, 4 + q, half * SEQ + t * P:half * SEQ + (t + 1) * P], a_o[:, t, b * P:b * P + n])
                last.then_inc(a_oT_done, 1)
            pe.wait_ge(a_oT_ready, 4)
            for i in range(2):
                tile = v3(panel_ready(14 + i), 0, 4, D)
                for k in range(4):
                    n = min(P, AW - (4 * i + k) * P)
                    for t in range(TT):
                        for c in range(2):
                            mm(banks[:, 2 * t + c, :], a_oT[0:n, 4 * i + k, t * P:(t + 1) * P], tile[0:n, k, c * 512:(c + 1) * 512],
                               start=i == 0 and k == 0, stop=i == 1 and k == 3)
                pe.drain().then_inc(panel_used, 1)
            pe.drain().then_inc(mix_done, 1)

            norm_pe(3)
            for t in range(TT):
                for k in range(KD):
                    last = mm(banks[:, 6, t * NE:(t + 1) * NE], HT[:, k, t * P:(t + 1) * P], router[:, k, :], start=k == 0, stop=k == KD - 1)
            last.then_inc(route_done, 1)
            pe.wait_ge(chosen_ready, 1)
            for t in range(TT):
                mm(banks[:, 7, t * NE:(t + 1) * NE], prefix[:], chosen[:, t, :], start=True, stop=t == 0)
                if t:
                    mm(banks[:, 7, t * NE:(t + 1) * NE], ones[:], chosen[:, 0, :], start=False, stop=True)
            for t in range(TT):
                mm(banks[:, 7, 16:16 + NE], ones[:], chosen[:, t, :], start=t == 0, stop=t == TT - 1)
            mm(banks[:, 6, 0:P], ones[:], prefix[:], start=True, stop=True).then_inc(counted, 1)
            pe.wait_ge(plan_ready, 1)
            items = pe.value_load(plan[0:1, ITEMS:ITEMS + 1], min_val=1, max_val=ITEMS - 1)
            gather_pe(pe, 0)
            first_step(pe, EXPERTS_AT, 0)
            with pe.Fori(0, items) as i:
                expert_pe(pe, EXPERTS_AT + i * NS, i)

        @block.scalar
        def _(act):
            act.drain().then_inc(silu_done, 1)
            act.wait_ge(setup_turned, 1)
            act_fn(mod_bias[:], banks[:, 0, 0:P], ACT.Copy)
            act_fn(misc_col[:, 0:8], banks[:, 0, P:P + 8], ACT.Silu)
            act_fn(misc_col[:, 8:32], banks[:, 0, P + 8:P + 32], ACT.Copy)
            act_fn(small[:, 320:324], banks[:, 0, 160:164], ACT.Copy).then_inc(col_ready, 1)
            act.wait_ge(angle_ready, 1)
            act_fn(sine.rearrange("p s t c -> p (s t c)"), arena[:, 0:P], ACT.Sin)
            act_fn(cosine.rearrange("p s t c -> p (s t c)"), arena[:, P:2 * P], ACT.Sin).then_inc(rope_ready, 1)

            with act.Fori(0, DEPTH) as l:
                n = l * FFN_LAYER
                gate_act(act, n, 0)
                turned_act(act, l * 12)
                ffn_act(act, n)
                std_act(act, l * LN_LAYER + 1, 4 * LN_EPS)
                ht_act(act, l * 12 + 4)
                mixer_act(act, l)
                std_act(act, l * LN_LAYER + 2, LN_EPS)
                gate_act(act, n + NS, 0)
                turned_act(act, l * 12 + 8)
                ffn_act(act, n + NS)
                std_act(act, l * LN_LAYER + 3, 4 * LN_EPS)

            def rms_act(j):
                act.wait_ge(var_ready, NORMS + 1 + j)
                for t in range(TT):
                    act_fn(x_norm[:, t, :], H[:, t, :], ACT.Square, accum_out=moments[:, t, 1:2])
                act.drain()
                act_fn(spread[:, :, 0], moments[:, :, 1], ACT.Sqrt, scale=1.0 / D, bias=RMS_EPS).then_inc(std_ready, 1)

            def norm_act(j):
                rms_act(j)
                for q in range(4):
                    act.wait_ge(turned, 4 * (NORMS + j) + q + 1)
                    for half in range(2):
                        b = 2 * q + half
                        last = act_fn(HT[:, b, :], banks[:, 4 + q, half * SEQ:(half + 1) * SEQ], ACT.Identity,
                                      scale=mod_scale[:, b:b + 1], bias=mod_col[:, 24 * j + b:24 * j + b + 1])
                    last.then_inc(ht_ready, 1)
                act.wait_ge(grow_done, j + 1)
                for i in range(2):
                    last = act_fn(gate_row[:, i * 512:(i + 1) * 512], banks[:, i, :], ACT.Copy)
                last.then_inc(grow_ready, 1)

            norm_act(0)
            for i in range(8):
                act.wait_ge(pair_done, PAIRS + i + 1)
                dst = b_conv if i < 4 else c_conv
                act_fn(dst[:, 2 * (i % 4):2 * (i % 4) + 2, :], banks[:, 4 + i % 4, :].rearrange("p (a b) -> p a b", a=2), ACT.Copy).then_inc(pair_taken, 1)
            norm_act(1)
            gate_act(act, FFN2, 0)
            x_high_act(act)
            ffn_act(act, FFN2)
            norm_act(2)
            for i in range(12):
                act.wait_ge(pair_done, PAIRS + 12 + i + 1)
                use, t = i // 2, i % 2
                cols = min(PANEL, 2 * AW - PANEL * use) if i < 8 else AW // 2
                dst = a_qk[:, t, use * PANEL:use * PANEL + cols] if i < 8 else a_v[:, t, (use - 4) * cols:(use - 3) * cols]
                act_fn(dst, banks[:, 4 + i % 4, 0:cols], ACT.Copy).then_inc(pair_taken, 1)

            def blocks_act(dst, bank, q):
                if q < 3:
                    return act_fn(dst[:, 2 * q:2 * q + 2, :], banks[:, bank, :].rearrange("p (a b) -> p a b", a=2), ACT.Copy)
                act_fn(dst[:, 6, :], banks[:, bank, 0:SEQ], ACT.Copy)
                return act_fn(dst[0:AW % P, 7, :], banks[0:AW % P, bank, SEQ:], ACT.Copy)

            for q in range(8):
                act.wait_ge(a_turned, q + 1)
                blocks_act(a_qT if q < 4 else a_kT, q, q % 4).then_inc(a_qk_ready, 1)
            act.wait_ge(a_max, 1)
            act_fn(a_up, a_up, ACT.Exp)
            for h in range(AH):
                for t in range(TT):
                    i = t * AH + h
                    s = a_s[:, h, 0:P] if t == 0 else a_s[:, h, P:]
                    act_fn(s, s, ACT.Exp, scale=A_SCALE, bias=a_neg[:, i:i + 1], accum_out=a_sum[:, i:i + 1])
                act.drain().then_inc(a_exp, 1)
            for q in range(4):
                act.wait_ge(a_oT_done, q + 1)
                blocks_act(a_oT, 4 + q, q).then_inc(a_oT_ready, 1)
            norm_act(3)
            act.wait_ge(route_exp, 1)
            act_fn(r_exp, r_exp, ACT.Exp).then_inc(route_exp, 1)

            def gathered_act(i):
                act.wait_ge(gathered, i + 1)
                for b in range(KD):
                    last = act_fn(HT[:, b, 0:P], banks[:, 6 + b // 4, (b % 4) * P:(b % 4 + 1) * P], ACT.Identity,
                                  scale=mod_scale[:, b:b + 1], bias=mod_col[:, 72 + b:73 + b])
                last.then_inc(x_ready, 1)
                x_high_act(act, slot_x_parts, P)

            act.wait_ge(plan_ready, 1)
            items = act.value_load(plan[0:1, ITEMS:ITEMS + 1], min_val=1, max_val=ITEMS - 1)
            gathered_act(0)
            gate_act(act, EXPERTS_AT, 0)
            up_act(act, EXPERTS_AT, 0)
            first_step_act(act, EXPERTS_AT)
            with act.Fori(0, items) as i:
                def weigh_act():
                    act.wait_ge(weigh_turned, i + 1)
                    act_fn(weighT.rearrange("p t c -> p (t c)"), banks[:, 2, 0:SEQ], ACT.Copy).then_inc(weigh_taken, 1)
                n = EXPERTS_AT + i * NS
                expert_act(act, n, weigh_act)
                gathered_act(i + 1)
                act.wait_ge(down_done, n + NS + 1)
                for c in range(2):
                    last = act_fn(slot_out[:, c * 512:(c + 1) * 512], banks[:, c, :], ACT.Copy)
                last.then_inc(slots_taken, 1)
                first_step_act(act, n + NS)
            rms_act(4)

        @block.vector
        def _(dve):
            for s in (gate_low, up_low, down_low, unit_ready, mod_used):
                dve.drain().then_inc(s, 1)
            dve.wait_ge(setup_in, 16)
            dve.drain().then_inc(norm_done, TT)
            dve.wait_ge(setup_row, 112)
            nc.vector.tensor_copy(small[0:2 * TT, 192:192 + P], small[0:2 * TT, 0:P].bitcast(I32)).then_inc(pos_ready, 1)
            dve.wait_ge(const_ready, 1)
            dve.wait_ge(col_ready, 1)
            angle, other, turns = arena[:, 0:P], arena[:, P:2 * P], arena[:, 2 * P:3 * P]
            for i in range(2 * TT):
                ts(angle[:, i * HALF:(i + 1) * HALF], inv_freq, small[:, 320 + i:321 + i], None, ALU.mult)
            dve.drain()
            ts(turns, angle, float(1 / TWO_PI), None, ALU.mult)
            dve.drain()
            ts(turns, turns, ROUND, None, ALU.add)
            dve.drain()
            ts(turns, turns, ROUND, None, ALU.subtract)
            for part_ in (PI_A, PI_B, PI_C):
                dve.drain()
                stt(angle, turns, -part_, angle, ALU.mult, ALU.add)
            dve.drain()
            ts(other, angle, float(np.pi / 2), None, ALU.add)
            dve.drain()
            ts(turns, other, float(np.pi), -TWO_PI, ALU.is_gt, ALU.mult)
            dve.drain()
            tt(other, other, turns, ALU.add)
            dve.drain()
            ts(arena[:, 0:2 * P], arena[:, 0:2 * P], PI_SAFE, -PI_SAFE, ALU.min, ALU.max)
            for g in (1, 2):
                r = DILATIONS[g]
                hot = arena[:, 3 * P + 16 * g:3 * P + 16 * g + r]
                nc.vector.tensor_reduce(hot, ident[:].rearrange("p (m r) -> p r m", r=r), AX.X, ALU.add)
                dve.drain()
                ts(hot, hot, 1.0, -MASKED, ALU.subtract, ALU.mult)
                dve.drain()
                nc.vector.tensor_copy(band[:, g, :, :].rearrange("p i (m r) -> p (i m) r", r=r),
                                      hot.rearrange("p (o r) -> p o r", o=1).to_broadcast([P, 3 * P // r, r]))
            dve.drain().then_inc(angle_ready, 1)
            dve.wait_ge(rope_ready, 1)
            dve.wait_ge(const_ready, 2)

            with dve.Fori(0, DEPTH) as l:
                n = l * FFN_LAYER
                gate_vec(dve, n, 0)
                turned_vec(dve, l * 2)
                ffn_vec(dve, n, l * 2)
                dve.wait_ge(down_done, n + NS + 1)
                layer_norm(dve, l * LN_LAYER + 1, 2 * ALPHA, l * 2)
                mixer_vec(dve, l)
                layer_norm(dve, l * LN_LAYER + 2, ALPHA)
                gate_vec(dve, n + NS, 0)
                turned_vec(dve, l * 2 + 1)
                ffn_vec(dve, n + NS, l * 2 + 1)
                dve.wait_ge(down_done, n + 2 * NS + 1)
                layer_norm(dve, l * LN_LAYER + 3, 2 * ALPHA, l * 2 + 1)

            def norm_vec(j):
                m = NORMS + 1 + j
                dve.drain()
                stt(mod_scale, mod_col[:, 24 * j + 8:24 * j + 16], 1.0, mod_bias[:, 96 + 8 * j:104 + 8 * j], ALU.add, ALU.mult)
                dve.drain().then_inc(var_ready, 1)
                for b in range(KD):
                    last = ts(diag[:, b, :], ident[:], mod_col[:, 24 * j + 16 + b:24 * j + 17 + b], None, ALU.mult)
                last.then_inc(diag_ready, 1)
                dve.wait_ge(std_ready, m)
                nc.vector.reciprocal(spread[:, :, 1], spread[:, :, 0])
                dve.drain()
                for t in range(TT):
                    ts(x_norm[:, t, :], H[:, t, :], spread[:, t, 1:2], None, ALU.mult).then_inc(norm_done, 1)

            def residual(j, src):
                dve.wait_ge(grow_ready, j + 1)
                for t in range(TT):
                    tt(x_norm[:, t, :], src[:, t, :], gate_row[:], ALU.mult)
                dve.drain()
                for t in range(TT):
                    tt(H[:, t, :], H[:, t, :], x_norm[:, t, :], ALU.add)

            norm_vec(0)
            nc.vector.memset(v_pad[:, :, 0:4], 0.0)
            dve.wait_ge(pair_taken, TAKEN + 8)
            for i in range(4):
                two = slice(2 * i, 2 * i + 2)
                dve.wait_ge(pair_done, PAIRS + 8 + i + 1)
                tt(v_pad[:, two, 4:260], banks[:, 4 + i, :].rearrange("p (a b) -> p a b", a=2), c_conv[:, two, :], ALU.mult)
                for j in range(3):
                    dve.drain()
                    for b in (2 * i, 2 * i + 1):
                        w = misc_col[:, 8 + 8 * j + b:9 + 8 * j + b]
                        if j == 0:
                            ts(conv_o[:, b, :], v_pad[:, b, 2:2 + SEQ], w, None, ALU.mult)
                        else:
                            stt(conv_o[:, b, :], v_pad[:, b, 2 + j:2 + j + SEQ], w, conv_o[:, b, :], ALU.mult, ALU.add)
                dve.drain()
                last = tt(conv_o[:, two, :], conv_o[:, two, :], b_conv[:, two, :], ALU.mult)
            last.then_inc(conv_ready, 1)
            dve.wait_ge(mix_done, DEPTH + 1)
            residual(0, acc)

            norm_vec(1)
            gate_vec(dve, FFN2, 0)
            x_low_vec(dve, FFNS - 1)
            ffn_vec(dve, FFN2)
            dve.wait_ge(down_done, FFN2 + NS + 1)
            residual(1, acc)

            norm_vec(2)
            dve.wait_ge(pair_taken, TAKEN + 8 + 8)
            for t in range(TT):
                src = a_qk[:, t, :].rearrange("p (h c) -> p h c", c=AD)
                dst = a_rot[:, t, :].rearrange("p (h c) -> p h c", c=AD)
                cos = cosine[:, 1, t:t + 1, :].to_broadcast([P, 2 * AH, HALF])
                sin = sine[:, 1, t:t + 1, :].to_broadcast([P, 2 * AH, HALF])
                p0, p1, p2, p3 = [x.rearrange("p (h c) -> p h c", c=HALF) for x in (a_t[:, 0, :], a_t[:, 1, :], a_t2[:, 0, :], a_t2[:, 1, :])]
                x1, x2 = src[:, :, 0:HALF], src[:, :, HALF:]
                dve.drain()
                tt(p0, x1, cos, ALU.mult)
                tt(p1, x2, sin, ALU.mult)
                tt(p2, x2, cos, ALU.mult)
                tt(p3, x1, sin, ALU.mult)
                dve.drain()
                tt(dst[:, :, 0:HALF], p0, p1, ALU.subtract)
                tt(dst[:, :, HALF:], p2, p3, ALU.add).then_inc(a_rotated, 1)
            dve.wait_ge(setup_done, 1)
            for h in range(AH):
                dve.wait_ge(a_scored, h + 1)
                tt(a_s[:, h, :], banks[:, h % 8, 0:3 * P], band[:, h // AJ, :, :].rearrange("p i c -> p (i c)"), ALU.add).then_inc(a_masked, 1)
            dve.drain()
            nc.vector.tensor_reduce(a_neg[:, 0:AH], a_s[:, :, 0:P], AX.X, ALU.max)
            nc.vector.tensor_reduce(a_neg[:, AH:], a_s[:, :, P:], AX.X, ALU.max)
            dve.drain()
            ts(a_neg, a_neg, -A_SCALE, None, ALU.mult)
            dve.drain()
            for t in range(TT):
                own = a_neg[:, t * AH:(t + 1) * AH]
                low = a_low[:, t * AJ:(t + 1) * AJ]
                nc.vector.tensor_reduce(low, own.rearrange("p (g j) -> p j g", g=AG), AX.X, ALU.min)
                dve.drain()
                tt(a_up[:, t * AH:(t + 1) * AH].rearrange("p (g j) -> p g j", g=AG), low.rearrange("p (o j) -> p o j", o=1).to_broadcast([P, AG, AJ]),
                   own.rearrange("p (g j) -> p g j", g=AG), ALU.subtract)
            dve.drain().then_inc(a_max, 1)
            for h in range(AH):
                dve.wait_ge(a_pT_done, h + 1)
                nc.vector.tensor_copy(a_pT[:, h, :, :].rearrange("p i c -> p (i c)"), banks[:, 4 + h % 4, 0:3 * P]).then_inc(a_pT_ready, 1)
            tt(a_coef, a_up, a_sum, ALU.mult)
            dve.drain()
            for t in range(TT):
                nc.vector.tensor_reduce(a_low[:, t * AJ:(t + 1) * AJ], a_coef[:, t * AH:(t + 1) * AH].rearrange("p (g j) -> p j g", g=AG), AX.X, ALU.add)
            dve.drain()
            nc.vector.reciprocal(a_low, a_low)
            dve.drain()
            for t in range(TT):
                tt(a_coef[:, t * AH:(t + 1) * AH].rearrange("p (g j) -> p g j", g=AG), a_up[:, t * AH:(t + 1) * AH].rearrange("p (g j) -> p g j", g=AG),
                   a_low[:, t * AJ:(t + 1) * AJ].rearrange("p (o j) -> p o j", o=1).to_broadcast([P, AG, AJ]), ALU.mult)
            dve.drain()
            dve.wait_ge(a_o_done, 1)
            for t in range(TT):
                for i, heads in enumerate((8, AH - 8)):
                    c = slice(8 * i * AD, (8 * i + heads) * AD)
                    last = tt(a_o[:, t, c].rearrange("p (h c) -> p h c", c=AD), banks[:, 2 * t + i, 0:heads * AD].rearrange("p (h c) -> p h c", c=AD),
                              wide(a_coef[:, t * AH + 8 * i:t * AH + 8 * i + heads], heads, AD), ALU.mult)
            last.then_inc(a_o_ready, 1)
            dve.wait_ge(mix_done, DEPTH + 2)
            residual(2, acc)

            norm_vec(3)
            for e in range(NE):
                nc.vector.memset(r_rank[:, e:e + 1], float(NE - e))
            nc.vector.memset(experts_sum, 0.0)
            dve.wait_ge(route_done, 1)
            nc.vector.tensor_copy(r_log.rearrange("p t e -> p (t e)"), banks[:, 6, 0:TT * NE])
            dve.drain()
            rank = r_rank.rearrange("p (o e) -> p o e", o=1).to_broadcast([P, TT, NE])

            def first_largest(src, top, hot):
                nc.vector.tensor_reduce(top, src, AX.X, ALU.max)
                dve.drain()
                tt(r_eq, src, wide(top, TT, NE), ALU.is_equal)
                dve.drain()
                tt(r_eq, r_eq, rank, ALU.mult)
                dve.drain()
                nc.vector.tensor_reduce(r_top, r_eq, AX.X, ALU.max)
                dve.drain()
                tt(hot, r_eq, wide(r_top, TT, NE), ALU.is_equal)
                dve.drain()

            first_largest(r_log, r_first, r_hot1)
            stt(r_rest, r_hot1, -3e38, r_log, ALU.mult, ALU.add)
            dve.drain()
            first_largest(r_rest, r_second, r_hot2)
            tt(r_exp, r_second, r_first, ALU.subtract).then_inc(route_exp, 1)
            nc.vector.memset(prefix[0:CHUNK, CHUNK:], 1.0)
            tt(chosen, r_hot1, r_hot2, ALU.add)
            dve.drain().then_inc(chosen_ready, 1)
            dve.wait_ge(route_exp, 2)
            ts(r_w1, r_exp, 1.0, None, ALU.add)
            dve.drain()
            nc.vector.reciprocal(r_w1, r_w1)
            dve.drain()
            tt(r_exp, r_exp, r_w1, ALU.mult)
            tt(r_hot1, r_hot1, wide(r_w1, TT, NE), ALU.mult)
            dve.drain()
            tt(r_hot2, r_hot2, wide(r_exp, TT, NE), ALU.mult)
            dve.drain()
            tt(v3(small, 256, TT, NE), r_hot1, r_hot2, ALU.add)
            dve.drain()
            dve.wait_ge(counted, 1)
            nc.vector.tensor_copy(count_up, banks[:, 6, 0:P])
            nc.vector.tensor_copy(counts, banks[:, 7, 16:16 + NE])
            tt(token_rank.rearrange("p t e -> p (t e)"), banks[:, 7, 0:TT * NE], chosen.rearrange("p t e -> p (t e)"), ALU.mult)
            dve.drain()
            ts(passes, counts, 0.0, None, ALU.is_gt)
            ts(more, counts, float(P), None, ALU.is_gt)
            dve.drain()
            tt(passes, passes, more, ALU.add)
            dve.drain()
            nc.vector.tensor_copy(end_item, passes)
            for e in range(1, NE):
                dve.drain()
                tt(end_item[:, e:e + 1], end_item[:, e:e + 1], end_item[:, e - 1:e], ALU.add)
            dve.drain()
            tt(first_item, end_item, passes, ALU.subtract)

            def by_item(ap):
                return ap.rearrange("p (i o) -> p i o", o=1).to_broadcast([P, ITEMS, NE])

            def by_expert(ap):
                return ap.rearrange("p (o e) -> p o e", o=1).to_broadcast([P, ITEMS, NE])

            def pick_expert(out_, src):
                tt(item_tmp, item_hot, by_expert(src), ALU.mult)
                dve.drain()
                nc.vector.tensor_reduce(out_, item_tmp, AX.X, ALU.add)
                dve.drain()

            tt(item_tmp, by_item(count_up[:, 0:ITEMS]), by_expert(end_item), ALU.is_gt)
            dve.drain()
            nc.vector.tensor_reduce(item_expert, item_tmp, AX.X, ALU.add)
            dve.drain()
            ts(plan[:, 0:ITEMS], item_expert, float(NE - 1), None, ALU.min)
            nc.vector.tensor_copy(plan[:, ITEMS:], end_item[:, NE - 1:])
            dve.drain().then_inc(plan_ready, 1)
            ts(item_expert, item_expert, 1.0, None, ALU.add)
            dve.drain()
            tt(item_hot, by_item(item_expert), by_expert(count_up[:, 0:NE]), ALU.is_equal)
            dve.drain()
            pick_expert(item_pass, first_item)
            tt(item_pass, count_up[:, 0:ITEMS], item_pass, ALU.subtract)
            dve.drain()
            ts(item_pass, item_pass, -1.0, -float(P), ALU.add, ALU.mult)
            for t in range(TT):
                pick_expert(item_slot[:, t, :], token_rank[:, t, :])
                tt(item_slot[:, t, :], item_slot[:, t, :], item_pass, ALU.add)
                pick_expert(item_gate[:, t, :], route[:, t * NE:(t + 1) * NE])

            def weigh_vec(i):
                for t in range(TT):
                    last = ts(weigh[:, t, :], count_up, mod_sum[:, bass.ds(256 + t * ITEMS + i, 1)], mod_sum[:, bass.ds(288 + t * ITEMS + i, 1)],
                              ALU.is_equal, ALU.mult)
                last.then_inc(weigh_ready, 1)

            def pick_vec(i):
                for t in range(TT):
                    last = ts(pick[:, t, :], count_up, mod_sum[:, bass.ds(256 + t * ITEMS + i, 1)], None, ALU.is_equal)
                last.then_inc(pick_ready, 1)

            dve.drain().then_inc(sum_done, 2)
            items = dve.value_load(plan[0:1, ITEMS:ITEMS + 1], min_val=1, max_val=ITEMS - 1)
            pick_vec(0)
            x_low_vec(dve, FFNS, slot_x_parts, P)
            gate_vec(dve, EXPERTS_AT, 0)
            up_vec(dve, EXPERTS_AT, 0)
            weigh_vec(0)
            pick_vec(1)
            first_step_vec(dve, EXPERTS_AT)
            with dve.Fori(0, items) as i:
                n = EXPERTS_AT + i * NS
                expert_vec(dve, n)
                x_low_vec(dve, i + FFNS + 1, slot_x_parts, P)
                first_step_vec(dve, n + NS)
                for t in range(TT):
                    dve.wait_ge(scattered, i * 2 + t + 1)
                    b = (2, 6)[t]
                    tt(experts_sum[:, t, :], experts_sum[:, t, :], banks[:, b:b + 2, :].rearrange("p b c -> p (b c)"), ALU.add).then_inc(sum_done, 1)
                weigh_vec(i + 1)
                pick_vec(i + 2)
                dve.drain()
            residual(3, experts_sum)

            dve.drain().then_inc(var_ready, 1)
            dve.wait_ge(std_ready, NORMS + 5)
            nc.vector.reciprocal(spread[:, :, 1], spread[:, :, 0])
            dve.wait_ge(norm_in, NORMS * 32 + 16)
            dve.drain()
            for t in range(TT):
                stt(H[:, t, :], H[:, t, :], spread[:, t, 1:2], row_b[:], ALU.mult, ALU.mult).then_inc(out_ready, 1)


_INS = ['x', 'positions', 'ln1_g', 'ln1_b', 'ffn1_w_gate', 'ffn1_w_up', 'ffn1_w_down', 'w_in', 'b_gate', 'dn_conv_w',
        'dn_a_log', 'dn_dt_bias', 'dn_norm_w', 'dn_w_o', 'cv_glu_b', 'cv_dw_w', 'cv_dw_b', 'cv_ln_g', 'cv_ln_b',
        'cv_w_pw2', 'cv_b_pw2', 'mla_q_norm_w', 'mla_w_uq', 'mla_kv_norm_w', 'mla_w_ukv', 'mla_w_o', 'w_out', 'ln2_g',
        'ln2_b', 'ffn2_w_gate', 'ffn2_w_up', 'ffn2_w_down', 'ln3_g', 'ln3_b', 'c_2', 'positions_2', 'mod_w_2',
        'mod_b_2', 'norm_g_2', 'conv_w_in_2', 'conv_w_2', 'conv_w_out_2', 'ffn_w_gate_2', 'ffn_w_up_2', 'ffn_w_down_2',
        'attn_w_qkv_2', 'attn_w_o_2', 'router_w_2', 'moe_w_gate_2', 'moe_w_up_2', 'moe_w_down_2', 'final_g_2']


def kernel(**inputs):
    import numpy as _np
    import concourse.bacc as _bacc
    from concourse import mybir as _mybir
    from concourse.bass_utils import run_bass_kernel_spmd as _run

    nc = _bacc.Bacc("TRN2", target_bir_lowering=False, num_devices=1)
    arrays, args = {}, {}
    for name in _INS:
        v = _np.ascontiguousarray(inputs[name])
        arrays[f"in_{name}_dram"] = v
        args[name] = nc.dram_tensor(f"in_{name}_dram", v.shape, _mybir.dt.from_np(v.dtype), kind="ExternalInput").ap()
    out = nc.dram_tensor("out_0_dram", (1, SEQ, D), F32, kind="ExternalOutput").ap()
    build(nc, args, out)
    r = _run(nc, [arrays], core_ids=[0])
    return r.results[0]["out_0_dram"]
```
